# Optimizing a Trainium2 kernel written in Bass

```python
import math
import jax, jax.numpy as jnp
from jax import lax
import numpy as np
import jax
import jax.numpy as jnp

D_MODEL = 1024
BATCH = 1
SEQ = 256
DEPTH = 1

N_META = 16
BLOCK = 128
D_FF = 2816
EPS = 1e-6
NEG_INF = -1e30
MLA_HEADS = 8
MLA_Q_RANK = 256
MLA_KV_RANK = 128
MLA_NOPE_DIM = 64
MLA_ROPE_DIM = 32
MLA_QK_DIM = MLA_NOPE_DIM + MLA_ROPE_DIM
MLA_V_DIM = 64
ROPE_THETA = 10000.0
FOX_HEADS = 8
FOX_HEAD_DIM = 64
D_MIX = MLA_HEADS * MLA_V_DIM + FOX_HEADS * FOX_HEAD_DIM
IN_SPLITS = (MLA_Q_RANK, MLA_KV_RANK, MLA_ROPE_DIM, 3 * FOX_HEADS * FOX_HEAD_DIM, FOX_HEADS)
D_IN = sum(IN_SPLITS)


def rms_norm(x, g):
    xf = x.astype(jnp.float32)
    y = xf * lax.rsqrt(jnp.mean(xf * xf, axis=-1, keepdims=True) + EPS)
    return (y * g.astype(jnp.float32)).astype(x.dtype)

def swiglu(x, w_gate, w_up, w_down):
    return (jax.nn.silu(x @ w_gate) * (x @ w_up)) @ w_down

def rope(x, pos):
    half = x.shape[-1] // 2
    inv_freq = 1.0 / (ROPE_THETA ** (jnp.arange(half, dtype=jnp.float32) / half))
    ang = pos.astype(jnp.float32)[:, None] * inv_freq[None, :]
    cos = jnp.cos(ang)[None, :, None, :].astype(x.dtype)
    sin = jnp.sin(ang)[None, :, None, :].astype(x.dtype)
    x1, x2 = x[..., :half], x[..., half:]
    return jnp.concatenate([x1 * cos - x2 * sin, x2 * cos + x1 * sin], axis=-1)

def block_causal_attention(q, k, v, scale, key_valid, cum=None):
    L = q.shape[1]
    outs = []
    for i in range(L // BLOCK):
        q0, q1 = i * BLOCK, (i + 1) * BLOCK
        s = jnp.einsum('bqhd,bkhd->bhqk', q[:, q0:q1], k[:, :q1],
                       preferred_element_type=jnp.float32) * scale
        if cum is not None:
            cq = jnp.transpose(cum[:, q0:q1], (0, 2, 1))[:, :, :, None]
            ck = jnp.transpose(cum[:, :q1], (0, 2, 1))[:, :, None, :]
            s = s + (cq - ck)
        q_pos = q0 + jnp.arange(BLOCK)
        k_pos = jnp.arange(q1)
        mask = (k_pos[None, :] <= q_pos[:, None]) & key_valid[None, :q1]
        s = jnp.where(mask[None, None], s, NEG_INF)
        p = jax.nn.softmax(s, axis=-1).astype(v.dtype)
        outs.append(jnp.einsum('bhqk,bkhd->bqhd', p, v[:, :q1]))
    return jnp.concatenate(outs, axis=1)

def hybrid_mixer(u, pos, key_valid, w_in, g_cq, w_uq, g_ckv, w_ukv, g_q_mla, g_k_mla,
                 b_forget, g_q_fox, g_k_fox, w_out):
    B, L, _ = u.shape
    proj = u @ w_in
    offs = [int(o) for o in np.cumsum(IN_SPLITS)[:-1]]
    c_q, c_kv, k_pe, fox_qkv, f_logit = jnp.split(proj, offs, axis=-1)

    q = (rms_norm(c_q, g_cq) @ w_uq).reshape(B, L, MLA_HEADS, MLA_QK_DIM)
    q = rms_norm(q, g_q_mla)
    q = jnp.concatenate([q[..., :MLA_NOPE_DIM], rope(q[..., MLA_NOPE_DIM:], pos)], axis=-1)
    kv = (rms_norm(c_kv, g_ckv) @ w_ukv).reshape(B, L, MLA_HEADS, MLA_NOPE_DIM + MLA_V_DIM)
    k_nope, v = kv[..., :MLA_NOPE_DIM], kv[..., MLA_NOPE_DIM:]
    k_pe_b = jnp.broadcast_to(k_pe[:, :, None, :], (B, L, MLA_HEADS, MLA_ROPE_DIM))
    k = rms_norm(jnp.concatenate([k_nope, k_pe_b], axis=-1), g_k_mla)
    k = jnp.concatenate([k[..., :MLA_NOPE_DIM], rope(k[..., MLA_NOPE_DIM:], pos)], axis=-1)
    o_mla = block_causal_attention(q, k, v, 1.0 / math.sqrt(MLA_QK_DIM), key_valid)

    fq, fk, fv = jnp.split(fox_qkv.reshape(B, L, 3, FOX_HEADS, FOX_HEAD_DIM), 3, axis=2)
    fq = rms_norm(fq[:, :, 0], g_q_fox)
    fk = rms_norm(fk[:, :, 0], g_k_fox)
    fv = fv[:, :, 0]
    log_f = jax.nn.log_sigmoid(f_logit.astype(jnp.float32) + b_forget.astype(jnp.float32))
    cum = jnp.cumsum(log_f, axis=1)
    o_fox = block_causal_attention(fq, fk, fv, 1.0 / math.sqrt(FOX_HEAD_DIM), key_valid, cum)

    o = jnp.concatenate([o_mla.reshape(B, L, MLA_HEADS * MLA_V_DIM),
                         o_fox.reshape(B, L, FOX_HEADS * FOX_HEAD_DIM)], axis=-1)
    return o @ w_out

def first_inputs(seed: int = 0) -> dict:
    key = jax.random.key(seed)
    ks = jax.random.split(key, 24)
    f32 = jnp.float32

    def nrm(k, shape, fan_in):
        return jax.random.normal(k, shape, f32) * (fan_in ** -0.5)

    def gain(k, n):
        return 1.0 + 0.02 * jax.random.normal(k, (DEPTH, n), f32)

    return {
        "x": jax.random.normal(ks[0], (BATCH, SEQ, D_MODEL), f32),
        "meta_tokens": jax.random.normal(ks[1], (N_META, D_MODEL), f32),
        "g_ffn1": gain(ks[2], D_MODEL),
        "w1_gate": nrm(ks[3], (DEPTH, D_MODEL, D_FF), D_MODEL),
        "w1_up": nrm(ks[4], (DEPTH, D_MODEL, D_FF), D_MODEL),
        "w1_down": nrm(ks[5], (DEPTH, D_FF, D_MODEL), D_FF),
        "g_mix": gain(ks[6], D_MODEL),
        "w_in": nrm(ks[7], (DEPTH, D_MODEL, D_IN), D_MODEL),
        "g_cq": gain(ks[8], MLA_Q_RANK),
        "w_uq": nrm(ks[9], (DEPTH, MLA_Q_RANK, MLA_HEADS * MLA_QK_DIM), MLA_Q_RANK),
        "g_ckv": gain(ks[10], MLA_KV_RANK),
        "w_ukv": nrm(ks[11], (DEPTH, MLA_KV_RANK, MLA_HEADS * (MLA_NOPE_DIM + MLA_V_DIM)), MLA_KV_RANK),
        "g_q_mla": gain(ks[12], MLA_QK_DIM),
        "g_k_mla": gain(ks[13], MLA_QK_DIM),
        "b_forget": jax.random.uniform(ks[14], (DEPTH, FOX_HEADS), f32, 1.0, 4.0),
        "g_q_fox": gain(ks[15], FOX_HEAD_DIM),
        "g_k_fox": gain(ks[16], FOX_HEAD_DIM),
        "w_out": nrm(ks[17], (DEPTH, D_MIX, D_MODEL), D_MIX),
        "g_ffn2": gain(ks[18], D_MODEL),
        "w2_gate": nrm(ks[19], (DEPTH, D_MODEL, D_FF), D_MODEL),
        "w2_up": nrm(ks[20], (DEPTH, D_MODEL, D_FF), D_MODEL),
        "w2_down": nrm(ks[21], (DEPTH, D_FF, D_MODEL), D_FF),
    }

def first_block(x, meta_tokens, g_ffn1, w1_gate, w1_up, w1_down, g_mix, w_in, g_cq, w_uq,
              g_ckv, w_ukv, g_q_mla, g_k_mla, b_forget, g_q_fox, g_k_fox, w_out,
              g_ffn2, w2_gate, w2_up, w2_down):
    B = x.shape[0]
    pad = BLOCK - N_META
    meta = jnp.broadcast_to(meta_tokens.astype(x.dtype)[None], (B, N_META, D_MODEL))
    h = jnp.concatenate([jnp.zeros((B, pad, D_MODEL), x.dtype), meta, x], axis=1)
    L = h.shape[1]
    idx = jnp.arange(L)
    key_valid = idx >= pad
    pos = jnp.maximum(idx - pad, 0).astype(jnp.int32)
    for l in range(DEPTH):
        h = h + 0.5 * swiglu(rms_norm(h, g_ffn1[l]), w1_gate[l], w1_up[l], w1_down[l])
        h = h + hybrid_mixer(rms_norm(h, g_mix[l]), pos, key_valid, w_in[l], g_cq[l], w_uq[l],
                             g_ckv[l], w_ukv[l], g_q_mla[l], g_k_mla[l], b_forget[l],
                             g_q_fox[l], g_k_fox[l], w_out[l])
        h = h + 0.5 * swiglu(rms_norm(h, g_ffn2[l]), w2_gate[l], w2_up[l], w2_down[l])
    return h[:, BLOCK:]


DEPTH_2 = 2

GRID_W = 64
CTX_LEN = 256
N_MIXERS = 2
N_LAYERS_A = (DEPTH_2 + N_MIXERS - 1) // N_MIXERS
N_LAYERS_B = DEPTH_2 // N_MIXERS
N_MOD = 6
NORM_EPS = 1e-6
CHUNK = 128
GMLP_WIDTH = 2 * D_MODEL
GMLP_GROUP_CH = 128
GMLP_GROUPS = GMLP_WIDTH // GMLP_GROUP_CH
LN_EPS = 1e-5
RWKV_HEAD = 64
RWKV_HEADS = D_MODEL // RWKV_HEAD
DECAY_LORA = 64
AAA_LORA = 64
GATE_LORA = 160
GN_EPS = 64e-5
N_DIR = 2
N_GROUPS = 4
EXPERTS_PER_GROUP = 8
N_EXPERTS = N_GROUPS * EXPERTS_PER_GROUP
EXPERT_HIDDEN = 512
TOP_K = 2
MOE_BLOCK = 128


def rmsnorm(x, g):
    xf = x.astype(jnp.float32)
    y = xf * lax.rsqrt(jnp.mean(xf * xf, axis=-1, keepdims=True) + NORM_EPS)
    return y.astype(x.dtype) * g

def layernorm(x, g, b, eps):
    xf = x.astype(jnp.float32)
    mu = jnp.mean(xf, axis=-1, keepdims=True)
    var = jnp.mean(jnp.square(xf - mu), axis=-1, keepdims=True)
    return ((xf - mu) * lax.rsqrt(var + eps)).astype(x.dtype) * g + b

def gmlp_mixer(h, w_in, b_in, ln_g, ln_b, w_s, b_s, w_out, b_out):
    bsz, n, _ = h.shape
    z = jax.nn.gelu(h @ w_in + b_in, approximate=False)
    u, v = jnp.split(z, 2, axis=-1)
    v = layernorm(v, ln_g, ln_b, LN_EPS)
    v = v.reshape(bsz, n // CHUNK, CHUNK, GMLP_GROUPS, GMLP_GROUP_CH)
    v = jnp.einsum('gpq,bcqgd->bcpgd', w_s, v) + b_s.T[:, :, None]
    return (u * v.reshape(bsz, n, GMLP_WIDTH)) @ w_out + b_out

def qshift_grid(h, rows):
    bsz, n, d = h.shape
    q = d // 4
    g = h.reshape(bsz, rows, GRID_W, d)
    left = jnp.pad(g[:, :, :-1, :q], ((0, 0), (0, 0), (1, 0), (0, 0)))
    right = jnp.pad(g[:, :, 1:, q:2 * q], ((0, 0), (0, 0), (0, 1), (0, 0)))
    up = jnp.pad(g[:, :-1, :, 2 * q:3 * q], ((0, 0), (1, 0), (0, 0), (0, 0)))
    down = jnp.pad(g[:, 1:, :, 3 * q:], ((0, 0), (0, 1), (0, 0), (0, 0)))
    return jnp.concatenate([left, right, up, down], axis=-1).reshape(bsz, n, d)

def bishift_1d(h):
    half = h.shape[-1] // 2
    prev = jnp.pad(h[:, :-1, :half], ((0, 0), (1, 0), (0, 0)))
    nxt = jnp.pad(h[:, 1:, half:], ((0, 0), (0, 1), (0, 0)))
    return jnp.concatenate([prev, nxt], axis=-1)

def _heads(z):
    return z.reshape(*z.shape[:-1], RWKV_HEADS, RWKV_HEAD)

def _both_dirs(z):
    return jnp.stack([z, z[:, ::-1]])

def _rev_dir1(z):
    return jnp.stack([z[0], z[1][:, ::-1]])

def _scan_layout(z):
    return jnp.moveaxis(_heads(z), 2, 0).astype(jnp.float32)

def rwkv_prepare(h, h_shift, mu, wr, wk, wv, w0, w1, w2, a0, a1, a2, k_k, k_a):
    xx = h_shift - h
    xr, xw, xk, xv, xa = [h + xx * mu[j] for j in range(5)]
    r = xr @ wr
    k = xk @ wk
    v = xv @ wv
    lw = jnp.einsum('zbtr,zrd->zbtd', jnp.tanh(jnp.einsum('btd,zdr->zbtr', xw, w1)), w2)
    w_log = -jax.nn.softplus(-(w0[:, None, None, :] + lw).astype(jnp.float32)) - 0.5
    decay = jnp.exp(-jnp.exp(w_log))
    la = jnp.einsum('zbtr,zrd->zbtd', jnp.einsum('btd,zdr->zbtr', xa, a1), a2)
    a = jax.nn.sigmoid((a0[:, None, None, :] + la).astype(jnp.float32))
    kk = _heads(k * k_k).astype(jnp.float32)
    kk = (kk * lax.rsqrt(jnp.sum(kk * kk, axis=-1, keepdims=True) + 1e-12)).reshape(k.shape)
    k_mod = k[None] * (1 + (a - 1) * k_a)
    scan_in = (_scan_layout(_both_dirs(r)), _scan_layout(_rev_dir1(decay)), _scan_layout(_rev_dir1(k_mod)),
               _scan_layout(_both_dirs(v)), _scan_layout(_both_dirs(-kk)), _scan_layout(_rev_dir1(kk[None] * a)))
    return scan_in, r, k_mod, v, xx

def _wkv_step(S, inp):
    r_t, w_t, k_t, v_t, a_t, b_t = inp
    sa = jnp.einsum('zbhvk,zbhk->zbhv', S, a_t)
    S = S * w_t[..., None, :] + sa[..., :, None] * b_t[..., None, :] + v_t[..., :, None] * k_t[..., None, :]
    return S, jnp.einsum('zbhvk,zbhk->zbhv', S, r_t)

def wkv_bidir(state0, scan_in):
    state, ys = lax.scan(_wkv_step, state0, scan_in)
    ys = jnp.moveaxis(ys, 0, 2)
    return state, ys[0] + ys[1][:, ::-1]

def rwkv_out(y, h, xx, r, k_mod, v, mu, ln_g, ln_b, r_k, g1, g2, wo):
    bsz, n, d = r.shape
    y = layernorm(y, ln_g.reshape(RWKV_HEADS, RWKV_HEAD), ln_b.reshape(RWKV_HEADS, RWKV_HEAD), GN_EPS)
    bonus = jnp.einsum('bthk,zbthk->bth', _heads(r) * r_k, _heads(k_mod))
    y = y.astype(r.dtype) + bonus[..., None] * _heads(v)
    xg = h + xx * mu[5]
    gate = jax.nn.sigmoid(xg @ g1) @ g2
    return (y.reshape(bsz, n, d) * gate) @ wo

def rwkv_mixer(hc, hl, rows, need_ctx_out, mu, wr, wk, wv, wo, w0, w1, w2, a0, a1, a2, g1, g2,
               k_k, k_a, r_k, ln_g, ln_b):
    proj = (mu, wr, wk, wv, w0, w1, w2, a0, a1, a2, k_k, k_a)
    scan_c, r_c, km_c, v_c, xx_c = rwkv_prepare(hc, bishift_1d(hc), *proj)
    scan_l, r_l, km_l, v_l, xx_l = rwkv_prepare(hl, qshift_grid(hl, rows), *proj)
    state0 = jnp.zeros((N_DIR, hc.shape[0], RWKV_HEADS, RWKV_HEAD, RWKV_HEAD), jnp.float32)
    state_c, y_c = wkv_bidir(state0, scan_c)
    _, y_l = wkv_bidir(state_c, scan_l)
    outp = (mu, ln_g, ln_b, r_k, g1, g2, wo)
    out_l = rwkv_out(y_l, hl, xx_l, r_l, km_l, v_l, *outp)
    out_c = rwkv_out(y_c, hc, xx_c, r_c, km_c, v_c, *outp) if need_ctx_out else None
    return out_c, out_l

def hier_moe(h, w_grp, b_grp, w_exp, b_exp, w_gate, w_up, w_down):
    n_tok, d = h.shape
    hf = h.astype(jnp.float32)
    grp_logits = hf @ w_grp.astype(jnp.float32) + b_grp.astype(jnp.float32)
    grp_prob = jax.nn.softmax(grp_logits, axis=-1)
    grp = jnp.argmax(grp_logits, axis=-1)
    p_grp = jnp.take_along_axis(grp_prob, grp[:, None], axis=-1)
    exp_logits = (hf @ w_exp.astype(jnp.float32) + b_exp.astype(jnp.float32)).reshape(n_tok, N_GROUPS, EXPERTS_PER_GROUP)
    exp_logits = jnp.take_along_axis(exp_logits, grp[:, None, None], axis=1)[:, 0]
    top_logit, top_idx = lax.top_k(exp_logits, TOP_K)
    weights = (p_grp * jax.nn.softmax(top_logit, axis=-1)).astype(h.dtype)
    expert_id = (grp[:, None] * EXPERTS_PER_GROUP + top_idx).reshape(-1)
    n_assign = n_tok * TOP_K
    order = jnp.argsort(expert_id)
    sorted_e = expert_id[order]
    token_of = order // TOP_K
    counts = jnp.bincount(expert_id, length=N_EXPERTS)
    padded = ((counts + MOE_BLOCK - 1) // MOE_BLOCK) * MOE_BLOCK
    pad_end = jnp.cumsum(padded)
    pad_start = pad_end - padded
    raw_start = jnp.cumsum(counts) - counts
    dest = pad_start[sorted_e] + (jnp.arange(n_assign) - raw_start[sorted_e])
    n_blocks = (n_assign + MOE_BLOCK - 1) // MOE_BLOCK + N_EXPERTS
    cap = n_blocks * MOE_BLOCK
    buf = jnp.zeros((cap, d), h.dtype).at[dest].set(h[token_of])
    block_expert = jnp.minimum(jnp.searchsorted(pad_end, jnp.arange(n_blocks) * MOE_BLOCK, side='right'),
                               N_EXPERTS - 1)

    def expert_block(args):
        xb, e = args
        return (jax.nn.silu(xb @ w_gate[e]) * (xb @ w_up[e])) @ w_down[e]

    out = lax.map(expert_block, (buf.reshape(n_blocks, MOE_BLOCK, d), block_expert)).reshape(cap, d)
    y = jnp.zeros((n_assign, d), h.dtype).at[order].set(out[dest]).reshape(n_tok, TOP_K, d)
    return jnp.einsum('tk,tkd->td', weights, y)

def second_inputs(seed: int = 0) -> dict:
    key = jax.random.key(seed)
    keys = iter(jax.random.split(key, 48))
    f32 = jnp.float32

    def nrm(shape, scale):
        return scale * jax.random.normal(next(keys), shape, f32)

    def gain(shape):
        return 1.0 + nrm(shape, 0.1)

    def unif(shape, lo, hi):
        return jax.random.uniform(next(keys), shape, f32, lo, hi)

    D, W, F = D_MODEL, GMLP_WIDTH, EXPERT_HIDDEN
    NA, NB = N_LAYERS_A, N_LAYERS_B
    return {
        'x': nrm((BATCH, SEQ, D), 1.0),
        'c': nrm((BATCH, D), 1.0),
        'ctx': nrm((BATCH, CTX_LEN, D), 1.0),
        'c_ctx': nrm((D,), 1.0),
        'ada_w': nrm((DEPTH_2, D, N_MOD * D), 0.5 * D ** -0.5),
        'ada_b': nrm((DEPTH_2, N_MOD * D), 0.05),
        'norm1_g': gain((DEPTH_2, D)),
        'norm2_g': gain((DEPTH_2, D)),
        'final_g': gain((D,)),
        'ga_w_in': nrm((NA, D, 2 * W), D ** -0.5),
        'ga_b_in': nrm((NA, 2 * W), 0.02),
        'ga_ln_g': gain((NA, W)),
        'ga_ln_b': nrm((NA, W), 0.02),
        'ga_w_s': nrm((NA, GMLP_GROUPS, CHUNK, CHUNK), 0.5 * CHUNK ** -0.5),
        'ga_b_s': gain((NA, GMLP_GROUPS, CHUNK)),
        'ga_w_out': nrm((NA, W, D), W ** -0.5),
        'ga_b_out': nrm((NA, D), 0.02),
        'rw_mu': unif((NB, N_MOD, D), 0.0, 1.0),
        'rw_wr': nrm((NB, D, D), D ** -0.5),
        'rw_wk': nrm((NB, D, D), D ** -0.5),
        'rw_wv': nrm((NB, D, D), D ** -0.5),
        'rw_wo': nrm((NB, D, D), D ** -0.5),
        'rw_w0': unif((NB, N_DIR, D), -6.0, 0.0),
        'rw_w1': nrm((NB, N_DIR, D, DECAY_LORA), 0.5 * D ** -0.5),
        'rw_w2': nrm((NB, N_DIR, DECAY_LORA, D), 0.5 * DECAY_LORA ** -0.5),
        'rw_a0': nrm((NB, N_DIR, D), 0.5),
        'rw_a1': nrm((NB, N_DIR, D, AAA_LORA), 0.5 * D ** -0.5),
        'rw_a2': nrm((NB, N_DIR, AAA_LORA, D), 0.5 * AAA_LORA ** -0.5),
        'rw_g1': nrm((NB, D, GATE_LORA), D ** -0.5),
        'rw_g2': nrm((NB, GATE_LORA, D), GATE_LORA ** -0.5),
        'rw_k_k': 0.85 + nrm((NB, D), 0.05),
        'rw_k_a': gain((NB, D)),
        'rw_r_k': nrm((NB, RWKV_HEADS, RWKV_HEAD), 0.1),
        'rw_ln_g': gain((NB, D)),
        'rw_ln_b': nrm((NB, D), 0.02),
        'moe_w_grp': nrm((DEPTH_2, D, N_GROUPS), D ** -0.5),
        'moe_b_grp': nrm((DEPTH_2, N_GROUPS), 0.01),
        'moe_w_exp': nrm((DEPTH_2, D, N_EXPERTS), D ** -0.5),
        'moe_b_exp': nrm((DEPTH_2, N_EXPERTS), 0.01),
        'moe_w_gate': nrm((DEPTH_2, N_EXPERTS, D, F), D ** -0.5),
        'moe_w_up': nrm((DEPTH_2, N_EXPERTS, D, F), D ** -0.5),
        'moe_w_down': nrm((DEPTH_2, N_EXPERTS, F, D), F ** -0.5),
    }

def second_block(x, c, ctx, c_ctx, ada_w, ada_b, norm1_g, norm2_g, final_g,
              ga_w_in, ga_b_in, ga_ln_g, ga_ln_b, ga_w_s, ga_b_s, ga_w_out, ga_b_out,
              rw_mu, rw_wr, rw_wk, rw_wv, rw_wo, rw_w0, rw_w1, rw_w2, rw_a0, rw_a1, rw_a2,
              rw_g1, rw_g2, rw_k_k, rw_k_a, rw_r_k, rw_ln_g, rw_ln_b,
              moe_w_grp, moe_b_grp, moe_w_exp, moe_b_exp, moe_w_gate, moe_w_up, moe_w_down):
    bsz, n, d = x.shape
    rows = n // GRID_W
    xc = ctx
    silu_c = jax.nn.silu(c)
    silu_cc = jax.nn.silu(c_ctx)
    for i in range(DEPTH_2):
        last = i == DEPTH_2 - 1
        j = i // N_MIXERS
        mod_l = silu_c @ ada_w[i] + ada_b[i]
        mod_c = silu_cc @ ada_w[i] + ada_b[i]
        sh1, sc1, gt1, sh2, sc2, gt2 = jnp.split(mod_l[:, None, :], N_MOD, axis=-1)
        csh1, csc1, cgt1, csh2, csc2, cgt2 = jnp.split(mod_c, N_MOD, axis=-1)
        hl = rmsnorm(x, norm1_g[i]) * (1 + sc1) + sh1
        hc = rmsnorm(xc, norm1_g[i]) * (1 + csc1) + csh1
        if i % N_MIXERS == 0:
            gp = (ga_w_in[j], ga_b_in[j], ga_ln_g[j], ga_ln_b[j], ga_w_s[j], ga_b_s[j], ga_w_out[j], ga_b_out[j])
            yl = gmlp_mixer(hl, *gp)
            yc = None if last else gmlp_mixer(hc, *gp)
        else:
            yc, yl = rwkv_mixer(hc, hl, rows, not last, rw_mu[j], rw_wr[j], rw_wk[j], rw_wv[j], rw_wo[j],
                                rw_w0[j], rw_w1[j], rw_w2[j], rw_a0[j], rw_a1[j], rw_a2[j], rw_g1[j], rw_g2[j],
                                rw_k_k[j], rw_k_a[j], rw_r_k[j], rw_ln_g[j], rw_ln_b[j])
        x = x + gt1 * yl
        hl2 = rmsnorm(x, norm2_g[i]) * (1 + sc2) + sh2
        mp = (moe_w_grp[i], moe_b_grp[i], moe_w_exp[i], moe_b_exp[i], moe_w_gate[i], moe_w_up[i], moe_w_down[i])
        if last:
            x = x + gt2 * hier_moe(hl2.reshape(-1, d), *mp).reshape(x.shape)
        else:
            xc = xc + cgt1 * yc
            hc2 = rmsnorm(xc, norm2_g[i]) * (1 + csc2) + csh2
            out = hier_moe(jnp.concatenate([hl2.reshape(-1, d), hc2.reshape(-1, d)], axis=0), *mp)
            x = x + gt2 * out[:bsz * n].reshape(x.shape)
            xc = xc + cgt2 * out[bsz * n:].reshape(xc.shape)
    return rmsnorm(x, final_g)


def setup_inputs(seed=0):
    out = dict(first_inputs(seed))
    for name, value in second_inputs(seed + 1).items():
        if name != "x":
            out[name + "_2"] = value
    return out


def reference(
    x, meta_tokens, g_ffn1, w1_gate, w1_up, w1_down, g_mix, w_in, g_cq, w_uq, g_ckv, w_ukv,
    g_q_mla, g_k_mla, b_forget, g_q_fox, g_k_fox, w_out, g_ffn2, w2_gate, w2_up, w2_down, c_2,
    ctx_2, c_ctx_2, ada_w_2, ada_b_2, norm1_g_2, norm2_g_2, final_g_2, ga_w_in_2, ga_b_in_2,
    ga_ln_g_2, ga_ln_b_2, ga_w_s_2, ga_b_s_2, ga_w_out_2, ga_b_out_2, rw_mu_2, rw_wr_2, rw_wk_2,
    rw_wv_2, rw_wo_2, rw_w0_2, rw_w1_2, rw_w2_2, rw_a0_2, rw_a1_2, rw_a2_2, rw_g1_2, rw_g2_2,
    rw_k_k_2, rw_k_a_2, rw_r_k_2, rw_ln_g_2, rw_ln_b_2, moe_w_grp_2, moe_b_grp_2, moe_w_exp_2,
    moe_b_exp_2, moe_w_gate_2, moe_w_up_2, moe_w_down_2,
):
    x = first_block(
        x, meta_tokens, g_ffn1, w1_gate, w1_up, w1_down, g_mix, w_in, g_cq, w_uq, g_ckv, w_ukv,
        g_q_mla, g_k_mla, b_forget, g_q_fox, g_k_fox, w_out, g_ffn2, w2_gate, w2_up, w2_down,
    )
    return second_block(
        x, c_2, ctx_2, c_ctx_2, ada_w_2, ada_b_2, norm1_g_2, norm2_g_2, final_g_2, ga_w_in_2,
        ga_b_in_2, ga_ln_g_2, ga_ln_b_2, ga_w_s_2, ga_b_s_2, ga_w_out_2, ga_b_out_2, rw_mu_2,
        rw_wr_2, rw_wk_2, rw_wv_2, rw_wo_2, rw_w0_2, rw_w1_2, rw_w2_2, rw_a0_2, rw_a1_2,
        rw_a2_2, rw_g1_2, rw_g2_2, rw_k_k_2, rw_k_a_2, rw_r_k_2, rw_ln_g_2, rw_ln_b_2,
        moe_w_grp_2, moe_b_grp_2, moe_w_exp_2, moe_b_exp_2, moe_w_gate_2, moe_w_up_2,
        moe_w_down_2,
    )


_drawn_inputs = setup_inputs


def setup_inputs(seed=0):
    import zlib

    import numpy as np

    out = dict(_drawn_inputs(seed))
    spreads = {}
    factors = {'g_ffn1': 4.703,
     'g_mix': 3.659,
     'g_cq': 8.0,
     'g_ckv': 7.666,
     'g_q_mla': 8.0,
     'g_k_mla': 8.0,
     'g_q_fox': 8.0,
     'g_k_fox': 6.954,
     'g_ffn2': 15.117,
     'ga_b_in_2': 52.908,
     'ga_ln_g_2': 32.536,
     'ga_ln_b_2': 64.0,
     'ga_b_out_2': 43.384,
     'rw_w1_2': 25.141,
     'rw_w2_2': 26.119,
     'rw_a1_2': 3.258,
     'rw_a2_2': 3.311,
     'rw_k_k_2': 200.0,
     'rw_ln_g_2': 200.0,
     'rw_ln_b_2': 200.0,
     'moe_b_grp_2': 40.224,
     'moe_b_exp_2': 64.0,
     'ctx_2': 51.84,
     'c_ctx_2': 58.672,
     'ada_b_2': 4.38,
     'norm1_g_2': 5.72,
     'norm2_g_2': 8.0,
     'ga_b_s_2': 8.0,
     'rw_w0_2': 3.129,
     'rw_a0_2': 8.0,
     'rw_g1_2': 3.563,
     'rw_k_a_2': 8.0,
     'rw_r_k_2': 6.767,
     'moe_w_grp_2': 6.224,
     'moe_w_exp_2': 6.049,
     'moe_w_gate_2': 5.784,
     'moe_w_up_2': 5.441,
     'moe_w_down_2': 5.398}
    for name, (base, spread) in spreads.items():
        noise = np.random.default_rng([zlib.crc32(name.encode()), seed]).standard_normal(out[name].shape)
        drawn = base * np.exp(spread * noise) if base else spread * noise
        out[name] = jnp.asarray(drawn.astype(out[name].dtype))
    for name, factor in factors.items():
        out[name] = (out[name] * factor).astype(out[name].dtype)
    return out
```

```python
from contextlib import ExitStack

import numpy as np
import concourse.bass as bass
from concourse import mybir

F32 = mybir.dt.float32
I32 = mybir.dt.int32
ALU = mybir.AluOpType
ACT = mybir.ActivationFunctionType
AX = mybir.AxisListType
ds = bass.ds

P = 128
D = 1024
DC = D // P
SEQ = 256
META = 16
TA = META + SEQ
TB = 2 * SEQ
D_FF = 2816
FC = D_FF // P
EPS = 1e-6
NEG = -1e30
HEADS = 8
QK = 96
NOPE = 64
ROPE = 32
GW = 2048
GC = GW // P
LN_EPS = 1e-5
RH = 64
GN_EPS = 64e-5
CH = 64
NCH = TB // CH
LCH = SEQ // CH
NE = 32
EG = 8
NG = 4
EH = 512
SLOTS = 64
SLOT = 8 * 264
RING = 6


class Segment:

    def __init__(self, tiles, source):
        self.tiles, self.source, self.first, self.behind = tiles, source, 0, []


class Stream:

    def __init__(self, nc, ctx, segments):
        self.slots = [ctx.enter_context(nc.sbuf_tensor(f"weights_{s}", [P, SLOT], F32)) for s in range(RING)]
        self.landed = [ctx.enter_context(nc.semaphore(f"weights_landed_{s}")) for s in range(RING)]
        self.order, self.need = [], []
        count = [0] * RING
        self.fed = RING
        for seg in segments:
            seg.first = len(self.order)
            for t in range(seg.tiles):
                s = len(self.order) % RING
                count[s] += 16 * len(seg.source(t // RING, t % RING))
                self.order.append((seg, t))
                self.need.append(count[s])

    def slot(self, seg, j):
        return self.slots[(seg.first + j) % RING]

    def start(self, sp, seg, i, j):
        s = (seg.first + j) % RING
        for where, what in seg.source(i, j):
            sp.dma_start(where(self.slots[s]), what).then_inc(self.landed[s], 16)

    def start_number(self, sp, n):
        self.fed = max(self.fed, n + 1)
        if n < len(self.order):
            seg, t = self.order[n]
            self.start(sp, seg, t // RING, t % RING)

    def wait(self, eng, seg, i, j):
        base = self.need[seg.first + j]
        step = self.need[seg.first + j + RING] - base if seg.tiles > j + RING else 0
        eng.wait_ge(self.landed[(seg.first + j) % RING], base + i * step if step else base)

    def feed(self, sp, seg, used, per_tile, per_round):
        self.fed = seg.first + seg.tiles + RING
        rounds = seg.tiles // RING
        looped = rounds - 1 if rounds > 2 else 0
        if looped:
            with sp.Fori(0, looped) as i:
                for j in range(RING):
                    sp.wait_ge(used, i * per_round + per_tile(j))
                    self.start(sp, seg, i + 1, j)
        for t in range(looped * RING, seg.tiles):
            sp.wait_ge(used, (t // RING) * per_round + per_tile(t % RING))
            self.start_number(sp, seg.first + t + RING)


class Chain:

    def __init__(self, eng, sem):
        self.eng, self.sem, self.n = eng, sem, 0

    def __call__(self, ins):
        self.n += 1
        ins.then_inc(self.sem, 1)
        self.eng.wait_ge(self.sem, self.n)


def columns(w, kc, c0, width):
    src = w.rearrange("(k p) m -> p k m", p=P)[:, :, ds(c0, width)]
    return lambda s: s[:, 0:kc * width].rearrange("p (k m) -> p k m", k=kc), src


class Kernel:

    def sem(self, name):
        self.sem_count += 1
        s = self.nc.alloc_semaphore(name=f"{name}_{self.sem_count}")
        self.stage_sems.append(s)
        return s

    def clear(self):
        self.nc.clear_and_free_semaphores(self.stage_sems)
        self.nc.all_engine_barrier()
        self.stage_sems = []


def param_rows(a):
    one = lambda v, n=P: v.rearrange("(c p) -> c p", p=n)
    flat = lambda v: v.rearrange("a b -> (a b)")
    two = lambda v: [(v, 0), (v, RH)]
    return [
        [("g_ffn1", [(one(flat(a["g_ffn1"])), 0)]), ("g_mix", [(one(flat(a["g_mix"])), 0)]),
         ("g_cq", [(one(flat(a["g_cq"])), 0)]), ("g_ckv", [(one(flat(a["g_ckv"])), 0)]),
         ("g_q_mla", [(a["g_q_mla"], 0)]), ("g_k_mla", [(a["g_k_mla"], 0)]),
         ("g_q_fox", two(a["g_q_fox"])), ("g_k_fox", two(a["g_k_fox"])),
         ("b_forget", [(a["b_forget"], 0)]), ("g_ffn2", [(one(flat(a["g_ffn2"])), 0)]),
         ("norm1", [(one(flat(a["norm1_g_2"])), 0)]), ("norm2", [(one(flat(a["norm2_g_2"])), 0)]),
         ("final", [(one(a["final_g_2"]), 0)]), ("ga_b_u", [(one(flat(a["ga_b_in_2"])[0:GW]), 0)]),
         ("ga_b_out", [(one(flat(a["ga_b_out_2"])), 0)])],
        [("mu", [(one(a["rw_mu_2"].rearrange("a b c -> (a b c)")), 0)]),
         ("k_k", [(one(flat(a["rw_k_k_2"])), 0)]), ("k_a", [(one(flat(a["rw_k_a_2"])), 0)]),
         ("r_k", [(one(a["rw_r_k_2"].rearrange("a b c -> (a b c)")), 0)]),
         ("gn_g", [(one(flat(a["rw_ln_g_2"])), 0)]), ("gn_b", [(one(flat(a["rw_ln_b_2"])), 0)]),
         ("w0", [(one(a["rw_w0_2"].rearrange("a b c -> (a b c)")), 0)]),
         ("a0", [(one(a["rw_a0_2"].rearrange("a b c -> (a b c)")), 0)])],
        [("ada_b", [(one(flat(a["ada_b_2"])), 0)]),
         ("c", [(one(flat(a["c_2"])), 0)]), ("c_ctx", [(one(a["c_ctx_2"]), 0)])],
    ]


def stage_setup(k):
    nc = k.nc
    groups = param_rows(k.a)
    width = sum(sum(p[1][0][0].shape[0] for p in g) for g in groups)
    k.params = k.sb("params", [P, width])
    k.col, at, starts = {}, 0, []
    for g in groups:
        starts.append(at)
        for name, pieces in g:
            k.col[name] = at
            at += pieces[0][0].shape[0]
    starts.append(at)
    with ExitStack() as ctx:
        raw = [ctx.enter_context(nc.sbuf_tensor(f"param_rows_{n}", [P, P], F32)) for n in range(len(groups))]
        rows = ctx.enter_context(nc.sbuf_tensor("token_rows", [P, 5, D], F32))
        cleared, param_landed, tokens_landed, ones_made, ident_made = (
            k.sem(n)
            for n in ("cleared", "param_landed", "tokens_landed", "ones_made", "ident_made"))
        turned, copied, tables, vsum = (k.sem(n) for n in ("turned", "copied", "tables", "vsum"))
        block = ctx.enter_context(nc.Block())
        n_dma = sum(len(p) for g in groups for _, p in g)
        tiles = [(k.a["meta_tokens"], META, k.h, 0)]
        tiles += [(k.a["x"][0, t * P:(t + 1) * P, :], P, k.h, META + t * P) for t in range(2)]
        tiles += [(k.a["ctx_2"][0, t * P:(t + 1) * P, :], P, k.x, SEQ + t * P) for t in range(2)]

        @block.sync
        def _(sp):
            for n, (src, rows_n, _, _) in enumerate(tiles):
                sp.dma_start(rows[0:rows_n, n, :], src).then_inc(tokens_landed, 16)
            for n in range(RING):
                k.stream.start_number(sp, n)

        @block.scalar
        def _(act):
            act.wait_ge(cleared, len(groups))
            for g, start in zip(groups, starts):
                for name, pieces in g:
                    for src, off in pieces:
                        r = k.col[name] - start
                        act.dma_start(raw[starts.index(start)][r:r + src.shape[0], off:off + src.shape[1]], src)\
                            .then_inc(param_landed, 16)
            act.dma_start(k.rope_cos[0:QK, :], k.a["rope_cos"]).then_inc(tables, 16)
            act.dma_start(k.rope_sin[0:QK, :], k.a["rope_sin"]).then_inc(tables, 16)
            act.dma_start(k.rope_turn[0:QK, :], k.a["rope_turn"]).then_inc(tables, 16)
            act.wait_ge(tables, 48)

        @block.gpsimd
        def _(pool):
            pool.memset(k.ident[:, :], 0.0).then_inc(ident_made, 1)
            pool.wait_ge(ident_made, 1)
            pool.affine_select(out=k.ident[:, :], in_=k.ident[:, :], compare_op=ALU.not_equal, fill=1.0,
                               base=0, pattern=[[-1, P]], channel_multiplier=1).then_inc(ident_made, 1)
            pool.memset(k.causal[:, :], 0.0).then_inc(ident_made, 1)
            pool.wait_ge(ident_made, 3)
            pool.affine_select(out=k.causal[:, :], in_=k.causal[:, :], compare_op=ALU.is_ge, fill=NEG,
                               base=0, pattern=[[-1, P]], channel_multiplier=1).then_inc(ident_made, 1)

        @block.tensor
        def _(pe):
            pe.wait_ge(ident_made, 2)
            pe.wait_ge(param_landed, 16 * n_dma)
            for n in range(len(groups)):
                last = nc.tensor.transpose(k.bank[n][:, 0:P], raw[n][:, :], k.ident[:, :])
            last.then_inc(turned, 1)
            pe.wait_ge(tokens_landed, 16 * len(tiles))
            for n, (_, r, _, _) in enumerate(tiles):
                for half in range(2):
                    b = (2 * n + half) % 5
                    if 2 * n + half >= 5:
                        pe.wait_ge(copied, 2 + 2 * n + half - 5)
                    for c in range(4):
                        f = (half * 4 + c) * P
                        last = nc.tensor.transpose(k.bank[3 + b][:, c * P:c * P + r], rows[0:r, n, f:f + P],
                                                   k.ident[0:r, 0:r])
                    last.then_inc(turned, 1)

        @block.vector
        def _(dve):
            for n in range(len(groups)):
                nc.vector.memset(raw[n][:, :], 0.0).then_inc(cleared, 1)
            nc.vector.memset(k.ones[:, :], 1.0).then_inc(ones_made, 1)
            nc.vector.memset(k.head_ones[:, :], 0.0).then_inc(ones_made, 1)
            dve.wait_ge(ones_made, 2)
            for h in range(2):
                nc.vector.memset(k.head_ones[h * RH:(h + 1) * RH, h * RH:(h + 1) * RH], 1.0).then_inc(ones_made, 1)
            dve.wait_ge(turned, 1)
            for n in range(len(groups)):
                w = starts[n + 1] - starts[n]
                last = nc.vector.tensor_copy(k.params[:, starts[n]:starts[n + 1]], k.bank[n][:, 0:w])
            last.then_inc(copied, 1)
            for n, (_, r, to, t0) in enumerate(tiles):
                for half in range(2):
                    dve.wait_ge(turned, 2 + 2 * n + half)
                    src = k.bank[3 + (2 * n + half) % 5][:, :].rearrange("p (c t) -> p c t", c=4)[:, :, 0:r]
                    nc.vector.tensor_copy(to[:, half * 4:half * 4 + 4, t0:t0 + r], src).then_inc(copied, 1)


def norm_stage(k, name, src, kc, width, eps, parts, dst, scratch=None):
    nc = k.nc
    T = parts[-1][1]
    t00 = parts[0][0]
    with ExitStack() as ctx:
        sq = scratch or ctx.enter_context(nc.sbuf_tensor(f"{name}_sq", [P, kc, T], F32))
        r0, mean, rr = (ctx.enter_context(nc.sbuf_tensor(f"{name}_{n}", [P, T], F32)) for n in ("r0", "mean", "rr"))
        squared, summed, rooted, vdone, ready, meaned = (k.sem(f"{name}_{n}") for n in (
            "squared", "summed", "rooted", "vdone", "ready", "meaned"))
        block = ctx.enter_context(nc.Block())
        ps = k.bank[0][:, t00:T]
        w = slice(t00, T)

        @block.scalar
        def _(act):
            for c in range(kc):
                nc.scalar.activation(sq[:, c, w], src[:, c, w], ACT.Square).then_inc(squared, 1)
            act.wait_ge(meaned, 1)
            nc.scalar.activation(r0[:, w], mean[:, w], ACT.Ln).then_inc(rooted, 1)
            act.wait_ge(rooted, 1)
            nc.scalar.activation(r0[:, w], r0[:, w], ACT.Exp, scale=-0.5).then_inc(rooted, 1)

        @block.tensor
        def _(pe):
            for c in range(kc):
                pe.wait_ge(squared, c + 1)
                last = nc.tensor.matmul(ps, k.ones[:, :], sq[:, c, w], start=(c == 0), stop=(c == kc - 1))
            last.then_inc(summed, 1)

        @block.vector
        def _(dve):
            link = Chain(dve, vdone)
            dve.wait_ge(summed, 1)
            nc.vector.tensor_scalar(mean[:, w], ps, 1.0 / width, eps, ALU.mult, ALU.add).then_inc(meaned, 1)
            dve.wait_ge(meaned, 1)
            dve.wait_ge(rooted, 2)
            link(nc.vector.tensor_tensor(rr[:, w], r0[:, w], r0[:, w], ALU.mult))
            link(nc.vector.scalar_tensor_tensor(out=rr[:, w], in0=rr[:, w], scalar=-0.5, in1=mean[:, w],
                                                op0=ALU.mult, op1=ALU.mult))
            link(nc.vector.scalar_tensor_tensor(out=rr[:, w], in0=rr[:, w], scalar=1.5, in1=r0[:, w],
                                                op0=ALU.add, op1=ALU.mult))
            for c in range(kc):
                for t0, t1, gain, shift in parts:
                    nc.vector.scalar_tensor_tensor(out=dst[:, c, t0:t1], in0=src[:, c, t0:t1],
                                                   scalar=gain[:, c:c + 1], in1=rr[:, t0:t1],
                                                   op0=ALU.mult, op1=ALU.mult).then_inc(ready, 1)
            if parts[0][3] is not None:
                dve.wait_ge(ready, kc * len(parts))
                for c in range(kc):
                    for t0, t1, _, shift in parts:
                        nc.vector.tensor_scalar(dst[:, c, t0:t1], dst[:, c, t0:t1], shift[:, c:c + 1], None, ALU.add)


def rounds(eng, tiles, body):
    whole = tiles // RING
    if whole > 1:
        with eng.Fori(0, whole) as i:
            body(i, range(RING))
        rest = whole
    else:
        rest = 0
    for i in range(rest, -(-tiles // RING)):
        body(i, range(min(RING, tiles - i * RING)))


def gate_up_stage(k, name, seg, rhs, N, hidden):
    nc = k.nc
    NB = 3
    with ExitStack() as ctx:
        act_out = ctx.enter_context(nc.sbuf_tensor(f"{name}_silu", [P, NB, N], F32))
        pairs, silued, gated = (k.sem(f"{name}_{n}") for n in ("pairs", "silued", "gated"))
        block = ctx.enter_context(nc.Block())

        @block.sync
        def _(sp):
            k.stream.feed(sp, seg, pairs, lambda j: 2 * (j // 2) + 2, RING)

        def each(i, js):
            for q in range(len(js) // 2):
                for c in range(2):
                    yield q, c, (2 * q + c) % NB, i * RING + 2 * q + c

        @block.tensor
        def _(pe):
            def body(i, js):
                for q, c, b, n in each(i, js):
                    if c == 0:
                        k.stream.wait(pe, seg, i, 2 * q)
                        k.stream.wait(pe, seg, i, 2 * q + 1)
                    pe.wait_ge(gated, n + 1)
                    for side in range(2):
                        w = k.stream.slot(seg, 2 * q + side)[:, 0:DC * 256].rearrange("p (k m) -> p k m", k=DC)
                        for f in range(DC):
                            last = nc.tensor.matmul(k.bank[b + side * NB][:, 0:N], w[:, f, c * P:(c + 1) * P],
                                                    rhs[:, f, 0:N], start=(f == 0), stop=(f == DC - 1))
                    last.then_inc(pairs, 1)
            rounds(pe, seg.tiles, body)

        @block.scalar
        def _(act):
            def body(i, js):
                for q, c, b, n in each(i, js):
                    act.wait_ge(pairs, n + 1)
                    nc.scalar.activation(act_out[:, b, :], k.bank[b][:, 0:N], ACT.Silu).then_inc(silued, 1)
            rounds(act, seg.tiles, body)

        @block.vector
        def _(dve):
            dve.sem_inc(gated, NB)

            def body(i, js):
                for q, c, b, n in each(i, js):
                    dve.wait_ge(silued, n + 1)
                    nc.vector.tensor_tensor(hidden[:, ds(n, 1), :].rearrange("p a t -> p (a t)"), act_out[:, b, :],
                                            k.bank[b + NB][:, 0:N], ALU.mult).then_inc(gated, 1)
            rounds(dve, seg.tiles, body)


def linear_stage(k, name, seg, tile_chunks, rhs, N, write, banks, per_chunk=1, on_scalar=False):
    nc = k.nc
    done_in_round = [sum(sum(1 for ch in tile_chunks(x) if ch[0]) for x in range(j + 1)) for j in range(RING)]
    with ExitStack() as ctx:
        made, emptied = (k.sem(f"{name}_{n}") for n in ("made", "emptied"))
        block = ctx.enter_context(nc.Block())
        per_round = done_in_round[-1]
        assert per_round % banks == 0 or seg.tiles <= RING, (name, per_round)

        @block.sync
        def _(sp):
            k.stream.feed(sp, seg, made, lambda j: done_in_round[j] + (0 if any(ch[0] for ch in tile_chunks(j)) else 1),
                          per_round)

        @block.tensor
        def _(pe):
            def body(i, js):
                for j in js:
                    k.stream.wait(pe, seg, i, j)
                    slot = k.stream.slot(seg, j)
                    before = done_in_round[j - 1] if j else 0
                    for ends, starts, pieces, width in tile_chunks(j):
                        n = i * per_round + before
                        ps = k.bank[before % banks][0:width, 0:N]
                        if starts:
                            pe.wait_ge(emptied, n + 1)
                        for p, (view, r) in enumerate(pieces):
                            last = nc.tensor.matmul(ps, view(slot), rhs(r), start=(starts and p == 0),
                                                    stop=(ends and p == len(pieces) - 1))
                        if ends:
                            last.then_inc(made, 1)
                            before += 1
            rounds(pe, seg.tiles, body)

        def empty(eng):
            eng.sem_inc(emptied, banks)

            def body(i, js):
                total = done_in_round[js[-1]]
                for b in range(total):
                    eng.wait_ge(made, i * per_round + b + 1)
                    write(eng, i * per_round + b, k.bank[b % banks]).then_inc(emptied, 1)
            rounds(eng, seg.tiles, body)

        if on_scalar:
            @block.scalar
            def _(act):
                empty(act)
        else:
            @block.vector
            def _(dve):
                empty(dve)


def whole_tiles(kc, width, chunk=P):
    def of(j):
        out = []
        for c0 in range(0, width, chunk):
            w = min(chunk, width - c0)
            pieces = [(lambda s, f=f, c0=c0, w=w: s[:, f * width + c0:f * width + c0 + w], f) for f in range(kc)]
            out.append((True, True, pieces, w))
        return out
    return of


def half_tiles(kc):
    def of(j):
        pieces = [(lambda s, f=f: s[:, f * P:(f + 1) * P], (j % 2) * kc + f) for f in range(kc)]
        return [(j % 2 == 1, j % 2 == 0, pieces, P)]
    return of


def flat(ap):
    return ap.rearrange("p a t -> p (a t)")


def in_proj_stage(k, seg, u, proj):
    starts = [0, P, 2 * P, 3 * P] + [3 * P + ROPE + P * i for i in range(12)] + [3 * P + ROPE + 12 * P]
    widths = [P, P, P, ROPE] + [P] * 12 + [HEADS]

    def of(j):
        lo, w = k.in_tiles[j]
        out = []
        for s, cw in zip(starts, widths):
            if lo <= s < lo + w:
                o = s - lo
                pieces = [(lambda sl, f=f, o=o, w=w, cw=cw: sl[:, f * w + o:f * w + o + cw], f) for f in range(DC)]
                out.append((True, True, pieces, cw))
        return out

    nc = k.nc
    with ExitStack() as ctx:
        made, emptied = (k.sem(f"in_{n}") for n in ("made", "emptied"))
        block = ctx.enter_context(nc.Block())
        count = [sum(len(of(x)) for x in range(j + 1)) for j in range(seg.tiles)]

        @block.sync
        def _(sp):
            for j in range(seg.tiles):
                sp.wait_ge(made, count[j])
                k.stream.start_number(sp, seg.first + j + RING)

        @block.tensor
        def _(pe):
            n = 0
            for j in range(seg.tiles):
                k.stream.wait(pe, seg, j // RING, j % RING)
                slot = k.stream.slot(seg, j)
                for _, _, pieces, w in of(j):
                    if n >= 4:
                        pe.wait_ge(emptied, n - 3)
                    for p, (view, f) in enumerate(pieces):
                        last = nc.tensor.matmul(k.bank[n % 4][0:w, 0:TA], view(slot), u[:, f, :],
                                                start=(p == 0), stop=(p == DC - 1))
                    last.then_inc(made, 1)
                    n += 1

        @block.vector
        def _(dve):
            for n, w in enumerate(widths):
                dve.wait_ge(made, n + 1)
                nc.vector.tensor_copy(proj[0:w, n, :], k.bank[n % 4][0:w, 0:TA]).then_inc(emptied, 1)


def head_norm_stage(k, name, src, dst, rows, heads, width, ones, gain, factor, t0, N, inv=None):
    nc = k.nc
    with ExitStack() as ctx:
        sq = ctx.enter_context(nc.sbuf_tensor(f"{name}_sq", [P, 2, N], F32))
        mean = ctx.enter_context(nc.sbuf_tensor(f"{name}_mean", [P, heads, N], F32))
        r0 = ctx.enter_context(nc.sbuf_tensor(f"{name}_r0", [P, heads, N], F32))
        rr = ctx.enter_context(nc.sbuf_tensor(f"{name}_rr", [P, heads, N], F32))
        squared, summed, meaned, rooted, vdone = (k.sem(f"{name}_{n}") for n in (
            "squared", "summed", "meaned", "rooted", "vdone"))
        block = ctx.enter_context(nc.Block())

        @block.scalar
        def _(act):
            for c in range(heads):
                if c >= 2:
                    act.wait_ge(summed, c - 1)
                nc.scalar.activation(sq[0:rows, c % 2, :], src[0:rows, c, t0:t0 + N], ACT.Square).then_inc(squared, 1)
            act.wait_ge(meaned, heads)
            nc.scalar.activation(flat(r0[0:rows, :, :]), flat(mean[0:rows, :, :]), ACT.Ln).then_inc(rooted, 1)
            act.wait_ge(rooted, 1)
            nc.scalar.activation(flat(r0[0:rows, :, :]), flat(r0[0:rows, :, :]), ACT.Exp, scale=-0.5).then_inc(rooted, 1)

        @block.tensor
        def _(pe):
            for c in range(heads):
                pe.wait_ge(squared, c + 1)
                if c >= 4:
                    pe.wait_ge(meaned, c - 3)
                nc.tensor.matmul(k.bank[c % 4][0:rows, 0:N], ones[0:rows, 0:rows], sq[0:rows, c % 2, :],
                                 start=True, stop=True).then_inc(summed, 1)

        @block.vector
        def _(dve):
            link = Chain(dve, vdone)
            for c in range(heads):
                dve.wait_ge(summed, c + 1)
                nc.vector.tensor_scalar(mean[0:rows, c, :], k.bank[c % 4][0:rows, 0:N], 1.0 / width, EPS,
                                        ALU.mult, ALU.add).then_inc(meaned, 1)
            dve.wait_ge(meaned, heads)
            dve.wait_ge(rooted, 2)
            m, a, b = (flat(x[0:rows, :, :]) for x in (mean, r0, rr))
            link(nc.vector.tensor_tensor(b, a, a, ALU.mult))
            link(nc.vector.scalar_tensor_tensor(out=b, in0=b, scalar=-0.5, in1=m, op0=ALU.mult, op1=ALU.mult))
            link(nc.vector.scalar_tensor_tensor(out=b, in0=b, scalar=1.5, in1=a, op0=ALU.add, op1=ALU.mult))
            if factor != 1.0:
                link(nc.vector.tensor_scalar(b, b, factor, None, ALU.mult))
            for c in range(heads):
                nc.vector.scalar_tensor_tensor(out=dst[0:rows, c, t0:t0 + N], in0=src[0:rows, c, t0:t0 + N],
                                               scalar=gain[0:rows, 0:1], in1=rr[0:rows, c, :],
                                               op0=ALU.mult, op1=ALU.mult)


def expand_stage(k, seg, proj, q, kk, vm):
    nc = k.nc
    uq, ukv = k.stream.slot(seg, 0), k.stream.slot(seg, 1)
    TT = [(0, META), (META, P), (META + P, P)]
    with ExitStack() as ctx:
        made, emptied, vmade, vemptied = (k.sem(f"expand_{n}") for n in (
            "made", "emptied", "vmade", "vemptied"))
        block = ctx.enter_context(nc.Block())
        per_head = 2

        @block.sync
        def _(sp):
            sp.wait_ge(made, HEADS * per_head)
            sp.wait_ge(vmade, 3)
            for j in range(2):
                k.stream.start_number(sp, seg.first + j + RING)

        @block.tensor
        def _(pe):
            k.stream.wait(pe, seg, 0, 0)
            k.stream.wait(pe, seg, 0, 1)
            for h in range(HEADS):
                for side in range(2):
                    n = h * per_head + side
                    if n >= 4:
                        pe.wait_ge(emptied, n - 3)
                    ps = k.bank[n % 4]
                    if side == 0:
                        for f in range(2):
                            o = f * HEADS * QK + h * QK
                            last = nc.tensor.matmul(ps[0:QK, 0:TA], uq[:, o:o + QK], proj[:, f, :],
                                                    start=(f == 0), stop=(f == 1))
                    else:
                        last = nc.tensor.matmul(ps[0:NOPE, 0:TA], ukv[:, h * P:h * P + NOPE], proj[:, 2, :],
                                                start=True, stop=True)
                    last.then_inc(made, 1)
            wv = ukv[:, 0:D].rearrange("p (h m) -> p h m", h=HEADS)[:, :, NOPE:P]
            for t, (t0, n) in enumerate(TT):
                nc.tensor.matmul(k.bank[4 + t][0:n, :], proj[:, 2, t0:t0 + n], wv, start=True, stop=True)\
                    .then_inc(vmade, 1)
            for t, (t0, n) in enumerate(TT):
                if t == 1:
                    pe.wait_ge(vemptied, 1)
                if t == 2:
                    pe.wait_ge(vemptied, 2)
                b = [7, 4, 5][t]
                for c in range(4):
                    last = nc.tensor.transpose(k.bank[b][0:n, c * P:(c + 1) * P], proj[:, 12 + c, t0:t0 + n],
                                               k.ident[:, :])
                last.then_inc(vmade, 1)

        @block.vector
        def _(dve):
            for h in range(HEADS):
                dve.wait_ge(made, 2 * h + 1)
                nc.vector.tensor_copy(q[0:QK, h, :], k.bank[2 * h % 4][0:QK, 0:TA]).then_inc(emptied, 1)
                dve.wait_ge(made, 2 * h + 2)
                nc.vector.tensor_copy(kk[0:NOPE, h, :], k.bank[(2 * h + 1) % 4][0:NOPE, 0:TA]).then_inc(emptied, 1)
                nc.vector.tensor_copy(kk[NOPE:QK, h, :], proj[0:ROPE, 3, :])

        @block.scalar
        def _(act):
            for t, (t0, n) in enumerate(TT):
                act.wait_ge(vmade, t + 1)
                nc.scalar.activation(vm[0:n, t, 0:512], k.bank[4 + t][0:n, :], ACT.Copy).then_inc(vemptied, 1)
            for t, (t0, n) in enumerate(TT):
                act.wait_ge(vmade, 4 + t)
                nc.scalar.activation(vm[0:n, t, 512:1024], k.bank[[7, 4, 5][t]][0:n, :], ACT.Copy)\
                    .then_inc(vemptied, 1)


def rope_stage(k, q, kk, proj, gates_q, gates_k):
    nc = k.nc
    with ExitStack() as ctx:
        tmp = ctx.enter_context(nc.sbuf_tensor("rope_tmp", [P, 2, TA], F32))
        g = ctx.enter_context(nc.sbuf_tensor("gate_tmp", [HEADS, 4, TA], F32))
        zeros = ctx.enter_context(nc.sbuf_tensor("gate_ones", [HEADS, TA], F32))
        turned, sdone, vdone, adone, moved, ready = (k.sem(f"rope_{n}") for n in (
            "turned", "sdone", "vdone", "adone", "moved", "ready"))
        block = ctx.enter_context(nc.Block())
        f = proj[0:HEADS, 16, :]
        b = k.params[0:HEADS, k.col["b_forget"]:k.col["b_forget"] + 1]
        work = [(x, h) for h in range(HEADS) for x in (q, kk)]

        @block.tensor
        def _(pe):
            for n, (x, h) in enumerate(work):
                if n >= 4:
                    pe.wait_ge(sdone, n - 3)
                nc.tensor.matmul(k.bank[n % 4][0:QK, 0:TA], k.rope_turn[0:QK, 0:QK], x[0:QK, h, :],
                                 start=True, stop=True).then_inc(turned, 1)

        @block.scalar
        def _(act):
            act.wait_ge(vdone, 1)
            nc.scalar.activation(g[:, 1, :], g[:, 0, :], ACT.Abs).then_inc(adone, 1)
            act.wait_ge(adone, 1)
            nc.scalar.activation(g[:, 1, :], g[:, 1, :], ACT.Exp, scale=-1.0).then_inc(adone, 1)
            act.wait_ge(adone, 2)
            nc.scalar.activation(g[:, 1, :], g[:, 1, :], ACT.Ln, bias=1.0).then_inc(adone, 1)

        @block.vector
        def _(dve):
            link = Chain(dve, vdone)
            link(nc.vector.tensor_scalar(g[:, 0, :], f, b, None, ALU.add))
            link(nc.vector.memset(zeros[:, :], 1.0))
            link(nc.vector.memset(gates_q[0:2, :, :], 1.0))
            link(nc.vector.memset(gates_k[0:2, :, :], 1.0))
            dve.wait_ge(adone, 3)
            link(nc.vector.scalar_tensor_tensor(out=g[:, 2, :], in0=g[:, 0, :], scalar=0.0, in1=g[:, 1, :],
                                                op0=ALU.min, op1=ALU.subtract))
            link(nc.vector.tensor_tensor_scan(g[:, 3, :], zeros[:, :], g[:, 2, :], 0.0, ALU.mult, ALU.add))
            link(nc.vector.tensor_scalar(g[:, 0, :], g[:, 3, :], -1.0, None, ALU.mult))
            nc.vector.nop().then_inc(ready, 1)
            for n, (x, h) in enumerate(work):
                dve.wait_ge(turned, n + 1)
                link(nc.vector.tensor_tensor(tmp[0:QK, n % 2, :], k.bank[n % 4][0:QK, 0:TA], k.rope_sin[0:QK, :],
                                             ALU.mult))
                nc.vector.tensor_tensor(x[0:QK, h, :], x[0:QK, h, :], k.rope_cos[0:QK, :], ALU.mult).then_inc(sdone, 1)
                dve.wait_ge(sdone, n + 1)
                nc.vector.tensor_tensor(x[0:QK, h, :], x[0:QK, h, :], tmp[0:QK, n % 2, :], ALU.add)

        @block.gpsimd
        def _(pool):
            pool.wait_ge(ready, 1)
            pool.dma_start(gates_q[0:1, :, :], g[:, 3, :]).then_inc(moved, 16)
            pool.dma_start(gates_k[1:2, :, :], g[:, 0, :]).then_inc(moved, 16)
            pool.wait_ge(moved, 32)


def attention_stage(k, q, kk, fq, fk, gates_q, gates_k, vm, o):
    nc = k.nc
    units = [(h, t) for h in range(2 * HEADS) for t in range(2)]
    KT = [(0, META), (META, P), (META + P, P)]
    with ExitStack() as ctx:
        s = ctx.enter_context(nc.sbuf_tensor("scores", [P, 2, TA], F32))
        pr = ctx.enter_context(nc.sbuf_tensor("probs", [P, 2, TA], F32))
        pt = ctx.enter_context(nc.sbuf_tensor("probs_turned", [P, 2, 3 * P], F32))
        st = ctx.enter_context(nc.sbuf_tensor("softmax_stats", [P, 2, 4], F32))
        scored, masked, maxed, powered, inverted, scaled, turned, moved, mixed, kept = (
            k.sem(f"attn_{n}") for n in (
                "scored", "masked", "maxed", "powered", "inverted", "scaled", "turned", "moved", "mixed", "kept"))
        block = ctx.enter_context(nc.Block())

        @block.tensor
        def _(pe):
            def scores(u):
                h, t = units[u]
                K = META + (t + 1) * P
                q0 = META + t * P
                if u >= 2:
                    pe.wait_ge(masked, u - 1)
                ps = k.bank[u % 2][:, 0:K]
                if h < HEADS:
                    nc.tensor.matmul(ps, q[0:QK, h, q0:q0 + P], kk[0:QK, h, 0:K], start=True, stop=True)\
                        .then_inc(scored, 1)
                else:
                    g, r = h - HEADS, (h % 2) * RH
                    nc.tensor.matmul(ps, fq[r:r + RH, g // 2, q0:q0 + P], fk[r:r + RH, g // 2, 0:K],
                                     start=True, stop=False)
                    nc.tensor.matmul(ps, gates_q[0:2, g, q0:q0 + P], gates_k[0:2, g, 0:K], start=False, stop=True)\
                        .then_inc(scored, 1)

            def turn(u):
                h, t = units[u]
                pe.wait_ge(scaled, u + 1)
                if u >= 2:
                    pe.wait_ge(moved, u - 1)
                for c in range(t + 2):
                    k0, n = KT[c]
                    last = nc.tensor.transpose(k.bank[2 + u % 2][0:n, c * P:(c + 1) * P], pr[:, u % 2, k0:k0 + n],
                                               k.ident[:, :])
                last.then_inc(turned, 1)

            def mix(u):
                h, t = units[u]
                pe.wait_ge(moved, u + 1)
                r = (h % 2) * RH
                if u >= 4:
                    pe.wait_ge(kept, u - 3)
                for c in range(t + 2):
                    _, n = KT[c]
                    last = nc.tensor.matmul(k.bank[4 + u % 4][r:r + RH, 0:P], vm[0:n, c, h * RH:(h + 1) * RH],
                                            pt[0:n, u % 2, c * P:(c + 1) * P], start=(c == 0), stop=(c == t + 1))
                last.then_inc(mixed, 1)

            for u in range(len(units) + 2):
                if u < len(units):
                    scores(u)
                if 1 <= u <= len(units):
                    turn(u - 1)
                if u >= 2:
                    mix(u - 2)

        @block.vector
        def _(dve):
            for u in range(len(units) + 1):
                if u < len(units):
                    h, t = units[u]
                    K = META + (t + 1) * P
                    dve.wait_ge(scored, u + 1)
                    if u >= 2:
                        dve.wait_ge(powered, u - 1)
                    nc.vector.tensor_copy(s[:, u % 2, 0:K - P], k.bank[u % 2][:, 0:K - P])
                    nc.vector.tensor_tensor(s[:, u % 2, K - P:K], k.bank[u % 2][:, K - P:K], k.causal[:, :],
                                            ALU.add).then_inc(masked, 1)
                    dve.wait_ge(masked, u + 1)
                    nc.vector.tensor_reduce(st[:, u % 2, 0:1], s[:, u % 2, 0:K], AX.X, ALU.max, negate=True)\
                        .then_inc(maxed, 1)
                    dve.wait_ge(powered, u + 1)
                    nc.vector.reciprocal(st[:, u % 2, 2:3], st[:, u % 2, 1:2]).then_inc(inverted, 1)
                    dve.wait_ge(inverted, u + 1)
                    if u >= 2:
                        dve.wait_ge(turned, u - 1)
                    nc.vector.tensor_scalar(pr[:, u % 2, 0:K], s[:, u % 2, 0:K], st[:, u % 2, 2:3], None, ALU.mult)\
                        .then_inc(scaled, 1)
                if u >= 1:
                    h, t = units[u - 1]
                    dve.wait_ge(turned, u)
                    if u >= 3:
                        dve.wait_ge(mixed, u - 2)
                    b = k.bank[2 + (u - 1) % 2]
                    nc.vector.tensor_copy(pt[0:META, (u - 1) % 2, 0:P], b[0:META, 0:P])
                    nc.vector.tensor_copy(pt[:, (u - 1) % 2, P:P * (t + 2)], b[:, P:P * (t + 2)]).then_inc(moved, 1)

        @block.scalar
        def _(act):
            for u in range(len(units) + 2):
                if u < len(units):
                    h, t = units[u]
                    K = META + (t + 1) * P
                    act.wait_ge(maxed, u + 1)
                    nc.scalar.activation(s[:, u % 2, 0:K], s[:, u % 2, 0:K], ACT.Exp, bias=st[:, u % 2, 0:1],
                                         accum_out=st[:, u % 2, 1:2]).then_inc(powered, 1)
                if u >= 2:
                    h, t = units[u - 2]
                    r = (h % 2) * RH
                    act.wait_ge(mixed, u - 1)
                    nc.scalar.activation(o[r:r + RH, h // 2, t * P:(t + 1) * P],
                                         k.bank[4 + (u - 2) % 4][r:r + RH, 0:P], ACT.Copy).then_inc(kept, 1)


def program(nc, a):
    with ExitStack() as ctx:
        k = Kernel()
        k.nc, k.a, k.stage_sems, k.sem_count = nc, a, [], 0
        k.sb = lambda name, shape, dt=F32: ctx.enter_context(nc.sbuf_tensor(name, shape, dt))
        k.bank = [ctx.enter_context(nc.psum_tensor(f"bank_{b}", [P, 512], F32)) for b in range(8)]
        first_model(k, ctx)
        k.clear()


def first_segments(k, a):
    w = lambda n: a[n][0]
    k.in_tiles = [(0, 256), (256, 160)] + [(416 + 256 * t, 256) for t in range(5)] + [(1696, 264)]
    seg = {}
    for n in ("1", "2"):
        seg["gu" + n] = Segment(4 * 11 // 2, lambda i, j, n=n: [columns(
            w(f"w{n}_gate" if j % 2 == 0 else f"w{n}_up"), DC, (i * 3 + j // 2) * 256, 256)])

        def down(i, j, n=n):
            src = w(f"w{n}_down").rearrange("(k p) m -> p k m", p=P)
            src = src[:, (j % 2) * 11:(j % 2) * 11 + 11, ds((i * 3 + j // 2) * P, P)]
            return [(lambda s: s[:, 0:11 * P].rearrange("p (k m) -> p k m", k=11), src)]
        seg["down" + n] = Segment(16, down)
    seg["in"] = Segment(8, lambda i, j: [columns(w("w_in"), DC, *k.in_tiles[i * RING + j])])
    seg["expand"] = Segment(2, lambda i, j: [columns(w("w_uq"), 2, 0, HEADS * QK) if j == 0
                                             else columns(w("w_ukv"), 1, 0, D)])
    seg["out"] = Segment(4, lambda i, j: [columns(w("w_out"), DC, j * 256, 256)])
    return seg


def ffn(k, n, h, u, T, t0, seg, gains, to):
    nc = k.nc
    norm_stage(k, f"ffn{n}", h, DC, D, EPS, [(t0, T, gains, None)], u)
    with nc.sbuf_tensor(f"hidden{n}", [P, FC, T - t0], F32) as hidden:
        gate_up_stage(k, f"gu{n}", seg["gu" + n], u[:, :, t0:T], T - t0, hidden)
        linear_stage(k, f"down{n}", seg["down" + n], half_tiles(11), lambda f: hidden[:, f, :], T - t0,
                     lambda dve, m, ps: nc.vector.scalar_tensor_tensor(
                         out=flat(to[:, ds(m, 1), :]), in0=ps[:, 0:T - t0], scalar=0.5,
                         in1=flat(h[:, ds(m, 1), t0:T]), op0=ALU.mult, op1=ALU.add), 3)


def param(k, name, n=1, at=0):
    return k.params[:, k.col[name] + at:k.col[name] + at + n]


def first_model(k, ctx):
    nc, a = k.nc, k.a
    seg = first_segments(k, a)
    order = [seg[n] for n in ("gu1", "down1", "in", "expand", "out", "gu2", "down2")]
    k.seg = seg
    more = second_segments(k, a)
    k.stream = Stream(nc, ctx, order + more)
    k.ident, k.ones, k.head_ones, k.causal = (k.sb(n, [P, P]) for n in ("ident", "ones", "head_ones", "causal"))
    k.rope_cos, k.rope_sin = (k.sb(n, [P, TA]) for n in ("rope_cos_sb", "rope_sin_sb"))
    k.rope_turn = k.sb("rope_turn_sb", [P, QK])
    k.h = k.sb("h", [P, DC, TA])
    k.x = k.sb("x", [P, DC, TB])
    stage_setup(k)
    with nc.sbuf_tensor("u1", [P, DC, TA], F32) as u:
        ffn(k, "1", k.h, u, TA, 0, seg, param(k, "g_ffn1", DC), k.h[:, :, :])
    with ExitStack() as c2:
        sb = lambda n, s: c2.enter_context(nc.sbuf_tensor(n, s, F32))
        proj = sb("proj", [P, 17, TA])
        fqk = sb("fox_qk", [P, 8, TA])
        o = sb("attn_out", [P, DC, SEQ])
        with nc.sbuf_tensor("u_mix", [P, DC, TA], F32) as u:
            norm_stage(k, "mix", k.h, DC, D, EPS, [(0, TA, param(k, "g_mix", DC), None)], u)
            in_proj_stage(k, seg["in"], u, proj)
        q = sb("q", [P, HEADS, TA])
        kk = sb("kk", [P, HEADS, TA])
        vm = sb("v_tokens", [P, 3, D])
        gq = sb("gates_q", [2, HEADS, TA])
        gk = sb("gates_k", [2, HEADS, TA])
        norm_stage(k, "cq", proj[:, 0:2, :], 2, 2 * P, EPS, [(0, TA, param(k, "g_cq", 2), None)], proj[:, 0:2, :])
        norm_stage(k, "ckv", proj[:, 2:3, :], 1, P, EPS, [(0, TA, param(k, "g_ckv", 1), None)], proj[:, 2:3, :])
        expand_stage(k, seg["expand"], proj, q, kk, vm)
        head_norm_stage(k, "qn", q, q, QK, HEADS, QK, k.ones, param(k, "g_q_mla"), QK ** -0.5, META, SEQ)
        head_norm_stage(k, "kn", kk, kk, QK, HEADS, QK, k.ones, param(k, "g_k_mla"), 1.0, 0, TA)
        head_norm_stage(k, "fqn", proj[:, 4:8, :], fqk[:, 0:4, :], P, 4, RH, k.head_ones, param(k, "g_q_fox"),
                        RH ** -0.5, META, SEQ)
        head_norm_stage(k, "fkn", proj[:, 8:12, :], fqk[:, 4:8, :], P, 4, RH, k.head_ones, param(k, "g_k_fox"),
                        1.0, 0, TA)
        rope_stage(k, q, kk, proj, gq, gk)
        attention_stage(k, q, kk, fqk[:, 0:4, :], fqk[:, 4:8, :], gq, gk, vm, o)
        linear_stage(k, "attn_out", seg["out"], whole_tiles(DC, 256), lambda f: o[:, f, :], SEQ,
                     lambda dve, m, ps: nc.vector.tensor_tensor(
                         k.h[:, m, META:TA], k.h[:, m, META:TA], ps[:, 0:SEQ], ALU.add), 4)
    with nc.sbuf_tensor("u2", [P, DC, TA], F32) as u:
        ffn(k, "2", k.h, u, TA, META, seg, param(k, "g_ffn2", DC), k.x[:, :, 0:SEQ])
    k.clear()
    second_model(k, ctx)


def shape_tables():
    half = ROPE // 2
    inv = 1.0 / (10000.0 ** (np.arange(half, dtype=np.float32) / np.float32(half)))
    ang = np.arange(TA, dtype=np.float32)[None, :] * inv.astype(np.float32)[:, None]
    cos, sin = np.ones((QK, TA), np.float32), np.zeros((QK, TA), np.float32)
    cos[NOPE:NOPE + half] = cos[NOPE + half:] = np.cos(ang)
    sin[NOPE:NOPE + half] = sin[NOPE + half:] = np.sin(ang)
    turn = np.zeros((QK, QK), np.float32)
    for i in range(half):
        turn[NOPE + half + i, NOPE + i] = -1.0
        turn[NOPE + i, NOPE + half + i] = 1.0
    return {"rope_cos": cos, "rope_sin": sin, "rope_turn": turn, "rwkv_masks": rwkv_masks()}


def second_segments(k, a):
    seg = k.seg
    w = lambda n: a[n][0]
    for l in range(2):
        seg[f"ada{l}"] = Segment(24, lambda i, j, l=l: [columns(a["ada_w_2"][l], DC, (i * RING + j) * 256, 256)])

        def expert(i, j, l=l):
            if j < 4:
                src = a["moe_w_gate_2" if j % 2 == 0 else "moe_w_up_2"][l]
                src = src.rearrange("e (k p) m -> p e k m", p=P)[:, ds(i, 1), :, (j // 2) * 256:(j // 2) * 256 + 256]
                return [(lambda s: s[:, 0:DC * 256].rearrange("p (e k m) -> p e k m", e=1, k=DC), src)]
            src = a["moe_w_down_2"][l].rearrange("e (k p) m -> p e k m", p=P)
            src = src[:, ds(i, 1), :, (j - 4) * 512:(j - 4) * 512 + 512]
            return [(lambda s: s[:, 0:4 * 512].rearrange("p (e k m) -> p e k m", e=1, k=4), src)]
        seg[f"moe{l}"] = Segment(RING * NE, expert)
    seg["ga_u"] = Segment(8, lambda i, j: [columns(w("ga_w_in_2"), DC, (i * RING + j) * 256, 256)])
    seg["ga_v"] = Segment(8, lambda i, j: [columns(w("ga_w_in_2"), DC, GW + (i * RING + j) * 256, 256)])
    seg["ga_out"] = Segment(8, lambda i, j: [columns(w("ga_w_out_2"), GC, (i * RING + j) * P, P)])
    order = ["ada0", "ga_u", "ga_v", "ga_out", "moe0", "ada1"]
    order += rwkv_segments(k, a)
    order += ["moe1"]
    return [seg[n] for n in order]


def mod_stage(k, l, extra):
    nc = k.nc
    cond = k.cond
    if l == 0:
        ready = k.sem("cond_ready")
        with nc.Block() as block:
            @block.scalar
            def _(act):
                nc.scalar.activation(cond[:, :, 0], param(k, "c", DC), ACT.Silu)
                nc.scalar.activation(cond[:, :, 1], param(k, "c_ctx", DC), ACT.Silu).then_inc(ready, 1)
                act.wait_ge(ready, 1)
    linear_stage(k, f"ada{l}", k.seg[f"ada{l}"], whole_tiles(DC, 256), lambda f: cond[:, f, :], 2,
                 lambda dve, m, ps: nc.vector.tensor_copy(
                     k.mod[:, :, ds(m, 1)].rearrange("p v a -> p (v a)"), ps[:, 0:2]), 6)
    done = k.sem("mod_done")
    with nc.Block() as block:
        @block.vector
        def _(dve):
            link = Chain(dve, done)
            for v in range(2):
                link(nc.vector.tensor_tensor(k.mod[:, v, :], k.mod[:, v, :], param(k, "ada_b", 48, 48 * l), ALU.add))
            for v in range(2):
                for g, at, n in ((k.gain1, DC, "norm1"), (k.gain2, 4 * DC, "norm2")):
                    link(nc.vector.scalar_tensor_tensor(out=g[:, v, :], in0=k.mod[:, v, at:at + DC], scalar=1.0,
                                                        in1=param(k, n, DC, DC * l), op0=ALU.add, op1=ALU.mult))
            if extra is not None:
                extra(link)


def gmlp(k):
    nc, a, seg = k.nc, k.a, k.seg
    V = [(0, SEQ), (SEQ, TB)]
    parts = [(t0, t1, k.gain1[:, v, :], k.mod[:, v, 0:DC]) for v, (t0, t1) in enumerate(V)]
    with nc.sbuf_tensor("gm_u", [P, GC, TB], F32) as u, nc.sbuf_tensor("gm_v", [P, 4, GW], F32) as v:
        with nc.sbuf_tensor("gm_h", [P, DC, TB], F32) as h:
            norm_stage(k, "gm_norm", k.x, DC, D, EPS, parts, h)
            linear_stage(k, "gm_u", seg["ga_u"], whole_tiles(DC, 256), lambda f: h[:, f, :], TB,
                         lambda act, m, ps: nc.scalar.activation(
                             u[:, m, :], ps[:, :], ACT.Gelu, bias=param(k, "ga_b_u", 1, m)), 4, on_scalar=True)
            gmlp_v_stage(k, h, v)
        gmlp_norm_stage(k, v)
        gmlp_spatial_stage(k, u, v)

        def write(dve, m, ps):
            for vv, (t0, t1) in enumerate(V):
                last = nc.vector.scalar_tensor_tensor(
                    out=k.x[:, m, t0:t1], in0=ps[:, t0:t1], scalar=k.mod[:, vv, 2 * DC + m:2 * DC + m + 1],
                    in1=k.x[:, m, t0:t1], op0=ALU.mult, op1=ALU.add)
            return last
        linear_stage(k, "gm_out", seg["ga_out"], whole_tiles(GC, P), lambda f: u[:, f, :], TB, write, 6)


def gmlp_v_stage(k, h, v):
    nc, seg = k.nc, k.seg["ga_v"]
    with ExitStack() as ctx:
        bias = ctx.enter_context(nc.sbuf_tensor("gm_bias", [P, GW], F32))
        landed, made, biased = (k.sem(f"gmv_{n}") for n in ("landed", "made", "biased"))
        block = ctx.enter_context(nc.Block())
        units = [(j, t) for j in range(seg.tiles) for t in range(4)]

        @block.sync
        def _(sp):
            for j in range(seg.tiles):
                sp.wait_ge(made, 4 * (j + 1))
                k.stream.start_number(sp, seg.first + j + RING)

        @block.tensor
        def _(pe):
            for n, (j, t) in enumerate(units):
                if t == 0:
                    k.stream.wait(pe, seg, j // RING, j % RING)
                if n >= 4:
                    pe.wait_ge(biased, n - 3)
                w = k.stream.slot(seg, j)
                for f in range(DC):
                    last = nc.tensor.matmul(k.bank[n % 4][:, 0:256], h[:, f, t * P:(t + 1) * P],
                                            w[:, f * 256:(f + 1) * 256], start=(f == 0), stop=(f == DC - 1))
                last.then_inc(made, 1)

        @block.vector
        def _(dve):
            dve.wait_ge(landed, 16)
            for n, (j, t) in enumerate(units):
                dve.wait_ge(made, n + 1)
                nc.vector.tensor_tensor(v[:, t, j * 256:(j + 1) * 256], k.bank[n % 4][:, 0:256],
                                        bias[:, j * 256:(j + 1) * 256], ALU.add).then_inc(biased, 1)

        @block.scalar
        def _(act):
            act.dma_start(bias[:, :], k.a["ga_b_in_2"][0:1, GW:2 * GW].to_broadcast([P, GW])).then_inc(landed, 16)
            for n, (j, t) in enumerate(units):
                act.wait_ge(biased, n + 1)
                nc.scalar.activation(v[:, t, j * 256:(j + 1) * 256], v[:, t, j * 256:(j + 1) * 256], ACT.Gelu)


def gmlp_norm_stage(k, v):
    nc = k.nc
    with ExitStack() as ctx:
        g = ctx.enter_context(nc.sbuf_tensor("gm_ln_g", [P, GW], F32))
        b = ctx.enter_context(nc.sbuf_tensor("gm_ln_b", [P, GW], F32))
        sq = ctx.enter_context(nc.sbuf_tensor("gm_sq", [P, GW], F32))
        st = ctx.enter_context(nc.sbuf_tensor("gm_st", [P, 4, 6], F32))
        landed, done, meaned, squared, rooted, ready = (k.sem(f"gmn_{n}") for n in (
            "landed", "done", "meaned", "squared", "rooted", "ready"))
        block = ctx.enter_context(nc.Block())

        @block.vector
        def _(dve):
            link = Chain(dve, done)
            for t in range(4):
                link(nc.vector.tensor_reduce(st[:, t, 0:1], v[:, t, :], AX.X, ALU.add))
                nc.vector.tensor_scalar(st[:, t, 1:2], st[:, t, 0:1], -1.0 / GW, None, ALU.mult).then_inc(meaned, 1)
            dve.wait_ge(squared, 4)
            link(nc.vector.tensor_scalar(st[:, :, 3], st[:, :, 2], 1.0 / GW, LN_EPS, ALU.mult, ALU.add))
            nc.vector.nop().then_inc(ready, 1)
            dve.wait_ge(rooted, 2)
            link(nc.vector.tensor_tensor(st[:, :, 5], st[:, :, 4], st[:, :, 4], ALU.mult))
            link(nc.vector.scalar_tensor_tensor(out=st[:, :, 5], in0=st[:, :, 5], scalar=-0.5, in1=st[:, :, 3],
                                                op0=ALU.mult, op1=ALU.mult))
            link(nc.vector.scalar_tensor_tensor(out=st[:, :, 5], in0=st[:, :, 5], scalar=1.5, in1=st[:, :, 4],
                                                op0=ALU.add, op1=ALU.mult))
            dve.wait_ge(landed, 32)
            for t in range(4):
                link(nc.vector.tensor_scalar(v[:, t, :], v[:, t, :], st[:, t, 1:2], st[:, t, 5:6], ALU.add, ALU.mult))
                link(nc.vector.tensor_tensor(v[:, t, :], v[:, t, :], g[:, :], ALU.mult))
                nc.vector.tensor_tensor(v[:, t, :], v[:, t, :], b[:, :], ALU.add)

        @block.scalar
        def _(act):
            act.dma_start(g[:, :], k.a["ga_ln_g_2"].to_broadcast([P, GW])).then_inc(landed, 16)
            act.dma_start(b[:, :], k.a["ga_ln_b_2"].to_broadcast([P, GW])).then_inc(landed, 16)
            for t in range(4):
                act.wait_ge(meaned, t + 1)
                if t:
                    act.wait_ge(squared, t)
                nc.scalar.activation(sq[:, :], v[:, t, :], ACT.Square, bias=st[:, t, 1:2],
                                     accum_out=st[:, t, 2:3]).then_inc(squared, 1)
            act.wait_ge(ready, 1)
            nc.scalar.activation(st[:, :, 4], st[:, :, 3], ACT.Ln).then_inc(rooted, 1)
            act.wait_ge(rooted, 1)
            nc.scalar.activation(st[:, :, 4], st[:, :, 4], ACT.Exp, scale=-0.5).then_inc(rooted, 1)


def gmlp_spatial_stage(k, u, v):
    nc = k.nc
    with ExitStack() as ctx:
        ws = ctx.enter_context(nc.sbuf_tensor("gm_ws", [P, GC, P], F32))
        wt = ctx.enter_context(nc.sbuf_tensor("gm_wt", [P, GC, P], F32))
        bs = ctx.enter_context(nc.sbuf_tensor("gm_bs", [1, GC, P], F32))
        landed, blanded, turned, copied, mixed, used = (k.sem(f"gms_{n}") for n in (
            "landed", "blanded", "turned", "copied", "mixed", "used"))
        block = ctx.enter_context(nc.Block())

        @block.tensor
        def _(pe):
            pe.wait_ge(landed, 16)
            pe.wait_ge(blanded, 16)
            for q in range(4):
                for c in range(4):
                    last = nc.tensor.transpose(k.bank[q][:, c * P:(c + 1) * P], ws[:, 4 * q + c, :], k.ident[:, :])
                last.then_inc(turned, 1)
            for g in range(GC):
                pe.wait_ge(copied, g // 4 + 1)
                if g >= 4:
                    pe.wait_ge(used, g - 3)
                for t in range(4):
                    ps = k.bank[4 + g % 4][:, t * P:(t + 1) * P]
                    nc.tensor.matmul(ps, v[:, t, g * P:(g + 1) * P], wt[:, g, :], start=True, stop=False)
                    last = nc.tensor.matmul(ps, k.ones[0:1, :], bs[0:1, g, :], start=False, stop=True)
                last.then_inc(mixed, 1)

        @block.vector
        def _(dve):
            for q in range(4):
                dve.wait_ge(turned, q + 1)
                nc.vector.tensor_copy(wt[:, 4 * q:4 * q + 4, :].rearrange("p a b -> p (a b)"), k.bank[q][:, :])\
                    .then_inc(copied, 1)
            for g in range(GC):
                dve.wait_ge(mixed, g + 1)
                nc.vector.tensor_tensor(u[:, g, :], k.bank[4 + g % 4][:, :], u[:, g, :], ALU.mult).then_inc(used, 1)

        @block.scalar
        def _(act):
            act.dma_start(ws[:, :, :], k.a["ga_w_s_2"][0].rearrange("g p q -> p g q")).then_inc(landed, 16)
            act.dma_start(bs[:, :, :], k.a["ga_b_s_2"]).then_inc(blanded, 16)


def route_stage(k, l, hm, T, rows, slot_token, table, dest, desti, wts, out_rows):
    nc, a = k.nc, k.a
    TT = T // P
    nov = 2 * T // SLOTS - 1
    cap = NE * SLOTS + nov * SLOTS
    with ExitStack() as ctx:
        sb = lambda n, s, dt=F32: ctx.enter_context(nc.sbuf_tensor(f"rt{l}_{n}", s, dt))
        wr = sb("wr", [P, DC, NG + NE])
        bias = sb("bias", [P, NG + NE])
        hrow = sb("hrow", [P, 2, D])
        L = sb("logits", [P, TT, NG + NE])
        A = sb("assigned", [P, TT, NE])
        one = sb("onehots", [P, TT, 2, NE])
        w4 = sb("w4", [P, 4 * NG])
        gexp = sb("gexp", [P, TT, NG])
        rank = sb("rank", [P, NE])
        prod = sb("prod", [P, NE])
        lm = sb("lm", [P, 2, NE])
        st = sb("st", [P, TT, 16])
        before = sb("before", [P, P])
        pos = sb("pos", [P, TT, NE])
        cnt = sb("cnt", [P, 6, NE])
        eid = sb("eid", [P, 4])
        ones_row = sb("ones_row", [P, NE])
        ids = sb("ids", [P, TT], I32)
        tab_f = sb("tab_f", [P, 2])
        tab_i = sb("tab_i", [P, 2], I32)
        zero = sb("zero", [P, SLOTS], I32)
        zero_row = sb("zero_row", [SLOTS, D])
        names = ("wl", "made", "vdone", "exped", "gmaxed", "assigned", "placed", "rturned", "rcopied", "rstored0",
                 "rstored1", "consts", "zeroed", "scattered", "destined", "diffed", "tabled", "cleared")
        (wl, made, vdone, exped, gmaxed, assigned, placed, rturned, rcopied, rstored0, rstored1, consts, zeroed,
         scattered, destined, diffed, tabled, cleared) = (k.sem(f"rt_{n}") for n in names)
        rstored = (rstored0, rstored1)
        block = ctx.enter_context(nc.Block())

        @block.sync
        def _(sp):
            sp.dma_start(wr[:, :, 0:NG], a["moe_w_grp_2"][l].rearrange("(k p) m -> p k m", p=P)).then_inc(wl, 16)
            sp.dma_start(wr[:, :, NG:], a["moe_w_exp_2"][l].rearrange("(k p) m -> p k m", p=P)).then_inc(wl, 16)
            sp.dma_start(bias[:, 0:NG], a["moe_b_grp_2"][l:l + 1, :].to_broadcast([P, NG])).then_inc(wl, 16)
            sp.dma_start(bias[:, NG:], a["moe_b_exp_2"][l:l + 1, :].to_broadcast([P, NE])).then_inc(wl, 16)
            for t in range(TT):
                sp.wait_ge(rcopied, 2 * t + 2)
                sp.dma_start(rows[t * P:(t + 1) * P, :], hrow[:, t % 2, :]).then_inc(rstored[t % 2], 16)
            sp.wait_ge(consts, 8)
            for b in range(nov):
                sp.dma_start(out_rows[(NE + b) * SLOTS:(NE + b + 1) * SLOTS, :], zero_row[:, :]).then_inc(cleared, 16)
            sp.wait_ge(cleared, 16 * nov)
            for b in range(2):
                sp.wait_ge(rstored[b], 16 * (TT // 2))

        @block.gpsimd
        def _(pool):
            pool.memset(zero[:, :], 0).then_inc(consts, 1)
            pool.wait_ge(consts, 1)
            nblk = cap // SLOTS
            pool.dma_start(slot_token.rearrange("(b s) o -> b (s o)", s=SLOTS), zero[0:nblk, :]).then_inc(zeroed, 16)
            pool.iota(rank[:, :], [[-1, NE]], base=NE, channel_multiplier=0,
                      allow_small_or_imprecise_dtypes=True).then_inc(consts, 1)
            pool.iota(w4[:, 0:NG], [[-1, NG]], base=NG, channel_multiplier=0,
                      allow_small_or_imprecise_dtypes=True).then_inc(consts, 1)
            pool.iota(eid[:, 0:1], [[0, 1]], base=0, channel_multiplier=1,
                      allow_small_or_imprecise_dtypes=True).then_inc(consts, 1)
            pool.iota(ids[:, :], [[P, TT]], base=0, channel_multiplier=1).then_inc(consts, 1)
            pool.memset(before[:, :], 1.0).then_inc(consts, 1)
            pool.wait_ge(consts, 6)
            pool.affine_select(out=before[:, :], in_=before[:, :], compare_op=ALU.is_ge, fill=0.0, base=-1,
                               pattern=[[1, P]], channel_multiplier=-1).then_inc(consts, 1)
            pool.memset(zero_row[:, :], 0.0).then_inc(consts, 1)
            pool.wait_ge(zeroed, 16)
            pool.wait_ge(destined, 1)
            for t in range(TT):
                for c in range(2):
                    pool.indirect_dma_start(slot_token, bass.IndirectOffsetOnAxis(ap=desti[:, t, c:c + 1], axis=0),
                                            ids[:, t:t + 1], None).then_inc(scattered, 16)
            pool.wait_ge(scattered, 32 * TT)
            pool.wait_ge(tabled, 1)
            pool.dma_start(table, tab_i[0:16, :]).then_inc(zeroed, 16)
            pool.wait_ge(zeroed, 32)

        @block.tensor
        def _(pe):
            pe.wait_ge(wl, 64)
            for t in range(TT):
                for f in range(DC):
                    last = nc.tensor.matmul(k.bank[0][:, 64 * t:64 * t + NG + NE], hm[:, f, t * P:(t + 1) * P],
                                            wr[:, f, :], start=(f == 0), stop=(f == DC - 1))
                last.then_inc(made, 1)
            for t in range(TT):
                for half in range(2):
                    n = 2 * t + half
                    if n >= 4:
                        pe.wait_ge(rcopied, n - 3)
                    for c in range(4):
                        last = nc.tensor.transpose(k.bank[1 + n % 4][:, c * P:(c + 1) * P],
                                                   hm[:, half * 4 + c, t * P:(t + 1) * P], k.ident[:, :])
                    last.then_inc(rturned, 1)
            pe.wait_ge(consts, 7)
            for t in range(TT):
                pe.wait_ge(assigned, t + 1)
                for s in range(t + 1):
                    last = nc.tensor.matmul(k.bank[5][:, NE * t:NE * t + NE], before[:, :] if s == t else k.ones[:, :],
                                            A[:, s, :], start=(s == 0), stop=(s == t))
                last.then_inc(placed, 1)
            for s in range(TT):
                last = nc.tensor.matmul(k.bank[6][:, 0:NE], k.ones[:, :], A[:, s, :], start=(s == 0), stop=(s == TT - 1))
            last.then_inc(placed, 1)

        @block.scalar
        def _(act):
            for t in range(TT):
                act.wait_ge(gmaxed, t + 1)
                nc.scalar.activation(gexp[:, t, :], L[:, t, 0:NG], ACT.Exp, bias=st[:, t, 0:1],
                                     accum_out=st[:, t, 1:2]).then_inc(exped, 1)
                for half in range(2):
                    n = 2 * t + half
                    act.wait_ge(rturned, n + 1)
                    if t >= 2:
                        act.wait_ge(rstored[t % 2], 16 * (t // 2))
                    nc.scalar.activation(hrow[:, t % 2, half * 512:(half + 1) * 512], k.bank[1 + n % 4][:, :],
                                         ACT.Copy).then_inc(rcopied, 1)
            act.wait_ge(diffed, 1)
            nc.scalar.activation(st[:, :, 9], st[:, :, 8], ACT.Exp).then_inc(exped, 1)

        @block.vector
        def _(dve):
            link = Chain(dve, vdone)
            dve.wait_ge(consts, 3)
            link(nc.vector.memset(ones_row[:, :], 1.0))
            for t in range(TT):
                lt = L[:, t, :]
                s = lambda n: st[:, t, n:n + 1]
                if t == 0:
                    dve.wait_ge(made, TT)
                link(nc.vector.tensor_tensor(lt, k.bank[0][:, 64 * t:64 * t + NG + NE], bias[:, :], ALU.add))
                link(nc.vector.tensor_reduce(s(2), lt[:, 0:NG], AX.X, ALU.max))
                nc.vector.tensor_scalar(s(0), s(2), -1.0, None, ALU.mult).then_inc(gmaxed, 1)
                link(nc.vector.scalar_tensor_tensor(out=w4[:, 12:16], in0=lt[:, 0:NG], scalar=s(2), in1=w4[:, 0:NG],
                                                    op0=ALU.is_equal, op1=ALU.mult))
                link(nc.vector.tensor_reduce(s(3), w4[:, 12:16], AX.X, ALU.max))
                link(nc.vector.tensor_scalar(w4[:, 12:16], w4[:, 0:NG], s(3), None, ALU.is_equal))
                link(nc.vector.tensor_scalar(w4[:, 12:16], w4[:, 12:16], -NEG, NEG, ALU.mult, ALU.add))
                for g in range(NG):
                    last = nc.vector.tensor_scalar(lm[:, 0, g * EG:(g + 1) * EG],
                                                   lt[:, NG + g * EG:NG + (g + 1) * EG], w4[:, 12 + g:13 + g], None,
                                                   ALU.add)
                link(last)
                for c in range(2):
                    link(nc.vector.tensor_reduce(s(4 + c), lm[:, c, :], AX.X, ALU.max))
                    link(nc.vector.scalar_tensor_tensor(out=prod[:, :], in0=lm[:, c, :], scalar=s(4 + c),
                                                        in1=rank[:, :], op0=ALU.is_equal, op1=ALU.mult))
                    link(nc.vector.tensor_reduce(s(6 + c), prod[:, :], AX.X, ALU.max))
                    link(nc.vector.tensor_scalar(one[:, t, c, :], rank[:, :], s(6 + c), None, ALU.is_equal))
                    if c == 0:
                        link(nc.vector.scalar_tensor_tensor(out=lm[:, 1, :], in0=one[:, t, 0, :], scalar=4 * NEG,
                                                            in1=lm[:, 0, :], op0=ALU.mult, op1=ALU.add))
                nc.vector.tensor_tensor(A[:, t, :], one[:, t, 0, :], one[:, t, 1, :], ALU.add).then_inc(assigned, 1)
            link(nc.vector.tensor_tensor(st[:, :, 8], st[:, :, 5], st[:, :, 4], ALU.subtract))
            nc.vector.nop().then_inc(diffed, 1)
            dve.wait_ge(exped, TT + 1)
            link(nc.vector.scalar_tensor_tensor(out=st[:, :, 10], in0=st[:, :, 9], scalar=1.0, in1=st[:, :, 1],
                                                op0=ALU.add, op1=ALU.mult))
            link(nc.vector.reciprocal(wts[:, :, 0], st[:, :, 10]))
            link(nc.vector.tensor_tensor(wts[:, :, 1], wts[:, :, 0], st[:, :, 9], ALU.mult))
            dve.wait_ge(placed, TT + 1)
            count, many, upto, front, far = (cnt[:, n, :] for n in range(5))
            link(nc.vector.tensor_copy(count, k.bank[6][:, 0:NE]))
            link(nc.vector.tensor_scalar(many, count, float(SLOTS), None, ALU.is_gt))
            for j in range(2, T // SLOTS):
                link(nc.vector.scalar_tensor_tensor(out=many, in0=count, scalar=float(SLOTS * j), in1=many,
                                                    op0=ALU.is_gt, op1=ALU.add))
            link(nc.vector.tensor_tensor_scan(upto, ones_row[:, :], many, 0.0, ALU.mult, ALU.add))
            link(nc.vector.tensor_tensor(front, upto, many, ALU.subtract))
            link(nc.vector.scalar_tensor_tensor(out=far, in0=front, scalar=-1.0, in1=rank[:, :], op0=ALU.add,
                                                op1=ALU.add))
            link(nc.vector.tensor_scalar(far, far, float(SLOTS), None, ALU.mult))
            for t in range(TT):
                link(nc.vector.tensor_copy(pos[:, t, :], k.bank[5][:, NE * t:NE * t + NE]))
                for c in range(2):
                    s = lambda n: st[:, t, n:n + 1]
                    link(nc.vector.tensor_tensor(prod[:, :], pos[:, t, :], one[:, t, c, :], ALU.mult))
                    link(nc.vector.tensor_reduce(s(11), prod[:, :], AX.X, ALU.add))
                    link(nc.vector.tensor_tensor(prod[:, :], far, one[:, t, c, :], ALU.mult))
                    link(nc.vector.tensor_reduce(s(12), prod[:, :], AX.X, ALU.add))
                    link(nc.vector.tensor_scalar(s(13), s(11), float(SLOTS), None, ALU.is_ge))
                    link(nc.vector.scalar_tensor_tensor(out=s(12), in0=s(12), scalar=s(13), in1=s(11),
                                                        op0=ALU.mult, op1=ALU.add))
                    link(nc.vector.tensor_scalar(s(14), s(6 + c), -float(SLOTS), float(NE * SLOTS), ALU.mult, ALU.add))
                    link(nc.vector.tensor_tensor(dest[:, t, c:c + 1], s(14), s(12), ALU.add))
            link(nc.vector.tensor_copy(desti[:, :, :], dest[:, :, :]))
            nc.vector.nop().then_inc(destined, 1)
            link(nc.vector.tensor_scalar(prod[:, :], front, eid[:, 0:1], None, ALU.is_le))
            link(nc.vector.scalar_tensor_tensor(out=prod[:, :], in0=upto, scalar=eid[:, 0:1], in1=prod[:, :],
                                                op0=ALU.is_gt, op1=ALU.mult))
            link(nc.vector.tensor_scalar(far, rank[:, :], -1.0, float(NE), ALU.mult, ALU.add))
            link(nc.vector.tensor_tensor(prod[:, :], prod[:, :], far, ALU.mult))
            link(nc.vector.tensor_reduce(tab_f[:, 0:1], prod[:, :], AX.X, ALU.add))
            link(nc.vector.tensor_copy(tab_f[:, 1:2], upto[:, NE - 1:NE]))
            link(nc.vector.tensor_copy(tab_i[:, :], tab_f[:, :]))
            nc.vector.nop().then_inc(tabled, 1)


def experts_stage(k, l, rows, slots, out_rows):
    nc = k.nc
    seg = k.seg[f"moe{l}"]
    with ExitStack() as ctx:
        sb = lambda n, s, dt=F32: ctx.enter_context(nc.sbuf_tensor(f"ex{l}_{n}", s, dt))
        idx = [sb(f"idx{s}", [SLOTS, 1], I32) for s in range(2)]
        xg = sb("xg", [SLOTS, 2, D])
        xt = sb("xt", [P, 2, DC * SLOTS])
        act_out = sb("silu", [P, 2, 4 * SLOTS])
        hid = sb("hidden", [P, 2, 4 * SLOTS])
        y = sb("y", [SLOTS, 2, D])
        (picked, got0, got1, turned, copied, spent, silued, gated, kept_a, kept_d, put0, put1) = (
            k.sem(f"ex_{n}") for n in (
                "picked", "got0", "got1", "turned", "copied", "spent", "silued", "gated", "kept_a", "kept_d",
                "put0", "put1"))
        asked = k.sem("ex_asked")
        got, put = (got0, got1), (put0, put1)
        block = ctx.enter_context(nc.Block())
        half = 2 * SLOTS

        def pairs(eng, body):
            with eng.Fori(0, NE // 2 - 1) as i:
                for s in range(2):
                    body(i, s, i * 2 + s, False)
            for s in range(2):
                body(NE // 2 - 1, s, NE - 2 + s, s == 1)

        @block.sync
        def _(sp):
            k.stream.feed(sp, seg, spent, lambda j: (1, 1, 2, 2, 3, 4)[j], 4)

        @block.gpsimd
        def _(pool):
            def gather(i, s, e, last):
                pool.wait_ge(turned, e + 1)
                nc.gpsimd.tensor_copy(idx[s][:, :], slots[0:SLOTS, ds(e, 1)]).then_inc(picked, 1)
                pool.wait_ge(picked, e + 1)
                pool.sem_inc(asked, 1)
                pool.indirect_dma_start(xg[:, s, :], None, rows, bass.IndirectOffsetOnAxis(ap=idx[s][:, :], axis=0))\
                    .then_inc(got[s], 16)
            pairs(pool, gather)

        @block.tensor
        def _(pe):
            pe.sem_inc(turned, 2)

            def turn(s):
                for f in range(DC):
                    last = nc.tensor.transpose(k.bank[s][:, f * SLOTS:(f + 1) * SLOTS], xg[:, s, f * P:(f + 1) * P],
                                               k.ident[0:SLOTS, 0:SLOTS])
                last.then_inc(turned, 1)

            def expert(i, s, e, last_one):
                pe.wait_ge(copied, e + 1)
                for q in range(2):
                    for side in range(2):
                        k.stream.wait(pe, seg, e, 2 * q + side)
                    for side in range(2):
                        w = k.stream.slot(seg, 2 * q + side)
                        for c in range(2):
                            o = (2 * side + c) * SLOTS
                            for f in range(DC):
                                if not last_one and (q, side, c, f) == (1, 1, 1, DC - 1):
                                    pe.wait_ge(got[1 - s], (i + s) * 16 + 16)
                                last = nc.tensor.matmul(k.bank[2 + q][:, o:o + SLOTS],
                                                        w[:, f * 256 + c * P:f * 256 + (c + 1) * P],
                                                        xt[:, s, f * SLOTS:(f + 1) * SLOTS],
                                                        start=(f == 0), stop=(f == DC - 1))
                    last.then_inc(spent, 1)
                if not last_one:
                    turn(1 - s)
                pe.wait_ge(gated, e * 2 + 2)
                pe.wait_ge(kept_a, e + 1)
                pe.wait_ge(kept_d, e + 1)
                for n in range(2):
                    k.stream.wait(pe, seg, e, 4 + n)
                    w = k.stream.slot(seg, 4 + n)
                    for f in range(4):
                        last = nc.tensor.matmul(k.bank[4 + 2 * s + n][0:SLOTS, :], hid[:, s, f * SLOTS:(f + 1) * SLOTS],
                                                w[:, f * 512:(f + 1) * 512], start=(f == 0), stop=(f == 3))
                    last.then_inc(spent, 1)

            pe.wait_ge(got[0], 16)
            turn(0)
            pairs(pe, expert)

        @block.scalar
        def _(act):
            act.sem_inc(kept_a, 2)

            def expert(i, s, e, last_one):
                for q in range(2):
                    act.wait_ge(spent, e * 4 + q + 1)
                    nc.scalar.activation(act_out[:, s, q * half:(q + 1) * half],
                                         k.bank[2 + q][:, 0:half], ACT.Silu).then_inc(silued, 1)
                act.wait_ge(spent, e * 4 + 3)
                act.wait_ge(put[s], i * 16)
                nc.scalar.activation(y[:, s, 0:512], k.bank[4 + 2 * s][0:SLOTS, :], ACT.Copy).then_inc(kept_a, 1)
                act.wait_ge(kept_a, e + 3)
                act.wait_ge(kept_d, e + 3)
                act.dma_start(out_rows[ds(e * SLOTS, SLOTS), :], y[:, s, :]).then_inc(put[s], 16)
            pairs(act, expert)
            for s in range(2):
                act.wait_ge(put[s], 16 * (NE // 2))

        @block.vector
        def _(dve):
            dve.sem_inc(kept_d, 2)

            def copy(i, s, e):
                dve.wait_ge(turned, e + 3)
                nc.vector.tensor_copy(xt[:, s, :], k.bank[s][:, :]).then_inc(copied, 1)

            def expert(i, s, e, last_one):
                for q in range(2):
                    dve.wait_ge(silued, e * 2 + q + 1)
                    nc.vector.tensor_tensor(hid[:, s, q * half:(q + 1) * half], act_out[:, s, q * half:(q + 1) * half],
                                            k.bank[2 + q][:, half:2 * half],
                                            ALU.mult).then_inc(gated, 1)
                if not last_one:
                    copy(i, 1 - s, e + 1)
                dve.wait_ge(spent, e * 4 + 4)
                dve.wait_ge(put[s], i * 16)
                nc.vector.tensor_copy(y[:, s, 512:1024], k.bank[5 + 2 * s][0:SLOTS, :]).then_inc(kept_d, 1)

            copy(0, 0, 0)
            pairs(dve, expert)


def overflow_stage(k, l, nov, rows, slots, tab, out_rows):
    nc, a = k.nc, k.a
    with ExitStack() as ctx:
        sb = lambda n, s, dt=F32: ctx.enter_context(nc.sbuf_tensor(f"ov{l}_{n}", s, dt))
        w = [sb(f"w{n}", [P, 2048]) for n in range(6)]
        idx = sb("idx", [SLOTS, 1], I32)
        xg = sb("xg", [SLOTS, D])
        xt = sb("xt", [P, DC * SLOTS])
        act_out = sb("silu", [P, 4 * SLOTS])
        hid = sb("hidden", [P, 4 * SLOTS])
        y = sb("y", [SLOTS, D])
        landed = [k.sem(f"ov_landed{n}") for n in range(6)]
        (picked, got, turned, copied, spent, silued, gated, kept, put) = (
            k.sem(f"ov_{n}") for n in (
                "picked", "got", "turned", "copied", "spent", "silued", "gated", "kept", "put"))
        asked = k.sem("ov_asked")
        block = ctx.enter_context(nc.Block())

        def blocks(eng, body):
            count = eng.value_load(tab[0:1, 0, 1:2], min_val=0, max_val=nov)
            with eng.Fori(0, nov) as b:
                with eng.If(b < count):
                    body(b)
            return count

        @block.sync
        def _(sp):
            def load(b):
                e = sp.value_load(tab[0:1, ds(b, 1), 0:1].rearrange("p a b -> p (a b)"), min_val=0, max_val=NE - 1)
                sp.wait_ge(spent, b)
                for j in range(6):
                    if j < 4:
                        src = a["moe_w_gate_2" if j % 2 == 0 else "moe_w_up_2"][l]
                        src = src.rearrange("e (k p) m -> p e k m", p=P)[:, ds(e, 1), :, (j // 2) * 256:(j // 2) * 256 + 256]
                        kc = DC
                    else:
                        src = a["moe_w_down_2"][l].rearrange("e (k p) m -> p e k m", p=P)
                        src = src[:, ds(e, 1), :, (j - 4) * 512:(j - 4) * 512 + 512]
                        kc = 4
                    sp.dma_start(w[j][:, :].rearrange("p (e k m) -> p e k m", e=1, k=kc), src).then_inc(landed[j], 16)
            blocks(sp, load)

        @block.gpsimd
        def _(pool):
            def gather(b):
                pool.wait_ge(turned, b)
                nc.gpsimd.tensor_copy(idx[:, :], slots[0:SLOTS, ds(b + NE, 1)]).then_inc(picked, 1)
                pool.wait_ge(picked, b + 1)
                pool.sem_inc(asked, 1)
                pool.indirect_dma_start(xg[:, :], None, rows, bass.IndirectOffsetOnAxis(ap=idx[:, :], axis=0))\
                    .then_inc(got, 16)
            blocks(pool, gather)

        @block.tensor
        def _(pe):
            def block_(b):
                pe.wait_ge(got, b * 16 + 16)
                for f in range(DC):
                    last = nc.tensor.matmul(k.bank[0][:, f * SLOTS:(f + 1) * SLOTS], xg[:, f * P:(f + 1) * P],
                                            k.ident[0:SLOTS, 0:SLOTS], start=True, stop=True)
                last.then_inc(turned, 1)
                pe.wait_ge(copied, b + 1)
                for j in range(4):
                    pe.wait_ge(landed[j], b * 16 + 16)
                    for c in range(2):
                        o = (j % 2) * 4 * SLOTS + (2 * (j // 2) + c) * SLOTS
                        for f in range(DC):
                            last = nc.tensor.matmul(k.bank[2][:, o:o + SLOTS],
                                                    w[j][:, f * 256 + c * P:f * 256 + (c + 1) * P],
                                                    xt[:, f * SLOTS:(f + 1) * SLOTS], start=(f == 0), stop=(f == DC - 1))
                last.then_inc(silued, 1)
                pe.wait_ge(gated, b + 1)
                for n in range(2):
                    pe.wait_ge(landed[4 + n], b * 16 + 16)
                    for f in range(4):
                        last = nc.tensor.matmul(k.bank[4 + n][0:SLOTS, :], hid[:, f * SLOTS:(f + 1) * SLOTS],
                                                w[4 + n][:, f * 512:(f + 1) * 512], start=(f == 0), stop=(f == 3))
                last.then_inc(spent, 1)
            blocks(pe, block_)

        @block.scalar
        def _(act):
            def block_(b):
                act.wait_ge(silued, b * 2 + 1)
                nc.scalar.activation(act_out[:, :], k.bank[2][:, 0:4 * SLOTS], ACT.Silu).then_inc(silued, 1)
                act.wait_ge(kept, b + 1)
                act.dma_start(out_rows[ds(b * SLOTS + NE * SLOTS, SLOTS), :], y[:, :]).then_inc(put, 16)
            blocks(act, block_)

        @block.vector
        def _(dve):
            def block_(b):
                dve.wait_ge(turned, b + 1)
                nc.vector.tensor_copy(xt[:, :], k.bank[0][:, :]).then_inc(copied, 1)
                dve.wait_ge(silued, b * 2 + 2)
                nc.vector.tensor_tensor(hid[:, :], act_out[:, :], k.bank[2][:, 4 * SLOTS:8 * SLOTS], ALU.mult)\
                    .then_inc(gated, 1)
                dve.wait_ge(spent, b + 1)
                dve.wait_ge(put, b * 16)
                for n in range(2):
                    last = nc.vector.tensor_copy(y[:, n * 512:(n + 1) * 512], k.bank[4 + n][0:SLOTS, :])
                last.then_inc(kept, 1)
            count = blocks(dve, block_)
            dve.wait_ge(put, count * 16)
            nc.vector.memset(y[0:1, 0:1], 0.0)


def combine_stage(k, l, T, desti, wts, out_rows):
    nc = k.nc
    TT = T // P
    with ExitStack() as ctx:
        y = ctx.enter_context(nc.sbuf_tensor(f"cb{l}_y", [P, TT, 2, D], F32))
        got = [k.sem(f"cb_got{t}") for t in range(TT)]
        weighed, summed, turned, added = (k.sem(f"cb_{n}") for n in (
            "weighed", "summed", "turned", "added"))
        block = ctx.enter_context(nc.Block())

        @block.gpsimd
        def _(pool):
            for t in range(TT):
                for c in range(2):
                    pool.indirect_dma_start(y[:, t, c, :], None, out_rows,
                                            bass.IndirectOffsetOnAxis(ap=desti[:, t, c:c + 1], axis=0))\
                        .then_inc(got[t], 16)

        @block.scalar
        def _(act):
            for t in range(TT):
                act.wait_ge(got[t], 32)
                nc.scalar.activation(y[:, t, 1, :], y[:, t, 1, :], ACT.Copy, scale=wts[:, t, 1:2]).then_inc(weighed, 1)

        @block.tensor
        def _(pe):
            for t in range(TT):
                pe.wait_ge(summed, t + 1)
                for half in range(2):
                    n = 2 * t + half
                    if n >= 4:
                        pe.wait_ge(added, n - 3)
                    for c in range(4):
                        f = (half * 4 + c) * P
                        last = nc.tensor.transpose(k.bank[n % 4][:, c * P:(c + 1) * P], y[:, t, 0, f:f + P],
                                                   k.ident[:, :])
                    last.then_inc(turned, 1)

        @block.vector
        def _(dve):
            for t in range(TT):
                dve.wait_ge(weighed, t + 1)
                nc.vector.scalar_tensor_tensor(out=y[:, t, 0, :], in0=y[:, t, 0, :], scalar=wts[:, t, 0:1],
                                               in1=y[:, t, 1, :], op0=ALU.mult, op1=ALU.add).then_inc(summed, 1)
                for half in range(2):
                    n = 2 * t + half
                    dve.wait_ge(turned, n + 1)
                    for c in range(4):
                        f = half * 4 + c
                        v = (t * P) // SEQ
                        last = nc.vector.scalar_tensor_tensor(
                            out=k.x[:, f, t * P:(t + 1) * P], in0=k.bank[n % 4][:, c * P:(c + 1) * P],
                            scalar=k.mod[:, v, 5 * DC + f:5 * DC + f + 1], in1=k.x[:, f, t * P:(t + 1) * P],
                            op0=ALU.mult, op1=ALU.add)
                    last.then_inc(added, 1)


def load_slots_stage(k, slot_token, table, slots, tab, nblk):
    nc = k.nc
    landed = k.sem("slots_landed")
    with nc.Block() as block:
        @block.sync
        def _(sp):
            with nc.allow_non_contiguous_dma(reason="token numbers, one block a column"):
                sp.dma_start(slots[0:SLOTS, 0:nblk], slot_token.rearrange("(b s) o -> s (b o)", s=SLOTS))\
                    .then_inc(landed, 16)
            sp.dma_start(tab[:, :, :], table.rearrange("(o b) c -> o b c", o=1)).then_inc(landed, 16)
            sp.wait_ge(landed, 32)


def moe(k, l, T):
    nc = k.nc
    nov = 2 * T // SLOTS - 1
    nblk = NE + nov
    V = [(0, SEQ), (SEQ, TB)][:T // SEQ]
    parts = [(t0, t1, k.gain2[:, v, :], k.mod[:, v, 3 * DC:4 * DC]) for v, (t0, t1) in enumerate(V)]
    rows = nc.dram_tensor(f"token_rows_{l}", (T, D), F32).ap()
    out_rows = nc.dram_tensor(f"slot_rows_{l}", (nblk * SLOTS, D), F32).ap()
    slot_token = nc.dram_tensor(f"slot_token_{l}", (nblk * SLOTS, 1), I32).ap()
    table = nc.dram_tensor(f"overflow_table_{l}", (16, 2), I32).ap()
    dest = k.sb(f"slot_of_{l}", [P, T // P, 2])
    desti = k.sb(f"slot_index_{l}", [P, T // P, 2], I32)
    wts = k.sb(f"weight_of_{l}", [P, T // P, 2])
    slots = k.sb(f"slots_{l}", [SLOTS, nblk], I32)
    tab = k.sb(f"table_{l}", [1, 16, 2], I32)
    with nc.sbuf_tensor(f"moe_h_{l}", [P, DC, T], F32) as hm:
        norm_stage(k, f"moe_norm{l}", k.x, DC, D, EPS, parts, hm)
        route_stage(k, l, hm, T, rows, slot_token, table, dest, desti, wts, out_rows)
    k.clear()
    load_slots_stage(k, slot_token, table, slots, tab, nblk)
    experts_stage(k, l, rows, slots, out_rows)
    overflow_stage(k, l, nov, rows, slots, tab, out_rows)
    combine_stage(k, l, T, desti, wts, out_rows)


def second_model(k, ctx):
    nc = k.nc
    k.cond = k.sb("cond", [P, DC, 2])
    k.mod = k.sb("mod", [P, 2, 6 * DC])
    k.gain1, k.gain2 = k.sb("gain1", [P, 2, DC]), k.sb("gain2", [P, 2, DC])
    gb = k.sb("gated_bias", [P, 2, DC])

    def bias_in(link):
        for v in range(2):
            link(nc.vector.tensor_tensor(gb[:, v, :], k.mod[:, v, 2 * DC:3 * DC], param(k, "ga_b_out", DC), ALU.mult))
    mod_stage(k, 0, bias_in)
    gmlp(k)
    bias_stage(k, gb)
    moe(k, 0, TB)
    mod_stage(k, 1, None)
    k.clear()
    rwkv(k)
    moe(k, 1, SEQ)
    final_stage(k)


def bias_stage(k, gb):
    nc = k.nc
    with nc.Block() as block:
        @block.vector
        def _(dve):
            for v in range(2):
                for c in range(DC):
                    nc.vector.tensor_scalar(k.x[:, c, v * SEQ:(v + 1) * SEQ], k.x[:, c, v * SEQ:(v + 1) * SEQ],
                                            gb[:, v, c:c + 1], None, ALU.add)


def rwkv_segments(k, a):
    seg = k.seg
    names = ("rw_wr_2", "rw_wk_2", "rw_wv_2")
    for n in names:
        seg[n] = Segment(4, lambda i, j, n=n: [columns(a[n][0], DC, j * 256, 256)])

    def lora(name):
        def source(i, j):
            w = a[name][0]
            return [(lambda s, z=z: s[:, 0:DC * P].rearrange("p (k m) -> p k m", k=DC)[:, :, z * RH:(z + 1) * RH],
                     w[z].rearrange("(k p) m -> p k m", p=P)) for z in range(2)]
        return source
    seg["w1"], seg["a1"] = Segment(1, lora("rw_w1_2")), Segment(1, lora("rw_a1_2"))
    seg["g1"] = Segment(1, lambda i, j: [columns(a["rw_g1_2"][0], DC, 0, 160)])
    g2 = a["rw_g2_2"][0]
    seg["g2"] = Segment(1, lambda i, j: [(lambda s: s[:, 0:D], g2[0:P, :]), (lambda s: s[0:32, D:2 * D], g2[P:160, :])])
    seg["wo"] = Segment(4, lambda i, j: [columns(a["rw_wo_2"][0], DC, j * 256, 256)])
    return ["rw_wr_2", "w1", "rw_wk_2", "rw_wv_2", "a1", "g1", "g2", "wo"]


def shift_stage(k, h, xx):
    nc = k.nc
    done, zeroed = k.sem("shift_done"), k.sem("shift_zeroed")
    with nc.Block() as block:
        @block.gpsimd
        def _(pool):
            pool.memset(xx[:, :, :], 0.0).then_inc(zeroed, 1)

        @block.vector
        def _(dve):
            dve.wait_ge(zeroed, 1)
            W, q = 64, DC // 4
            for c in range(DC):
                lat = lambda x: x[:, c, 0:SEQ].rearrange("p (r w) -> p r w", w=W)
                to, of = lat(xx), lat(h)
                if c < q:
                    last = nc.vector.tensor_copy(to[:, :, 1:W], of[:, :, 0:W - 1])
                elif c < 2 * q:
                    last = nc.vector.tensor_copy(to[:, :, 0:W - 1], of[:, :, 1:W])
                elif c < 3 * q:
                    last = nc.vector.tensor_copy(xx[:, c, W:SEQ], h[:, c, 0:SEQ - W])
                else:
                    last = nc.vector.tensor_copy(xx[:, c, 0:SEQ - W], h[:, c, W:SEQ])
                last.then_inc(done, 1)
                if c < DC // 2:
                    last = nc.vector.tensor_copy(xx[:, c, SEQ + 1:TB], h[:, c, SEQ:TB - 1])
                else:
                    last = nc.vector.tensor_copy(xx[:, c, SEQ:TB - 1], h[:, c, SEQ + 1:TB])
                last.then_inc(done, 1)
            dve.wait_ge(done, 2 * DC)
            for c in range(DC):
                nc.vector.tensor_tensor(xx[:, c, :], xx[:, c, :], h[:, c, :], ALU.subtract)


def mix_stage(k, xx, h, n, to, T=TB):
    nc = k.nc
    with nc.Block() as block:
        @block.vector
        def _(dve):
            for c in range(DC):
                nc.vector.scalar_tensor_tensor(out=to[:, c, 0:T], in0=xx[:, c, 0:T], scalar=param(k, "mu", 1, n * DC + c),
                                               in1=h[:, c, 0:T], op0=ALU.mult, op1=ALU.add)


def copy_to(nc, dst):
    return lambda dve, m, ps: nc.vector.tensor_copy(dst[:, m, :], ps[:, :])


def rwkv(k):
    nc, a, seg = k.nc, k.a, k.seg
    with ExitStack() as ctx:
        sb = lambda n, s: ctx.enter_context(nc.sbuf_tensor(f"rw_{n}", s, F32))
        gate = sb("gate", [P, DC, SEQ])
        lw, la = sb("lw", [P, TB]), sb("la", [P, TB])
        r, kx, v = (sb(n, [P, DC, TB]) for n in ("r", "k", "v"))
        with ExitStack() as c2:
            sb2 = lambda n, s: c2.enter_context(nc.sbuf_tensor(f"rw_{n}", s, F32))
            h, xx, xm = (sb2(n, [P, DC, TB]) for n in ("h", "xx", "xm"))
            parts = [(t0, t1, k.gain1[:, n, :], k.mod[:, n, 0:DC]) for n, (t0, t1) in enumerate([(0, SEQ), (SEQ, TB)])]
            norm_stage(k, "rw_norm", k.x, DC, D, EPS, parts, h, xm)
            shift_stage(k, h, xx)
            for n, name, dst in ((0, "rw_wr_2", r), (1, "w1", lw), (2, "rw_wk_2", kx), (3, "rw_wv_2", v),
                                 (4, "a1", la)):
                mix_stage(k, xx, h, n, xm)
                if name in ("w1", "a1"):
                    f = ACT.Tanh if name == "w1" else ACT.Copy
                    linear_stage(k, name, seg[name], whole_tiles(DC, P), lambda f: xm[:, f, :], TB,
                                 lambda act, m, ps, f=f, dst=dst: nc.scalar.activation(dst[:, :], ps[:, :], f), 4,
                                 on_scalar=True)
                else:
                    linear_stage(k, name, seg[name], whole_tiles(DC, 256), lambda f: xm[:, f, :], TB,
                                 copy_to(nc, dst), 4)
            mix_stage(k, xx, h, 5, xm, SEQ)
            s1 = sb2("gate_hidden", [P, 2, SEQ])
            linear_stage(k, "g1", seg["g1"], whole_tiles(DC, 160), lambda f: xm[:, f, 0:SEQ], SEQ,
                         lambda act, m, ps: nc.scalar.activation(
                             s1[0:(P, 32)[m], m, :], ps[0:(P, 32)[m], 0:SEQ], ACT.Sigmoid), 4, on_scalar=True)

            def g2(j):
                return [(True, True, [(lambda s, c=c: s[:, c * P:(c + 1) * P], 0),
                                      (lambda s, c=c: s[0:32, D + c * P:D + (c + 1) * P], 1)], P) for c in range(DC)]
            linear_stage(k, "g2", seg["g2"], g2, lambda f: s1[0:(P, 32)[f], f, :], SEQ,
                         lambda dve, m, ps: nc.vector.tensor_copy(gate[:, m, :], ps[:, 0:SEQ]), 4)
        k.clear()
        scan_heads(k, r, kx, v, lw, la, gate)

        def write(dve, m, ps):
            return nc.vector.scalar_tensor_tensor(out=k.x[:, m, 0:SEQ], in0=ps[:, 0:SEQ],
                                                  scalar=k.mod[:, 0, 2 * DC + m:2 * DC + m + 1],
                                                  in1=k.x[:, m, 0:SEQ], op0=ALU.mult, op1=ALU.add)
        linear_stage(k, "wo", seg["wo"], whole_tiles(DC, 256), lambda f: gate[:, f, :], SEQ, write, 4)


LEVELS = 6
M_US, M_LS, M_UI, M_LI, M_ID, M_LEVEL = 0, 1, 2, 3, 4, 5


def rwkv_masks():
    s, t = np.meshgrid(np.arange(CH), np.arange(CH), indexing="ij")
    tables = [t > s, t < s, t >= s, t <= s, t == s]
    for level in range(LEVELS):
        b = 1 << level
        tables.append((s // (2 * b) == t // (2 * b)) & (s // b != t // b))
    tables.append(np.broadcast_to(t > 0, t.shape))
    return np.stack([np.tile(m.astype(np.float32), (2, 1)) for m in tables], axis=1)


def scan_heads(k, r, kx, v, lw, la, gate):
    nc = k.nc
    with ExitStack() as ctx:
        sb = lambda n, s: ctx.enter_context(nc.sbuf_tensor(f"sc_{n}", s, F32))
        q = Kernel()
        q.masks = sb("masks", [P, M_LEVEL + LEVELS + 1, CH])
        q.starts = sb("chunk_starts", [P, TB])
        q.w2, q.a2 = sb("w2", [P, D]), sb("a2", [P, D])
        q.om = sb("one_minus_ka", [P, DC])
        names = ("w2c", "a2c")
        q.w2c, q.a2c = (sb(n, [P, P]) for n in names)
        q.pc = sb("param_c", [P, 10])
        q.v = sb("v", [P, TB])
        q.at, q.bt, q.kt, q.rt, q.s1, q.s2 = (sb(n, [P, 2, TB]) for n in ("at", "bt", "kt", "rt", "s1", "s2"))
        q.s3, q.s4, q.s5 = (sb(n, [P, 2, TB]) for n in ("s3", "s4", "s5"))
        q.pend = sb("pend", [P, 2, NCH])
        q.bonus = sb("bonus", [P, SEQ])
        landed = k.sem("sc_landed")
        done = k.sem("sc_om")
        with nc.Block() as block:
            @block.sync
            def _(sp):
                sp.dma_start(q.masks[:, :, :], k.a["rwkv_masks"]).then_inc(landed, 16)
                sp.dma_start(q.w2[:, :], k.a["rw_w2_2"][0].rearrange("z r d -> (z r) d")).then_inc(landed, 16)
                sp.dma_start(q.a2[:, :], k.a["rw_a2_2"][0].rearrange("z r d -> (z r) d")).then_inc(landed, 16)
                sp.wait_ge(landed, 48)

            @block.vector
            def _(dve):
                nc.vector.tensor_scalar(q.om[:, :], param(k, "k_a", DC), -1.0, 1.0, ALU.mult, ALU.add)
                dve.wait_ge(landed, 48)
                nc.vector.tensor_copy(chunked(q.starts[:, :]), mask_of(q, M_LEVEL + LEVELS)).then_inc(done, 1)
        k.clear()
        with nc.Fori(0, DC) as c:
            scan_prepare(k, q, c, r, kx, v, lw, la)
            with ExitStack() as c2:
                sb2 = lambda n, s: c2.enter_context(nc.sbuf_tensor(f"sc_{n}", s, F32))
                q.n, q.nt, q.akt, q.x, q.xt = q.s1, q.s2, q.s3, q.s4, q.s5
                q.rbk, q.btt, q.ktt = (sb2(n, [P, 2, TB]) for n in ("rbk", "btt", "ktt"))
                q.t1, q.vt = q.bt, q.kt[:, 0, :]
                scan_matrices(k, q)
                scan_invert(k, q)
                scan_states(k, q)
                scan_output(k, q, c, gate)
            k.clear()


def scan_prepare(k, q, c, r, kx, v, lw, la):
    nc = k.nc
    cols = ("k_k", "k_a", "r_k", "gn_g", "gn_b", "w0", "a0")
    s = lambda n: k.sem(f"sp_{n}")
    copied, wmade, smade, vdone, adone, pdone, summed, bsummed, scaled, ready, kmade = (s(n) for n in (
        "copied", "wmade", "smade", "vdone", "adone", "pdone", "summed", "bsummed", "scaled", "ready", "kmade"))
    with ExitStack() as ctx:
        kk, sq, r0, t0 = q.s3[:, 0, :], q.s3[:, 1, :], q.s4[:, 0, :], q.s4[:, 1, :]
        block = ctx.enter_context(nc.Block())
        az, km, G, Gp, lg, F = q.bt, q.kt, q.rt, q.at, q.s1, q.s2
        rc = r[:, ds(c, 1), :].rearrange("p a t -> p (a t)")
        kc = kx[:, ds(c, 1), :].rearrange("p a t -> p (a t)")
        vc = v[:, ds(c, 1), :].rearrange("p a t -> p (a t)")
        p = lambda n: q.pc[:, n:n + 1]
        DECAY = -float(np.exp(-0.5))

        @block.gpsimd
        def _(pool):
            for n, name in enumerate(cols):
                nc.gpsimd.tensor_copy(q.pc[:, n:n + 1], k.params[:, ds(c + k.col[name], 1)])
            for n, name in enumerate(("w0", "a0")):
                nc.gpsimd.tensor_copy(q.pc[:, 7 + n:8 + n], k.params[:, ds(c + (k.col[name] + DC), 1)])
            nc.gpsimd.tensor_copy(q.pc[:, 9:10], q.om[:, ds(c, 1)]).then_inc(pdone, 1)
            nc.gpsimd.tensor_copy(q.v[:, :], vc)

        @block.tensor
        def _(pe):
            pe.wait_ge(copied, 2)
            for n, (w, src) in enumerate(((q.w2c, lw), (q.a2c, la))):
                for z in range(2):
                    nc.tensor.matmul(k.bank[2 * n + z][:, :], w[z * RH:(z + 1) * RH, :], src[z * RH:(z + 1) * RH, :],
                                     start=True, stop=True).then_inc(wmade, 1)
            pe.wait_ge(adone, 1)
            nc.tensor.matmul(k.bank[4][:, :], k.head_ones[:, :], sq[:, :], start=True, stop=True).then_inc(summed, 1)
            pe.wait_ge(kmade, 1)
            nc.tensor.matmul(k.bank[5][:, 0:SEQ], k.head_ones[:, :], t0[:, 0:SEQ], start=True, stop=True)\
                .then_inc(bsummed, 1)

        @block.scalar
        def _(act):
            act.wait_ge(vdone, 1)
            nc.scalar.activation(sq[:, :], kk[:, :], ACT.Square).then_inc(adone, 1)
            act.wait_ge(pdone, 1)
            for z in range(2):
                act.wait_ge(wmade, 3 + z)
                nc.scalar.activation(az[:, z, :], k.bank[2 + z][:, :], ACT.Sigmoid, bias=p(6 if z == 0 else 8))\
                    .then_inc(smade, 1)
                nc.scalar.activation(lg[:, z, :], k.bank[z][:, :], ACT.Sigmoid, bias=p(5 if z == 0 else 7))\
                    .then_inc(smade, 1)
            act.wait_ge(ready, 1)
            nc.scalar.activation(r0[:, :], sq[:, :], ACT.Ln).then_inc(adone, 1)
            act.wait_ge(adone, 2)
            nc.scalar.activation(r0[:, :], r0[:, :], ACT.Exp, scale=-0.5).then_inc(adone, 1)
            act.wait_ge(bsummed, 1)
            nc.scalar.activation(q.bonus[:, :], k.bank[5][:, 0:SEQ], ACT.Copy)
            act.wait_ge(scaled, 1)
            fl = lambda x: x[:, :, :].rearrange("p a t -> p (a t)")
            nc.scalar.activation(fl(lg), fl(G), ACT.Exp, scale=-1.0).then_inc(adone, 1)
            act.wait_ge(adone, 4)
            nc.scalar.activation(fl(G), fl(G), ACT.Exp).then_inc(adone, 1)
            nc.scalar.activation(fl(Gp), fl(Gp), ACT.Exp).then_inc(adone, 1)
            nc.scalar.activation(q.pend[:, :, :], F[:, :, CH - 1::CH], ACT.Exp).then_inc(adone, 1)

        @block.vector
        def _(dve):
            link = Chain(dve, vdone)
            dve.wait_ge(pdone, 1)
            link(nc.vector.tensor_scalar(kk[:, :], kc, p(0), None, ALU.mult))
            nc.vector.tensor_copy(q.w2c[:, :], q.w2[:, ds(c * P, P)]).then_inc(copied, 1)
            nc.vector.tensor_copy(q.a2c[:, :], q.a2[:, ds(c * P, P)]).then_inc(copied, 1)
            dve.wait_ge(summed, 1)
            link(nc.vector.tensor_scalar(sq[:, :], k.bank[4][:, :], 1e-12, None, ALU.add))
            nc.vector.nop().then_inc(ready, 1)
            for z in range(2):
                dve.wait_ge(smade, 2 * z + 1)
                link(nc.vector.tensor_scalar(km[:, z, :], az[:, z, :], p(1), p(9), ALU.mult, ALU.add))
                link(nc.vector.tensor_tensor(km[:, z, :], km[:, z, :], kc, ALU.mult))
                dve.wait_ge(smade, 2 * z + 2)
                link(nc.vector.tensor_scalar(lg[:, z, :], lg[:, z, :], DECAY, None, ALU.mult))
                link(nc.vector.tensor_tensor_scan(F[:, z, :], q.starts[:, :], lg[:, z, :], 0.0,
                                                  ALU.mult, ALU.add))
            link(nc.vector.tensor_tensor(t0[:, 0:SEQ], km[:, 0, 0:SEQ], km[:, 1, 0:SEQ], ALU.add))
            link(nc.vector.scalar_tensor_tensor(out=t0[:, 0:SEQ], in0=t0[:, 0:SEQ], scalar=p(2), in1=rc[:, 0:SEQ],
                                                op0=ALU.mult, op1=ALU.mult))
            nc.vector.nop().then_inc(kmade, 1)
            link(nc.vector.tensor_copy(G[:, 0, :], F[:, 0, :]))
            link(nc.vector.tensor_tensor(Gp[:, 0, :], F[:, 0, :], lg[:, 0, :], ALU.subtract))
            for j in range(NCH):
                o = j * CH
                link(nc.vector.tensor_scalar(Gp[:, 1, o:o + CH], F[:, 1, o:o + CH], F[:, 1, o + CH - 1:o + CH], -1.0,
                                             ALU.subtract, ALU.mult))
            link(nc.vector.tensor_tensor(G[:, 1, :], Gp[:, 1, :], lg[:, 1, :], ALU.add))
            nc.vector.nop().then_inc(scaled, 1)
            dve.wait_ge(adone, 3)
            dve.wait_ge(bsummed, 1)
            link(nc.vector.tensor_tensor(t0[:, :], r0[:, :], r0[:, :], ALU.mult))
            link(nc.vector.scalar_tensor_tensor(out=t0[:, :], in0=t0[:, :], scalar=-0.5, in1=sq[:, :],
                                                op0=ALU.mult, op1=ALU.mult))
            link(nc.vector.scalar_tensor_tensor(out=t0[:, :], in0=t0[:, :], scalar=1.5, in1=r0[:, :],
                                                op0=ALU.add, op1=ALU.mult))
            link(nc.vector.tensor_tensor(kk[:, :], kk[:, :], t0[:, :], ALU.mult))
            dve.wait_ge(adone, 7)
            for z in range(2):
                nc.vector.scalar_tensor_tensor(out=q.at[:, z, :], in0=kk[:, :], scalar=-1.0, in1=Gp[:, z, :],
                                               op0=ALU.mult, op1=ALU.mult)
                nc.vector.tensor_tensor(q.kt[:, z, :], km[:, z, :], lg[:, z, :], ALU.mult)
                nc.vector.tensor_tensor(q.rt[:, z, :], rc, G[:, z, :], ALU.mult)
                link(nc.vector.tensor_tensor(q.bt[:, z, :], kk[:, :], az[:, z, :], ALU.mult))
                nc.vector.tensor_tensor(q.bt[:, z, :], q.bt[:, z, :], lg[:, z, :], ALU.mult)


HALVES = (0, RH)


def chunked(x):
    return x.rearrange("p (j s) -> p j s", s=CH)


def mask_of(q, n):
    return q.masks[:, n:n + 1, :].broadcast_to([P, NCH, CH])


def scan_matrices(k, q):
    nc = k.nc
    s = lambda n: k.sem(f"sm_{n}")
    made, emptied, vmade, vinit = (s(n) for n in ("made", "emptied", "vmade", "vinit"))
    jobs = []
    for z in range(2):
        up, low = ((M_US, M_LS), (M_LS, M_US))[z]
        incl = (M_UI, M_LI)[z]
        jobs += [("nt", z, (q.bt, q.at), q.nt, up), ("n", z, (q.at, q.bt), q.n, low), ("akt", z, (q.kt, q.at), q.akt, up),
                 ("rbk", z, None, q.rbk, incl), ("btt", z, (q.bt, None), q.btt, None), ("ktt", z, (q.kt, None), q.ktt, None)]
    jobs.append(("vt", 0, (q.v, None), q.vt, None))
    with nc.Block() as block:
        @block.tensor
        def _(pe):
            for n, (kind, z, ops, dst, mask) in enumerate(jobs):
                if n >= 4:
                    pe.wait_ge(emptied, n - 3)
                ps = k.bank[n % 4]
                for j in range(NCH):
                    for h in HALVES:
                        rows = slice(h, h + RH)
                        to = ps[rows, j * CH:(j + 1) * CH]
                        t = slice(j * CH, (j + 1) * CH)
                        if kind == "rbk":
                            src = (q.bt, q.kt)[j // LCH]
                            t = slice((j % LCH) * CH, (j % LCH + 1) * CH)
                            last = nc.tensor.matmul(to, src[rows, z, t], q.rt[rows, z, t], start=True, stop=True)
                        elif ops[1] is None:
                            src = ops[0][rows, t] if kind == "vt" else ops[0][rows, z, t]
                            last = nc.tensor.matmul(to, src, k.ident[rows, rows], start=True, stop=True)
                        else:
                            last = nc.tensor.matmul(to, ops[0][rows, z, t], ops[1][rows, z, t], start=True, stop=True)
                last.then_inc(made, 1)

        @block.vector
        def _(dve):
            for n, (kind, z, ops, dst, mask) in enumerate(jobs):
                dve.wait_ge(made, n + 1)
                ps = k.bank[n % 4][:, :]
                if mask is not None:
                    nc.vector.tensor_tensor(chunked(dst[:, z, :]), chunked(ps), mask_of(q, mask), ALU.mult).then_inc(emptied, 1)
                else:
                    nc.vector.tensor_copy(dst[:, :] if kind == "vt" else dst[:, z, :], ps).then_inc(emptied, 1)
            dve.wait_ge(emptied, len(jobs))
            link = Chain(dve, vinit)
            for z in range(2):
                for x, n in ((q.x, q.n), (q.xt, q.nt)):
                    link(nc.vector.tensor_tensor(chunked(x[:, z, :]), chunked(n[:, z, :]), mask_of(q, M_LEVEL), ALU.mult))
                    link(nc.vector.tensor_tensor(chunked(x[:, z, :]), chunked(x[:, z, :]), mask_of(q, M_ID), ALU.add))


def blocks_matmul(nc, ps, lhsT, rhs):
    for j in range(NCH):
        t = slice(j * CH, (j + 1) * CH)
        for h in HALVES:
            rows = slice(h, h + RH)
            last = nc.tensor.matmul(ps[rows, t], lhsT[rows, t], rhs[rows, t], start=True, stop=True)
    return last


def scan_invert(k, q):
    nc = k.nc
    s = lambda n: k.sem(f"si_{n}")
    masked, t1made, t1kept, xmade, xtmade, xkept, xtkept = (s(n) for n in (
        "masked", "t1made", "t1kept", "xmade", "xtmade", "xkept", "xtkept"))
    steps = [(level, z) for level in range(1, LEVELS) for z in range(2)]
    noff = q.n
    with nc.Block() as block:
        @block.tensor
        def _(pe):
            def t1(n):
                level, z = steps[n]
                pe.wait_ge(masked, n + 1)
                if level > 1:
                    pe.wait_ge(xkept, n - 1)
                blocks_matmul(nc, k.bank[z], noff[:, z, :], q.x[:, z, :]).then_inc(t1made, 1)

            def x(n):
                level, z = steps[n]
                pe.wait_ge(t1kept, n + 1)
                if level > 1:
                    pe.wait_ge(xtkept, n - 1)
                blocks_matmul(nc, k.bank[4 + z], q.t1[:, z, :], q.xt[:, z, :]).then_inc(xtmade, 1)
                if level < LEVELS - 1:
                    blocks_matmul(nc, k.bank[2 + z], q.xt[:, z, :], q.t1[:, z, :]).then_inc(xmade, 1)
            for n in range(0, len(steps), 2):
                t1(n)
                t1(n + 1)
                x(n)
                x(n + 1)

        @block.scalar
        def _(act):
            for n, (level, z) in enumerate(steps):
                act.wait_ge(t1made, n + 1)
                if level > 1:
                    act.wait_ge(xmade, n - 1)
                    act.wait_ge(xtmade, n - 1)
                nc.scalar.activation(q.t1[:, z, :], k.bank[z][:, :], ACT.Copy).then_inc(t1kept, 1)

        @block.vector
        def _(dve):
            for n, (level, z) in enumerate(steps):
                if n < 2:
                    nc.vector.tensor_tensor(chunked(noff[:, z, :]), chunked(q.nt[:, z, :]), mask_of(q, M_LEVEL + level), ALU.mult)\
                        .then_inc(masked, 1)
            for n, (level, z) in enumerate(steps):
                dve.wait_ge(t1made, n + 1)
                if level < LEVELS - 1:
                    nc.vector.tensor_tensor(chunked(noff[:, z, :]), chunked(q.nt[:, z, :]), mask_of(q, M_LEVEL + level + 1),
                                            ALU.mult)\
                        .then_inc(masked, 1)
                    dve.wait_ge(xmade, n + 1)
                    nc.vector.tensor_tensor(q.x[:, z, :], k.bank[2 + z][:, :], q.x[:, z, :], ALU.add).then_inc(xkept, 1)
                else:
                    dve.wait_ge(xtmade, n + 1)
                nc.vector.tensor_tensor(q.xt[:, z, :], k.bank[4 + z][:, :], q.xt[:, z, :], ALU.add).then_inc(xtkept, 1)


def scan_states(k, q):
    nc = k.nc
    s = lambda n: k.sem(f"ss_{n}")
    rmade, rkept, samade, sakept, smade, skept, spre, zeroed, ymade = (s(n) for n in (
        "rmade", "rkept", "samade", "sakept", "smade", "skept", "spre", "zeroed", "ymade"))
    order = [[4, 5, 6, 7, 0, 1, 2, 3], [7, 6, 5, 4, 3, 2, 1, 0]]
    with ExitStack() as ctx:
        st, stp, rs, sa = ([q.n[:, z, n * RH:(n + 1) * RH] for z in range(2)] for n in range(4))
        block = ctx.enter_context(nc.Block())
        last_step = NCH - 1

        @block.tensor
        def _(pe):
            for i in range(NCH):
                for z in range(2):
                    j = order[z][i]
                    t = slice(j * CH, (j + 1) * CH)
                    n = 2 * i + z
                    if i:
                        pe.wait_ge(skept, n - 1)
                    for h in HALVES:
                        rows = slice(h, h + RH)
                        if i:
                            nc.tensor.matmul(k.bank[z][rows, 0:RH], q.at[rows, z, t], st[z][rows, :],
                                             start=True, stop=False)
                        last = nc.tensor.matmul(k.bank[z][rows, 0:RH], q.akt[rows, z, t], q.vt[rows, t],
                                                start=(i == 0), stop=True)
                    last.then_inc(rmade, 1)
                for z in range(2):
                    t = slice(order[z][i] * CH, (order[z][i] + 1) * CH)
                    n = 2 * i + z
                    pe.wait_ge(rkept, n + 1)
                    for h in HALVES:
                        rows = slice(h, h + RH)
                        last = nc.tensor.matmul(k.bank[z][rows, RH:2 * RH], q.xt[rows, z, t], rs[z][rows, :],
                                                start=True, stop=True)
                    last.then_inc(samade, 1)
                for z in range(2):
                    t = slice(order[z][i] * CH, (order[z][i] + 1) * CH)
                    n = 2 * i + z
                    pe.wait_ge(sakept, n + 1)
                    if i < last_step:
                        for h in HALVES:
                            rows = slice(h, h + RH)
                            ps = k.bank[z][rows, 2 * RH:3 * RH]
                            nc.tensor.matmul(ps, q.btt[rows, z, t], sa[z][rows, :], start=True, stop=False)
                            last = nc.tensor.matmul(ps, q.ktt[rows, z, t], q.vt[rows, t], start=False, stop=True)
                        last.then_inc(smade, 1)
                if i >= LCH:
                    for z in range(2):
                        j = order[z][i]
                        t, t2 = slice(j * CH, (j + 1) * CH), slice((LCH + j) * CH, (LCH + j + 1) * CH)
                        for h in HALVES:
                            rows = slice(h, h + RH)
                            ps = k.bank[2 + z][rows, t]
                            nc.tensor.matmul(ps, st[z][rows, :], q.rt[rows, z, t], start=True, stop=False)
                            nc.tensor.matmul(ps, sa[z][rows, :], q.rbk[rows, z, t], start=False, stop=False)
                            last = nc.tensor.matmul(ps, q.vt[rows, t], q.rbk[rows, z, t2], start=False, stop=True)
                        last.then_inc(ymade, 1)

        @block.vector
        def _(dve):
            for i in range(NCH):
                for z in range(2):
                    n = 2 * i + z
                    dve.wait_ge(rmade, n + 1)
                    nc.vector.tensor_copy(rs[z][:, :], k.bank[z][:, 0:RH]).then_inc(rkept, 1)
                for z in range(2):
                    n = 2 * i + z
                    dve.wait_ge(samade, n + 1)
                    if i > LCH:
                        dve.wait_ge(ymade, 2 * (i - LCH - 1) + z + 1)
                    elif i:
                        dve.wait_ge(smade, n - 1)
                    nc.vector.tensor_copy(sa[z][:, :], k.bank[z][:, RH:2 * RH]).then_inc(sakept, 1)
                if i < last_step:
                    for z in range(2):
                        n, j = 2 * i + z, order[z][i]
                        dve.wait_ge(smade, n + 1)
                        pend = q.pend[:, z, j:j + 1]
                        if i == 0:
                            nc.vector.tensor_scalar(st[z][:, :], k.bank[z][:, 2 * RH:3 * RH], pend, None, ALU.mult)\
                                .then_inc(skept, 1)
                            continue
                        nc.vector.tensor_scalar(stp[z][:, :], st[z][:, :], pend, None, ALU.mult).then_inc(spre, 1)
                        dve.wait_ge(spre, n - 1)
                        if i >= LCH:
                            dve.wait_ge(ymade, 2 * (i - LCH) + z + 1)
                        nc.vector.scalar_tensor_tensor(out=st[z][:, :], in0=k.bank[z][:, 2 * RH:3 * RH], scalar=pend,
                                                       in1=stp[z][:, :], op0=ALU.mult, op1=ALU.add).then_inc(skept, 1)


def scan_output(k, q, c, gate):
    nc = k.nc
    s = lambda n: k.sem(f"so_{n}")
    vdone, summed, adone, sqd = (s(n) for n in ("vdone", "summed", "adone", "sqd"))
    with ExitStack() as ctx:
        y, m, r0, t0 = q.n[:, 0, 0:SEQ], q.n[:, 0, SEQ:], q.n[:, 1, 0:SEQ], q.n[:, 1, SEQ:]
        block = ctx.enter_context(nc.Block())
        g = gate[:, ds(c, 1), :].rearrange("p a t -> p (a t)")

        @block.tensor
        def _(pe):
            pe.wait_ge(vdone, 2)
            nc.tensor.matmul(k.bank[4][:, 0:SEQ], k.head_ones[:, :], y[:, :], start=True, stop=True).then_inc(summed, 1)
            pe.wait_ge(adone, 1)
            nc.tensor.matmul(k.bank[5][:, 0:SEQ], k.head_ones[:, :], t0[:, :], start=True, stop=True)\
                .then_inc(summed, 1)

        @block.scalar
        def _(act):
            act.wait_ge(vdone, 3)
            nc.scalar.activation(t0[:, :], y[:, :], ACT.Square).then_inc(adone, 1)
            act.wait_ge(vdone, 4)
            nc.scalar.activation(r0[:, :], m[:, :], ACT.Ln).then_inc(adone, 1)
            act.wait_ge(adone, 2)
            nc.scalar.activation(r0[:, :], r0[:, :], ACT.Exp, scale=-0.5).then_inc(adone, 1)

        @block.vector
        def _(dve):
            link = Chain(dve, vdone)
            link(nc.vector.tensor_copy(y[:, :], k.bank[2][:, 0:SEQ]))
            link(nc.vector.tensor_tensor(y[:, :], y[:, :], k.bank[3][:, 0:SEQ], ALU.add))
            dve.wait_ge(summed, 1)
            link(nc.vector.scalar_tensor_tensor(out=y[:, :], in0=k.bank[4][:, 0:SEQ], scalar=-1.0 / RH, in1=y[:, :],
                                                op0=ALU.mult, op1=ALU.add))
            dve.wait_ge(summed, 2)
            link(nc.vector.tensor_scalar(m[:, :], k.bank[5][:, 0:SEQ], 1.0 / RH, GN_EPS, ALU.mult, ALU.add))
            dve.wait_ge(adone, 3)
            link(nc.vector.tensor_tensor(t0[:, :], r0[:, :], r0[:, :], ALU.mult))
            link(nc.vector.scalar_tensor_tensor(out=t0[:, :], in0=t0[:, :], scalar=-0.5, in1=m[:, :],
                                                op0=ALU.mult, op1=ALU.mult))
            link(nc.vector.scalar_tensor_tensor(out=t0[:, :], in0=t0[:, :], scalar=1.5, in1=r0[:, :],
                                                op0=ALU.add, op1=ALU.mult))
            link(nc.vector.tensor_tensor(y[:, :], y[:, :], t0[:, :], ALU.mult))
            link(nc.vector.tensor_scalar(y[:, :], y[:, :], q.pc[:, 3:4], q.pc[:, 4:5], ALU.mult, ALU.add))
            link(nc.vector.tensor_tensor(t0[:, :], q.bonus[:, :], q.v[:, 0:SEQ], ALU.mult))
            link(nc.vector.tensor_tensor(y[:, :], y[:, :], t0[:, :], ALU.add))
            nc.vector.tensor_tensor(g, y[:, :], g, ALU.mult)


def final_stage(k):
    nc = k.nc
    with nc.sbuf_tensor("fin", [P, DC, SEQ], F32) as f, nc.sbuf_tensor("fin_rows", [P, 2, D], F32) as rows:
        norm_stage(k, "final", k.x, DC, D, EPS, [(0, SEQ, param(k, "final", DC), None)], f)
        turned, copied, stored = (k.sem(f"fin_{n}") for n in ("turned", "copied", "stored"))
        with nc.Block() as block:
            @block.tensor
            def _(pe):
                for n in range(4):
                    t, half = n // 2, n % 2
                    for c in range(4):
                        last = nc.tensor.transpose(k.bank[n][:, c * P:(c + 1) * P],
                                                   f[:, half * 4 + c, t * P:(t + 1) * P], k.ident[:, :])
                    last.then_inc(turned, 1)

            @block.vector
            def _(dve):
                for n in range(4):
                    dve.wait_ge(turned, n + 1)
                    nc.vector.tensor_copy(rows[:, n // 2, (n % 2) * 512:(n % 2 + 1) * 512], k.bank[n][:, :])\
                        .then_inc(copied, 1)

            @block.sync
            def _(sp):
                for t in range(2):
                    sp.wait_ge(copied, 2 * t + 2)
                    sp.dma_start(k.a["out"][0, t * P:(t + 1) * P, :], rows[:, t, :]).then_inc(stored, 16)
                sp.wait_ge(stored, 32)


def kernel(**inputs):
    import concourse.bacc as bacc
    from concourse.bass_utils import run_bass_kernel_spmd

    nc = bacc.Bacc("TRN2", target_bir_lowering=False, num_devices=1)
    arrays, a = {}, {}
    for name, value in {**inputs, **shape_tables()}.items():
        value = np.ascontiguousarray(value)
        arrays[f"in_{name}_dram"] = value
        a[name] = nc.dram_tensor(f"in_{name}_dram", value.shape, mybir.dt.from_np(value.dtype),
                                 kind="ExternalInput").ap()
    a["out"] = nc.dram_tensor("out_0_dram", (1, SEQ, D), F32, kind="ExternalOutput").ap()
    program(nc, a)
    r = run_bass_kernel_spmd(nc, [arrays], core_ids=[0])
    return r.results[0]["out_0_dram"]
```

```python
from contextlib import ExitStack

import numpy as np
import concourse.bass as bass
from concourse import mybir

F32 = mybir.dt.float32
I32 = mybir.dt.int32
ALU = mybir.AluOpType
ACT = mybir.ActivationFunctionType
AX = mybir.AxisListType
ds = bass.ds

P = 128
D = 1024
DC = D // P
SEQ = 256
META = 16
TA = META + SEQ
TB = 2 * SEQ
D_FF = 2816
FC = D_FF // P
EPS = 1e-6
NEG = -1e30
HEADS = 8
QK = 96
NOPE = 64
ROPE = 32
GW = 2048
GC = GW // P
LN_EPS = 1e-5
RH = 64
GN_EPS = 64e-5
CH = 64
NCH = TB // CH
LCH = SEQ // CH
NE = 32
EG = 8
NG = 4
EH = 512
SLOTS = 64
SLOT = 8 * 264
RING = 6


class Segment:

    def __init__(self, tiles, source):
        self.tiles, self.source, self.first, self.behind = tiles, source, 0, []


class Stream:

    def __init__(self, nc, ctx, segments):
        self.slots = [ctx.enter_context(nc.sbuf_tensor(f"weights_{s}", [P, SLOT], F32)) for s in range(RING)]
        self.landed = [ctx.enter_context(nc.semaphore(f"weights_landed_{s}")) for s in range(RING)]
        self.order, self.need = [], []
        count = [0] * RING
        self.fed = RING
        for seg in segments:
            seg.first = len(self.order)
            for t in range(seg.tiles):
                s = len(self.order) % RING
                count[s] += 16 * len(seg.source(t // RING, t % RING))
                self.order.append((seg, t))
                self.need.append(count[s])
        self.hold = len(self.order)

    def slot(self, seg, j):
        return self.slots[(seg.first + j) % RING]

    def start(self, sp, seg, i, j):
        s = (seg.first + j) % RING
        for where, what in seg.source(i, j):
            sp.dma_start(where(self.slots[s]), what).then_inc(self.landed[s], 16)

    def start_number(self, sp, n):
        self.fed = max(self.fed, n + 1)
        if n < min(len(self.order), self.hold):
            seg, t = self.order[n]
            self.start(sp, seg, t // RING, t % RING)

    def resume(self, sp):
        held, self.hold = self.hold, len(self.order)
        for n in range(held, held + RING):
            self.start_number(sp, n)

    def wait(self, eng, seg, i, j):
        base = self.need[seg.first + j]
        step = self.need[seg.first + j + RING] - base if seg.tiles > j + RING else 0
        eng.wait_ge(self.landed[(seg.first + j) % RING], base + i * step if step else base)

    def feed(self, sp, seg, used, per_tile, per_round):
        self.fed = seg.first + seg.tiles + RING
        rounds = seg.tiles // RING
        looped = rounds - 1 if rounds > 2 else 0
        if looped:
            with sp.Fori(0, looped) as i:
                for j in range(RING):
                    sp.wait_ge(used, i * per_round + per_tile(j))
                    self.start(sp, seg, i + 1, j)
        for t in range(looped * RING, seg.tiles):
            sp.wait_ge(used, (t // RING) * per_round + per_tile(t % RING))
            self.start_number(sp, seg.first + t + RING)


class Chain:

    def __init__(self, eng, sem):
        self.eng, self.sem, self.n = eng, sem, 0

    def __call__(self, ins):
        self.n += 1
        ins.then_inc(self.sem, 1)
        self.eng.wait_ge(self.sem, self.n)


def columns(w, kc, c0, width):
    src = w.rearrange("(k p) m -> p k m", p=P)[:, :, ds(c0, width)]
    return lambda s: s[:, 0:kc * width].rearrange("p (k m) -> p k m", k=kc), src


class Kernel:

    def sem(self, name):
        self.sem_count += 1
        s = self.nc.alloc_semaphore(name=f"{name}_{self.sem_count}")
        self.stage_sems.append(s)
        return s

    def clear(self):
        self.nc.clear_and_free_semaphores(self.stage_sems)
        self.nc.all_engine_barrier()
        self.stage_sems = []


def param_rows(a):
    one = lambda v, n=P: v.rearrange("(c p) -> c p", p=n)
    flat = lambda v: v.rearrange("a b -> (a b)")
    two = lambda v: [(v, 0), (v, RH)]
    return [
        [("g_ffn1", [(one(flat(a["g_ffn1"])), 0)]), ("g_mix", [(one(flat(a["g_mix"])), 0)]),
         ("g_cq", [(one(flat(a["g_cq"])), 0)]), ("g_ckv", [(one(flat(a["g_ckv"])), 0)]),
         ("g_q_mla", [(a["g_q_mla"], 0)]), ("g_k_mla", [(a["g_k_mla"], 0)]),
         ("g_q_fox", two(a["g_q_fox"])), ("g_k_fox", two(a["g_k_fox"])),
         ("b_forget", [(a["b_forget"], 0)]), ("g_ffn2", [(one(flat(a["g_ffn2"])), 0)]),
         ("norm1", [(one(flat(a["norm1_g_2"])), 0)]), ("norm2", [(one(flat(a["norm2_g_2"])), 0)]),
         ("final", [(one(a["final_g_2"]), 0)]), ("ga_b_u", [(one(flat(a["ga_b_in_2"])[0:GW]), 0)]),
         ("ga_b_out", [(one(flat(a["ga_b_out_2"])), 0)])],
        [("mu", [(one(a["rw_mu_2"].rearrange("a b c -> (a b c)")), 0)]),
         ("k_k", [(one(flat(a["rw_k_k_2"])), 0)]), ("k_a", [(one(flat(a["rw_k_a_2"])), 0)]),
         ("r_k", [(one(a["rw_r_k_2"].rearrange("a b c -> (a b c)")), 0)]),
         ("gn_g", [(one(flat(a["rw_ln_g_2"])), 0)]), ("gn_b", [(one(flat(a["rw_ln_b_2"])), 0)]),
         ("w0", [(one(a["rw_w0_2"].rearrange("a b c -> (a b c)")), 0)]),
         ("a0", [(one(a["rw_a0_2"].rearrange("a b c -> (a b c)")), 0)])],
        [("ada_b", [(one(flat(a["ada_b_2"])), 0)]),
         ("c", [(one(flat(a["c_2"])), 0)]), ("c_ctx", [(one(a["c_ctx_2"]), 0)])],
    ]


def stage_setup(k):
    nc = k.nc
    groups = param_rows(k.a)
    width = sum(sum(p[1][0][0].shape[0] for p in g) for g in groups)
    k.params = k.sb("params", [P, width])
    k.col, at, starts = {}, 0, []
    for g in groups:
        starts.append(at)
        for name, pieces in g:
            k.col[name] = at
            at += pieces[0][0].shape[0]
    starts.append(at)
    with ExitStack() as ctx:
        raw = [ctx.enter_context(nc.sbuf_tensor(f"param_rows_{n}", [P, P], F32)) for n in range(len(groups))]
        rows = ctx.enter_context(nc.sbuf_tensor("token_rows", [P, 5, D], F32))
        cleared, param_landed, tokens_landed, ones_made, ident_made = (
            k.sem(n)
            for n in ("cleared", "param_landed", "tokens_landed", "ones_made", "ident_made"))
        turned, copied, tables, vsum = (k.sem(n) for n in ("turned", "copied", "tables", "vsum"))
        block = ctx.enter_context(nc.Block())
        n_dma = sum(len(p) for g in groups for _, p in g)
        tiles = [(k.a["meta_tokens"], META, k.h, 0)]
        tiles += [(k.a["x"][0, t * P:(t + 1) * P, :], P, k.h, META + t * P) for t in range(2)]
        tiles += [(k.a["ctx_2"][0, t * P:(t + 1) * P, :], P, k.x, SEQ + t * P) for t in range(2)]

        @block.sync
        def _(sp):
            for n, (src, rows_n, _, _) in enumerate(tiles):
                sp.dma_start(rows[0:rows_n, n, :], src).then_inc(tokens_landed, 16)
            for n in range(RING):
                k.stream.start_number(sp, n)

        @block.scalar
        def _(act):
            act.wait_ge(cleared, len(groups))
            for g, start in zip(groups, starts):
                for name, pieces in g:
                    for src, off in pieces:
                        r = k.col[name] - start
                        act.dma_start(raw[starts.index(start)][r:r + src.shape[0], off:off + src.shape[1]], src)\
                            .then_inc(param_landed, 16)
            act.dma_start(k.rope_cos[0:QK, :], k.a["rope_cos"]).then_inc(tables, 16)
            act.dma_start(k.rope_sin[0:QK, :], k.a["rope_sin"]).then_inc(tables, 16)
            act.dma_start(k.rope_turn[0:QK, :], k.a["rope_turn"]).then_inc(tables, 16)
            act.wait_ge(tables, 48)

        @block.gpsimd
        def _(pool):
            pool.memset(k.ident[:, :], 0.0).then_inc(ident_made, 1)
            pool.wait_ge(ident_made, 1)
            pool.affine_select(out=k.ident[:, :], in_=k.ident[:, :], compare_op=ALU.not_equal, fill=1.0,
                               base=0, pattern=[[-1, P]], channel_multiplier=1).then_inc(ident_made, 1)
            pool.memset(k.causal[:, :], 0.0).then_inc(ident_made, 1)
            pool.wait_ge(ident_made, 3)
            pool.affine_select(out=k.causal[:, :], in_=k.causal[:, :], compare_op=ALU.is_ge, fill=NEG,
                               base=0, pattern=[[-1, P]], channel_multiplier=1).then_inc(ident_made, 1)

        @block.tensor
        def _(pe):
            pe.wait_ge(ident_made, 2)
            pe.wait_ge(param_landed, 16 * n_dma)
            for n in range(len(groups)):
                last = nc.tensor.transpose(k.bank[n][:, 0:P], raw[n][:, :], k.ident[:, :])
            last.then_inc(turned, 1)
            pe.wait_ge(tokens_landed, 16 * len(tiles))
            for n, (_, r, _, _) in enumerate(tiles):
                for half in range(2):
                    b = (2 * n + half) % 5
                    if 2 * n + half >= 5:
                        pe.wait_ge(copied, 2 + 2 * n + half - 5)
                    for c in range(4):
                        f = (half * 4 + c) * P
                        last = nc.tensor.transpose(k.bank[3 + b][:, c * P:c * P + r], rows[0:r, n, f:f + P],
                                                   k.ident[0:r, 0:r])
                    last.then_inc(turned, 1)

        @block.vector
        def _(dve):
            for n in range(len(groups)):
                nc.vector.memset(raw[n][:, :], 0.0).then_inc(cleared, 1)
            nc.vector.memset(k.ones[:, :], 1.0).then_inc(ones_made, 1)
            nc.vector.memset(k.head_ones[:, :], 0.0).then_inc(ones_made, 1)
            dve.wait_ge(ones_made, 2)
            for h in range(2):
                nc.vector.memset(k.head_ones[h * RH:(h + 1) * RH, h * RH:(h + 1) * RH], 1.0).then_inc(ones_made, 1)
            dve.wait_ge(turned, 1)
            for n in range(len(groups)):
                w = starts[n + 1] - starts[n]
                last = nc.vector.tensor_copy(k.params[:, starts[n]:starts[n + 1]], k.bank[n][:, 0:w])
            last.then_inc(copied, 1)
            for n, (_, r, to, t0) in enumerate(tiles):
                for half in range(2):
                    dve.wait_ge(turned, 2 + 2 * n + half)
                    src = k.bank[3 + (2 * n + half) % 5][:, :].rearrange("p (c t) -> p c t", c=4)[:, :, 0:r]
                    nc.vector.tensor_copy(to[:, half * 4:half * 4 + 4, t0:t0 + r], src).then_inc(copied, 1)


def norm_stage(k, name, src, kc, width, eps, parts, dst, scratch=None):
    nc = k.nc
    T = parts[-1][1]
    t00 = parts[0][0]
    with ExitStack() as ctx:
        sq = scratch[0] if scratch else ctx.enter_context(nc.sbuf_tensor(f"{name}_sq", [P, kc, T], F32))
        r0, mean, rr = (scratch[1][:, n, 0:T] for n in range(3)) if scratch else (ctx.enter_context(nc.sbuf_tensor(f"{name}_{n}", [P, T], F32)) for n in ("r0", "mean", "rr"))
        squared, summed, rooted, vdone, ready, meaned = (k.sem(f"{name}_{n}") for n in (
            "squared", "summed", "rooted", "vdone", "ready", "meaned"))
        block = ctx.enter_context(nc.Block())
        ps = k.bank[0][:, t00:T]
        w = slice(t00, T)

        @block.scalar
        def _(act):
            for c in range(kc):
                nc.scalar.activation(sq[:, c, w], src[:, c, w], ACT.Square).then_inc(squared, 1)
            act.wait_ge(meaned, 1)
            nc.scalar.activation(r0[:, w], mean[:, w], ACT.Ln).then_inc(rooted, 1)
            act.wait_ge(rooted, 1)
            nc.scalar.activation(r0[:, w], r0[:, w], ACT.Exp, scale=-0.5).then_inc(rooted, 1)

        @block.tensor
        def _(pe):
            for c in range(kc):
                pe.wait_ge(squared, c + 1)
                last = nc.tensor.matmul(ps, k.ones[:, :], sq[:, c, w], start=(c == 0), stop=(c == kc - 1))
            last.then_inc(summed, 1)

        @block.vector
        def _(dve):
            link = Chain(dve, vdone)
            dve.wait_ge(summed, 1)
            nc.vector.tensor_scalar(mean[:, w], ps, 1.0 / width, eps, ALU.mult, ALU.add).then_inc(meaned, 1)
            dve.wait_ge(meaned, 1)
            dve.wait_ge(rooted, 2)
            link(nc.vector.tensor_tensor(rr[:, w], r0[:, w], r0[:, w], ALU.mult))
            link(nc.vector.scalar_tensor_tensor(out=rr[:, w], in0=rr[:, w], scalar=-0.5, in1=mean[:, w],
                                                op0=ALU.mult, op1=ALU.mult))
            link(nc.vector.scalar_tensor_tensor(out=rr[:, w], in0=rr[:, w], scalar=1.5, in1=r0[:, w],
                                                op0=ALU.add, op1=ALU.mult))
            for c in range(kc):
                for t0, t1, gain, shift in parts:
                    nc.vector.scalar_tensor_tensor(out=dst[:, c, t0:t1], in0=src[:, c, t0:t1],
                                                   scalar=gain[:, c:c + 1], in1=rr[:, t0:t1],
                                                   op0=ALU.mult, op1=ALU.mult).then_inc(ready, 1)
            if parts[0][3] is not None:
                dve.wait_ge(ready, kc * len(parts))
                for c in range(kc):
                    for t0, t1, _, shift in parts:
                        nc.vector.tensor_scalar(dst[:, c, t0:t1], dst[:, c, t0:t1], shift[:, c:c + 1], None, ALU.add)


def rounds(eng, tiles, body):
    whole = tiles // RING
    if whole > 1:
        with eng.Fori(0, whole) as i:
            body(i, range(RING))
        rest = whole
    else:
        rest = 0
    for i in range(rest, -(-tiles // RING)):
        body(i, range(min(RING, tiles - i * RING)))


def gate_up_stage(k, name, seg, rhs, N, hidden, side):
    nc = k.nc
    NB = 3
    with ExitStack() as ctx:
        act_out = ctx.enter_context(nc.sbuf_tensor(f"{name}_silu", [P, NB, N], F32))
        pairs, silued, gated = (k.sem(f"{name}_{n}") for n in ("pairs", "silued", "gated"))
        block = ctx.enter_context(nc.Block())
        side.begun = -(-seg.tiles // RING)

        @block.sync
        def _(sp):
            k.stream.feed(sp, seg, pairs, lambda j: 2 * (j // 2) + 2, RING)

        def each(i, js):
            for q in range(len(js) // 2):
                for c in range(2):
                    yield q, c, (2 * q + c) % NB, i * RING + 2 * q + c

        @block.tensor
        def _(pe):
            def body(i, js):
                for q, c, b, n in each(i, js):
                    if c == 0:
                        k.stream.wait(pe, seg, i, 2 * q)
                        k.stream.wait(pe, seg, i, 2 * q + 1)
                    pe.wait_ge(gated, n + 1)
                    for side in range(2):
                        w = k.stream.slot(seg, 2 * q + side)[:, 0:DC * 256].rearrange("p (k m) -> p k m", k=DC)
                        for f in range(DC):
                            last = nc.tensor.matmul(k.bank[b + side * NB][:, 0:N], w[:, f, c * P:(c + 1) * P],
                                                    rhs[:, f, 0:N], start=(f == 0), stop=(f == DC - 1))
                    last.then_inc(pairs, 1)
            rounds(pe, seg.tiles, body)

        @block.scalar
        def _(act):
            for s in range(2):
                side.load(act, 0, s)

            def body(i, js):
                for q, c, b, n in each(i, js):
                    act.wait_ge(pairs, n + 1)
                    nc.scalar.activation(act_out[:, b, :], k.bank[b][:, 0:N], ACT.Silu).then_inc(silued, 1)
                    if 2 * q + c in (len(js) // 2, len(js) - 1):
                        side.reload(act, i, 0 if 2 * q + c == len(js) // 2 else 1)
            rounds(act, seg.tiles, body)

        @block.vector
        def _(dve):
            dve.sem_inc(gated, NB)

            def body(i, js):
                for q, c, b, n in each(i, js):
                    dve.wait_ge(silued, n + 1)
                    nc.vector.tensor_tensor(hidden[:, ds(n, 1), :].rearrange("p a t -> p (a t)"), act_out[:, b, :],
                                            k.bank[b + NB][:, 0:N], ALU.mult).then_inc(gated, 1)
                    side.share(dve, i, 2 * q + c, len(js))
            rounds(dve, seg.tiles, body)


def linear_stage(k, name, seg, tile_chunks, rhs, N, write, banks, on_scalar=False, side=None, first=None):
    nc = k.nc
    done_in_round = [sum(sum(1 for ch in tile_chunks(x) if ch[0]) for x in range(j + 1)) for j in range(RING)]
    with ExitStack() as ctx:
        made, emptied = (k.sem(f"{name}_{n}") for n in ("made", "emptied"))
        block = ctx.enter_context(nc.Block())
        if side is not None:
            @block.scalar
            def _(act):
                for r in range(side.begun, side.ROUNDS - 1):
                    for s in range(2):
                        side.reload(act, r, s)
        per_round = done_in_round[-1]
        assert per_round % banks == 0 or seg.tiles <= RING, (name, per_round)

        @block.sync
        def _(sp):
            k.stream.feed(sp, seg, made, lambda j: done_in_round[j] + (0 if any(ch[0] for ch in tile_chunks(j)) else 1),
                          per_round)

        @block.tensor
        def _(pe):
            def body(i, js):
                for j in js:
                    k.stream.wait(pe, seg, i, j)
                    slot = k.stream.slot(seg, j)
                    before = done_in_round[j - 1] if j else 0
                    for ends, starts, pieces, width in tile_chunks(j):
                        n = i * per_round + before
                        ps = k.bank[before % banks][0:width, 0:N]
                        if starts:
                            pe.wait_ge(emptied, n + 1)
                        for p, (view, r) in enumerate(pieces):
                            last = nc.tensor.matmul(ps, view(slot), rhs(r), start=(starts and p == 0),
                                                    stop=(ends and p == len(pieces) - 1))
                        if ends:
                            last.then_inc(made, 1)
                            before += 1
            rounds(pe, seg.tiles, body)

        def empty(eng):
            eng.sem_inc(emptied, banks)

            def body(i, js):
                total = done_in_round[js[-1]]
                for b in range(total):
                    eng.wait_ge(made, i * per_round + b + 1)
                    write(eng, i * per_round + b, k.bank[b % banks]).then_inc(emptied, 1)
                    if side is not None and len(js) == RING:
                        side.share(eng, i + side.begun, b, total)
            rounds(eng, seg.tiles, body)

        if on_scalar:
            @block.scalar
            def _(act):
                empty(act)

            if first is not None:
                block.vector(first)
        else:
            @block.vector
            def _(dve):
                if first is not None:
                    first(dve)
                empty(dve)


def whole_tiles(kc, width, chunk=P):
    def of(j):
        out = []
        for c0 in range(0, width, chunk):
            w = min(chunk, width - c0)
            pieces = [(lambda s, f=f, c0=c0, w=w: s[:, f * width + c0:f * width + c0 + w], f) for f in range(kc)]
            out.append((True, True, pieces, w))
        return out
    return of


def half_tiles(kc):
    def of(j):
        pieces = [(lambda s, f=f: s[:, f * P:(f + 1) * P], (j % 2) * kc + f) for f in range(kc)]
        return [(j % 2 == 1, j % 2 == 0, pieces, P)]
    return of


def flat(ap):
    return ap.rearrange("p a t -> p (a t)")


def in_proj_stage(k, seg, u, proj):
    starts = [0, P, 2 * P, 3 * P] + [3 * P + ROPE + P * i for i in range(12)] + [3 * P + ROPE + 12 * P]
    widths = [P, P, P, ROPE] + [P] * 12 + [HEADS]

    def of(j):
        lo, w = k.in_tiles[j]
        out = []
        for s, cw in zip(starts, widths):
            if lo <= s < lo + w:
                o = s - lo
                pieces = [(lambda sl, f=f, o=o, w=w, cw=cw: sl[:, f * w + o:f * w + o + cw], f) for f in range(DC)]
                out.append((True, True, pieces, cw))
        return out

    nc = k.nc
    with ExitStack() as ctx:
        made, emptied = (k.sem(f"in_{n}") for n in ("made", "emptied"))
        block = ctx.enter_context(nc.Block())
        count = [sum(len(of(x)) for x in range(j + 1)) for j in range(seg.tiles)]

        @block.sync
        def _(sp):
            for j in range(seg.tiles):
                sp.wait_ge(made, count[j])
                k.stream.start_number(sp, seg.first + j + RING)

        @block.tensor
        def _(pe):
            n = 0
            for j in range(seg.tiles):
                k.stream.wait(pe, seg, j // RING, j % RING)
                slot = k.stream.slot(seg, j)
                for _, _, pieces, w in of(j):
                    if n >= 4:
                        pe.wait_ge(emptied, n - 3)
                    for p, (view, f) in enumerate(pieces):
                        last = nc.tensor.matmul(k.bank[n % 4][0:w, 0:TA], view(slot), u[:, f, :],
                                                start=(p == 0), stop=(p == DC - 1))
                    last.then_inc(made, 1)
                    n += 1

        @block.vector
        def _(dve):
            for n, w in enumerate(widths):
                dve.wait_ge(made, n + 1)
                nc.vector.tensor_copy(proj[0:w, n, :], k.bank[n % 4][0:w, 0:TA]).then_inc(emptied, 1)


def head_norm_stage(k, name, src, dst, rows, heads, width, ones, gain, factor, t0, N, inv=None):
    nc = k.nc
    with ExitStack() as ctx:
        sq = ctx.enter_context(nc.sbuf_tensor(f"{name}_sq", [P, 2, N], F32))
        mean = ctx.enter_context(nc.sbuf_tensor(f"{name}_mean", [P, heads, N], F32))
        r0 = ctx.enter_context(nc.sbuf_tensor(f"{name}_r0", [P, heads, N], F32))
        rr = ctx.enter_context(nc.sbuf_tensor(f"{name}_rr", [P, heads, N], F32))
        squared, summed, meaned, rooted, vdone = (k.sem(f"{name}_{n}") for n in (
            "squared", "summed", "meaned", "rooted", "vdone"))
        block = ctx.enter_context(nc.Block())

        @block.scalar
        def _(act):
            for c in range(heads):
                if c >= 2:
                    act.wait_ge(summed, c - 1)
                nc.scalar.activation(sq[0:rows, c % 2, :], src[0:rows, c, t0:t0 + N], ACT.Square).then_inc(squared, 1)
            act.wait_ge(meaned, heads)
            nc.scalar.activation(flat(r0[0:rows, :, :]), flat(mean[0:rows, :, :]), ACT.Ln).then_inc(rooted, 1)
            act.wait_ge(rooted, 1)
            nc.scalar.activation(flat(r0[0:rows, :, :]), flat(r0[0:rows, :, :]), ACT.Exp, scale=-0.5).then_inc(rooted, 1)

        @block.tensor
        def _(pe):
            for c in range(heads):
                pe.wait_ge(squared, c + 1)
                if c >= 4:
                    pe.wait_ge(meaned, c - 3)
                nc.tensor.matmul(k.bank[c % 4][0:rows, 0:N], ones[0:rows, 0:rows], sq[0:rows, c % 2, :],
                                 start=True, stop=True).then_inc(summed, 1)

        @block.vector
        def _(dve):
            link = Chain(dve, vdone)
            for c in range(heads):
                dve.wait_ge(summed, c + 1)
                nc.vector.tensor_scalar(mean[0:rows, c, :], k.bank[c % 4][0:rows, 0:N], 1.0 / width, EPS,
                                        ALU.mult, ALU.add).then_inc(meaned, 1)
            dve.wait_ge(meaned, heads)
            dve.wait_ge(rooted, 2)
            m, a, b = (flat(x[0:rows, :, :]) for x in (mean, r0, rr))
            link(nc.vector.tensor_tensor(b, a, a, ALU.mult))
            link(nc.vector.scalar_tensor_tensor(out=b, in0=b, scalar=-0.5, in1=m, op0=ALU.mult, op1=ALU.mult))
            link(nc.vector.scalar_tensor_tensor(out=b, in0=b, scalar=1.5, in1=a, op0=ALU.add, op1=ALU.mult))
            if factor != 1.0:
                link(nc.vector.tensor_scalar(b, b, factor, None, ALU.mult))
            for c in range(heads):
                nc.vector.scalar_tensor_tensor(out=dst[0:rows, c, t0:t0 + N], in0=src[0:rows, c, t0:t0 + N],
                                               scalar=gain[0:rows, 0:1], in1=rr[0:rows, c, :],
                                               op0=ALU.mult, op1=ALU.mult)


def expand_stage(k, seg, proj, q, kk, vm):
    nc = k.nc
    uq, ukv = k.stream.slot(seg, 0), k.stream.slot(seg, 1)
    TT = [(0, META), (META, P), (META + P, P)]
    with ExitStack() as ctx:
        made, emptied, vmade, vemptied = (k.sem(f"expand_{n}") for n in (
            "made", "emptied", "vmade", "vemptied"))
        block = ctx.enter_context(nc.Block())
        per_head = 2

        @block.sync
        def _(sp):
            sp.wait_ge(made, HEADS * per_head)
            sp.wait_ge(vmade, 3)
            for j in range(2):
                k.stream.start_number(sp, seg.first + j + RING)

        @block.tensor
        def _(pe):
            k.stream.wait(pe, seg, 0, 0)
            k.stream.wait(pe, seg, 0, 1)
            for h in range(HEADS):
                for side in range(2):
                    n = h * per_head + side
                    if n >= 4:
                        pe.wait_ge(emptied, n - 3)
                    ps = k.bank[n % 4]
                    if side == 0:
                        for f in range(2):
                            o = f * HEADS * QK + h * QK
                            last = nc.tensor.matmul(ps[0:QK, 0:TA], uq[:, o:o + QK], proj[:, f, :],
                                                    start=(f == 0), stop=(f == 1))
                    else:
                        last = nc.tensor.matmul(ps[0:NOPE, 0:TA], ukv[:, h * P:h * P + NOPE], proj[:, 2, :],
                                                start=True, stop=True)
                    last.then_inc(made, 1)
            wv = ukv[:, 0:D].rearrange("p (h m) -> p h m", h=HEADS)[:, :, NOPE:P]
            for t, (t0, n) in enumerate(TT):
                nc.tensor.matmul(k.bank[4 + t][0:n, :], proj[:, 2, t0:t0 + n], wv, start=True, stop=True)\
                    .then_inc(vmade, 1)
            for t, (t0, n) in enumerate(TT):
                if t == 1:
                    pe.wait_ge(vemptied, 1)
                if t == 2:
                    pe.wait_ge(vemptied, 2)
                b = [7, 4, 5][t]
                for c in range(4):
                    last = nc.tensor.transpose(k.bank[b][0:n, c * P:(c + 1) * P], proj[:, 12 + c, t0:t0 + n],
                                               k.ident[:, :])
                last.then_inc(vmade, 1)

        @block.vector
        def _(dve):
            for h in range(HEADS):
                dve.wait_ge(made, 2 * h + 1)
                nc.vector.tensor_copy(q[0:QK, h, :], k.bank[2 * h % 4][0:QK, 0:TA]).then_inc(emptied, 1)
                dve.wait_ge(made, 2 * h + 2)
                nc.vector.tensor_copy(kk[0:NOPE, h, :], k.bank[(2 * h + 1) % 4][0:NOPE, 0:TA]).then_inc(emptied, 1)
                nc.vector.tensor_copy(kk[NOPE:QK, h, :], proj[0:ROPE, 3, :])

        @block.scalar
        def _(act):
            for t, (t0, n) in enumerate(TT):
                act.wait_ge(vmade, t + 1)
                nc.scalar.activation(vm[0:n, t, 0:512], k.bank[4 + t][0:n, :], ACT.Copy).then_inc(vemptied, 1)
            for t, (t0, n) in enumerate(TT):
                act.wait_ge(vmade, 4 + t)
                nc.scalar.activation(vm[0:n, t, 512:1024], k.bank[[7, 4, 5][t]][0:n, :], ACT.Copy)\
                    .then_inc(vemptied, 1)


def rope_stage(k, q, kk, proj, gates_q, gates_k):
    nc = k.nc
    with ExitStack() as ctx:
        tmp = ctx.enter_context(nc.sbuf_tensor("rope_tmp", [P, 2, TA], F32))
        g = ctx.enter_context(nc.sbuf_tensor("gate_tmp", [HEADS, 4, TA], F32))
        zeros = ctx.enter_context(nc.sbuf_tensor("gate_ones", [HEADS, TA], F32))
        turned, sdone, vdone, adone, moved, ready = (k.sem(f"rope_{n}") for n in (
            "turned", "sdone", "vdone", "adone", "moved", "ready"))
        block = ctx.enter_context(nc.Block())
        f = proj[0:HEADS, 16, :]
        b = k.params[0:HEADS, k.col["b_forget"]:k.col["b_forget"] + 1]
        work = [(x, h) for h in range(HEADS) for x in (q, kk)]

        @block.tensor
        def _(pe):
            for n, (x, h) in enumerate(work):
                if n >= 4:
                    pe.wait_ge(sdone, n - 3)
                nc.tensor.matmul(k.bank[n % 4][0:QK, 0:TA], k.rope_turn[0:QK, 0:QK], x[0:QK, h, :],
                                 start=True, stop=True).then_inc(turned, 1)

        @block.scalar
        def _(act):
            act.wait_ge(vdone, 1)
            nc.scalar.activation(g[:, 1, :], g[:, 0, :], ACT.Abs).then_inc(adone, 1)
            act.wait_ge(adone, 1)
            nc.scalar.activation(g[:, 1, :], g[:, 1, :], ACT.Exp, scale=-1.0).then_inc(adone, 1)
            act.wait_ge(adone, 2)
            nc.scalar.activation(g[:, 1, :], g[:, 1, :], ACT.Ln, bias=1.0).then_inc(adone, 1)

        @block.vector
        def _(dve):
            link = Chain(dve, vdone)
            link(nc.vector.tensor_scalar(g[:, 0, :], f, b, None, ALU.add))
            link(nc.vector.memset(zeros[:, :], 1.0))
            link(nc.vector.memset(gates_q[0:2, :, :], 1.0))
            link(nc.vector.memset(gates_k[0:2, :, :], 1.0))
            dve.wait_ge(adone, 3)
            link(nc.vector.scalar_tensor_tensor(out=g[:, 2, :], in0=g[:, 0, :], scalar=0.0, in1=g[:, 1, :],
                                                op0=ALU.min, op1=ALU.subtract))
            link(nc.vector.tensor_tensor_scan(g[:, 3, :], zeros[:, :], g[:, 2, :], 0.0, ALU.mult, ALU.add))
            link(nc.vector.tensor_scalar(g[:, 0, :], g[:, 3, :], -1.0, None, ALU.mult))
            nc.vector.nop().then_inc(ready, 1)
            for n, (x, h) in enumerate(work):
                dve.wait_ge(turned, n + 1)
                link(nc.vector.tensor_tensor(tmp[0:QK, n % 2, :], k.bank[n % 4][0:QK, 0:TA], k.rope_sin[0:QK, :],
                                             ALU.mult))
                nc.vector.tensor_tensor(x[0:QK, h, :], x[0:QK, h, :], k.rope_cos[0:QK, :], ALU.mult).then_inc(sdone, 1)
                dve.wait_ge(sdone, n + 1)
                nc.vector.tensor_tensor(x[0:QK, h, :], x[0:QK, h, :], tmp[0:QK, n % 2, :], ALU.add)

        @block.gpsimd
        def _(pool):
            pool.wait_ge(ready, 1)
            pool.dma_start(gates_q[0:1, :, :], g[:, 3, :]).then_inc(moved, 16)
            pool.dma_start(gates_k[1:2, :, :], g[:, 0, :]).then_inc(moved, 16)
            pool.wait_ge(moved, 32)


def attention_stage(k, q, kk, fq, fk, gates_q, gates_k, vm, o):
    nc = k.nc
    units = [(h, t) for h in range(2 * HEADS) for t in range(2)]
    KT = [(0, META), (META, P), (META + P, P)]
    with ExitStack() as ctx:
        s = ctx.enter_context(nc.sbuf_tensor("scores", [P, 2, TA], F32))
        pr = ctx.enter_context(nc.sbuf_tensor("probs", [P, 2, TA], F32))
        pt = ctx.enter_context(nc.sbuf_tensor("probs_turned", [P, 2, 3 * P], F32))
        st = ctx.enter_context(nc.sbuf_tensor("softmax_stats", [P, 2, 4], F32))
        scored, masked, maxed, powered, inverted, scaled, turned, moved, mixed, kept = (
            k.sem(f"attn_{n}") for n in (
                "scored", "masked", "maxed", "powered", "inverted", "scaled", "turned", "moved", "mixed", "kept"))
        block = ctx.enter_context(nc.Block())

        @block.tensor
        def _(pe):
            def scores(u):
                h, t = units[u]
                K = META + (t + 1) * P
                q0 = META + t * P
                if u >= 2:
                    pe.wait_ge(masked, u - 1)
                ps = k.bank[u % 2][:, 0:K]
                if h < HEADS:
                    nc.tensor.matmul(ps, q[0:QK, h, q0:q0 + P], kk[0:QK, h, 0:K], start=True, stop=True)\
                        .then_inc(scored, 1)
                else:
                    g, r = h - HEADS, (h % 2) * RH
                    nc.tensor.matmul(ps, fq[r:r + RH, g // 2, q0:q0 + P], fk[r:r + RH, g // 2, 0:K],
                                     start=True, stop=False)
                    nc.tensor.matmul(ps, gates_q[0:2, g, q0:q0 + P], gates_k[0:2, g, 0:K], start=False, stop=True)\
                        .then_inc(scored, 1)

            def turn(u):
                h, t = units[u]
                pe.wait_ge(scaled, u + 1)
                if u >= 2:
                    pe.wait_ge(moved, u - 1)
                for c in range(t + 2):
                    k0, n = KT[c]
                    last = nc.tensor.transpose(k.bank[2 + u % 2][0:n, c * P:(c + 1) * P], pr[:, u % 2, k0:k0 + n],
                                               k.ident[:, :])
                last.then_inc(turned, 1)

            def mix(u):
                h, t = units[u]
                pe.wait_ge(moved, u + 1)
                r = (h % 2) * RH
                if u >= 4:
                    pe.wait_ge(kept, u - 3)
                for c in range(t + 2):
                    _, n = KT[c]
                    last = nc.tensor.matmul(k.bank[4 + u % 4][r:r + RH, 0:P], vm[0:n, c, h * RH:(h + 1) * RH],
                                            pt[0:n, u % 2, c * P:(c + 1) * P], start=(c == 0), stop=(c == t + 1))
                last.then_inc(mixed, 1)

            for u in range(len(units) + 2):
                if u < len(units):
                    scores(u)
                if 1 <= u <= len(units):
                    turn(u - 1)
                if u >= 2:
                    mix(u - 2)

        @block.vector
        def _(dve):
            for u in range(len(units) + 1):
                if u < len(units):
                    h, t = units[u]
                    K = META + (t + 1) * P
                    dve.wait_ge(scored, u + 1)
                    if u >= 2:
                        dve.wait_ge(powered, u - 1)
                    nc.vector.tensor_copy(s[:, u % 2, 0:K - P], k.bank[u % 2][:, 0:K - P])
                    nc.vector.tensor_tensor(s[:, u % 2, K - P:K], k.bank[u % 2][:, K - P:K], k.causal[:, :],
                                            ALU.add).then_inc(masked, 1)
                    dve.wait_ge(masked, u + 1)
                    nc.vector.tensor_reduce(st[:, u % 2, 0:1], s[:, u % 2, 0:K], AX.X, ALU.max, negate=True)\
                        .then_inc(maxed, 1)
                    dve.wait_ge(powered, u + 1)
                    nc.vector.reciprocal(st[:, u % 2, 2:3], st[:, u % 2, 1:2]).then_inc(inverted, 1)
                    dve.wait_ge(inverted, u + 1)
                    if u >= 2:
                        dve.wait_ge(turned, u - 1)
                    nc.vector.tensor_scalar(pr[:, u % 2, 0:K], s[:, u % 2, 0:K], st[:, u % 2, 2:3], None, ALU.mult)\
                        .then_inc(scaled, 1)
                if u >= 1:
                    h, t = units[u - 1]
                    dve.wait_ge(turned, u)
                    if u >= 3:
                        dve.wait_ge(mixed, u - 2)
                    b = k.bank[2 + (u - 1) % 2]
                    nc.vector.tensor_copy(pt[0:META, (u - 1) % 2, 0:P], b[0:META, 0:P])
                    nc.vector.tensor_copy(pt[:, (u - 1) % 2, P:P * (t + 2)], b[:, P:P * (t + 2)]).then_inc(moved, 1)

        @block.scalar
        def _(act):
            for u in range(len(units) + 2):
                if u < len(units):
                    h, t = units[u]
                    K = META + (t + 1) * P
                    act.wait_ge(maxed, u + 1)
                    nc.scalar.activation(s[:, u % 2, 0:K], s[:, u % 2, 0:K], ACT.Exp, bias=st[:, u % 2, 0:1],
                                         accum_out=st[:, u % 2, 1:2]).then_inc(powered, 1)
                if u >= 2:
                    h, t = units[u - 2]
                    r = (h % 2) * RH
                    act.wait_ge(mixed, u - 1)
                    nc.scalar.activation(o[r:r + RH, h // 2, t * P:(t + 1) * P],
                                         k.bank[4 + (u - 2) % 4][r:r + RH, 0:P], ACT.Copy).then_inc(kept, 1)


def program(nc, a):
    with ExitStack() as ctx:
        k = Kernel()
        k.nc, k.a, k.stage_sems, k.sem_count = nc, a, [], 0
        k.sb = lambda name, shape, dt=F32: ctx.enter_context(nc.sbuf_tensor(name, shape, dt))
        k.bank = [ctx.enter_context(nc.psum_tensor(f"bank_{b}", [P, 512], F32)) for b in range(8)]
        first_model(k, ctx)
        k.clear()


def first_segments(k, a):
    w = lambda n: a[n][0]
    k.in_tiles = [(0, 256), (256, 160)] + [(416 + 256 * t, 256) for t in range(5)] + [(1696, 264)]
    seg = {}
    for n in ("1", "2"):
        seg["gu" + n] = Segment(4 * 11 // 2, lambda i, j, n=n: [columns(
            w(f"w{n}_gate" if j % 2 == 0 else f"w{n}_up"), DC, (i * 3 + j // 2) * 256, 256)])

        def down(i, j, n=n):
            src = w(f"w{n}_down").rearrange("(k p) m -> p k m", p=P)
            src = src[:, (j % 2) * 11:(j % 2) * 11 + 11, ds((i * 3 + j // 2) * P, P)]
            return [(lambda s: s[:, 0:11 * P].rearrange("p (k m) -> p k m", k=11), src)]
        seg["down" + n] = Segment(16, down)
    seg["in"] = Segment(8, lambda i, j: [columns(w("w_in"), DC, *k.in_tiles[i * RING + j])])
    seg["expand"] = Segment(2, lambda i, j: [columns(w("w_uq"), 2, 0, HEADS * QK) if j == 0
                                             else columns(w("w_ukv"), 1, 0, D)])
    seg["out"] = Segment(4, lambda i, j: [columns(w("w_out"), DC, j * 256, 256)])
    return seg


def cond_stage(k):
    with k.nc.Block() as block:
        @block.scalar
        def _(act):
            k.nc.scalar.activation(k.cond[:, :, 0], param(k, "c", DC), ACT.Silu)
            k.nc.scalar.activation(k.cond[:, :, 1], param(k, "c_ctx", DC), ACT.Silu)


class ModSums:

    WIDTH = 512
    OPS = 2 * DC
    ROUND = 2 * OPS
    ROUNDS = 6 * D // WIDTH // 2

    def __init__(self, k, l, ctx):
        nc = k.nc
        self.k, self.l = k, l
        self.w = [ctx.enter_context(nc.sbuf_tensor(f"ada{l}_w{s}", [P, DC, self.WIDTH], F32)) for s in range(2)]
        self.acc = ctx.enter_context(nc.sbuf_tensor(f"ada{l}_acc", [P, 2, 6 * D], F32))
        self.landed = [k.sem(f"ada_landed{s}") for s in range(2)]
        self.added = k.sem("ada_added")

    def load(self, eng, r, s):
        w = self.WIDTH
        src = self.k.a["ada_w_2"][self.l].rearrange("(k p) m -> p k m", p=P)
        eng.dma_start(self.w[s][:, :, :], src[:, :, ds(r * (2 * w) + s * w, w)]).then_inc(self.landed[s], 16)

    def reload(self, eng, r, s):
        eng.wait_ge(self.added, r * self.ROUND + (s + 1) * self.OPS)
        self.load(eng, r + 1, s)

    def add(self, dve, r, first, end):
        nc, w = self.k.nc, self.WIDTH
        for m in range(first, end):
            s, f, v = m // self.OPS, m % self.OPS // 2, m % 2
            if m % self.OPS == 0:
                dve.wait_ge(self.landed[s], r * 16 + 16)
            to = self.acc[:, v, ds(r * (2 * w) + s * w, w)]
            src, c = self.w[s][:, f, :], self.k.cond[:, f, v:v + 1]
            if f == 0:
                last = nc.vector.tensor_scalar(to, src, c, None, ALU.mult)
            else:
                dve.wait_ge(self.added, r * self.ROUND + m - 1)
                last = nc.vector.scalar_tensor_tensor(out=to, in0=src, scalar=c, in1=to, op0=ALU.mult, op1=ALU.add)
            last.then_inc(self.added, 1)

    def share(self, dve, r, b, of):
        self.add(dve, r, b * self.ROUND // of, (b + 1) * self.ROUND // of)

    def finish(self):
        k, nc, l = self.k, self.k.nc, self.l
        mod, (gain1, gain2) = k.mods[l], k.gains[l]
        summed, done = k.sem("mod_summed"), k.sem("mod_done")
        with nc.Block() as block:
            @block.tensor
            def _(pe):
                for m in range(6 * DC):
                    for v in range(2):
                        last = nc.tensor.matmul(k.bank[0][:, 2 * m + v:2 * m + v + 1],
                                                self.acc[:, v, m * P:(m + 1) * P], k.ones[:, 0:1], start=True, stop=True)
                last.then_inc(summed, 1)

            @block.vector
            def _(dve):
                link = Chain(dve, done)
                dve.wait_ge(summed, 1)
                for v in range(2):
                    link(nc.vector.tensor_tensor(mod[:, v, :], k.bank[0][:, v:12 * DC:2],
                                                 param(k, "ada_b", 6 * DC, 6 * DC * l), ALU.add))
                for v in range(2):
                    for g, at, name in ((gain1, DC, "norm1"), (gain2, 4 * DC, "norm2")):
                        nc.vector.scalar_tensor_tensor(out=g[:, v, :], in0=mod[:, v, at:at + DC], scalar=1.0,
                                                       in1=param(k, name, DC, DC * l), op0=ALU.add, op1=ALU.mult)


def ffn(k, n, h, u, T, t0, seg, gains, to):
    nc = k.nc
    with ExitStack() as ctx:
        hidden = ctx.enter_context(nc.sbuf_tensor(f"hidden{n}", [P, FC, T - t0], F32))
        side = ModSums(k, int(n) - 1, ctx)
        norm_stage(k, f"ffn{n}", h, DC, D, EPS, [(t0, T, gains, None)], u)
        gate_up_stage(k, f"gu{n}", seg["gu" + n], u[:, :, t0:T], T - t0, hidden, side)
        linear_stage(k, f"down{n}", seg["down" + n], half_tiles(11), lambda f: hidden[:, f, :], T - t0,
                     lambda dve, m, ps: nc.vector.scalar_tensor_tensor(
                         out=flat(to[:, ds(m, 1), :]), in0=ps[:, 0:T - t0], scalar=0.5,
                         in1=flat(h[:, ds(m, 1), t0:T]), op0=ALU.mult, op1=ALU.add), 3,
                     side=side)
        side.finish()


def param(k, name, n=1, at=0):
    return k.params[:, k.col[name] + at:k.col[name] + at + n]


def first_model(k, ctx):
    nc, a = k.nc, k.a
    seg = first_segments(k, a)
    order = [seg[n] for n in ("gu1", "down1", "in", "expand", "out", "gu2", "down2")]
    k.seg = seg
    more = second_segments(k, a)
    k.stream = Stream(nc, ctx, order + more)
    k.ident, k.ones, k.head_ones, k.causal = (k.sb(n, [P, P]) for n in ("ident", "ones", "head_ones", "causal"))
    k.rope_cos, k.rope_sin = (k.sb(n, [P, TA]) for n in ("rope_cos_sb", "rope_sin_sb"))
    k.rope_turn = k.sb("rope_turn_sb", [P, QK])
    k.h = k.sb("h", [P, DC, TA])
    k.x = k.sb("x", [P, DC, TB])
    k.cond = k.sb("cond", [P, DC, 2])
    k.mods = [k.sb(f"mod{l}", [P, 2, 6 * DC]) for l in range(2)]
    k.gains = [(k.sb(f"gain1_{l}", [P, 2, DC]), k.sb(f"gain2_{l}", [P, 2, DC])) for l in range(2)]
    stage_setup(k)
    cond_stage(k)
    with nc.sbuf_tensor("u1", [P, DC, TA], F32) as u:
        ffn(k, "1", k.h, u, TA, 0, seg, param(k, "g_ffn1", DC), k.h[:, :, :])
    with ExitStack() as c2:
        sb = lambda n, s: c2.enter_context(nc.sbuf_tensor(n, s, F32))
        proj = sb("proj", [P, 17, TA])
        fqk = sb("fox_qk", [P, 8, TA])
        o = sb("attn_out", [P, DC, SEQ])
        with nc.sbuf_tensor("u_mix", [P, DC, TA], F32) as u:
            norm_stage(k, "mix", k.h, DC, D, EPS, [(0, TA, param(k, "g_mix", DC), None)], u)
            in_proj_stage(k, seg["in"], u, proj)
        q = sb("q", [P, HEADS, TA])
        kk = sb("kk", [P, HEADS, TA])
        vm = sb("v_tokens", [P, 3, D])
        gq = sb("gates_q", [2, HEADS, TA])
        gk = sb("gates_k", [2, HEADS, TA])
        norm_stage(k, "cq", proj[:, 0:2, :], 2, 2 * P, EPS, [(0, TA, param(k, "g_cq", 2), None)], proj[:, 0:2, :])
        norm_stage(k, "ckv", proj[:, 2:3, :], 1, P, EPS, [(0, TA, param(k, "g_ckv", 1), None)], proj[:, 2:3, :])
        expand_stage(k, seg["expand"], proj, q, kk, vm)
        head_norm_stage(k, "qn", q, q, QK, HEADS, QK, k.ones, param(k, "g_q_mla"), QK ** -0.5, META, SEQ)
        head_norm_stage(k, "kn", kk, kk, QK, HEADS, QK, k.ones, param(k, "g_k_mla"), 1.0, 0, TA)
        head_norm_stage(k, "fqn", proj[:, 4:8, :], fqk[:, 0:4, :], P, 4, RH, k.head_ones, param(k, "g_q_fox"),
                        RH ** -0.5, META, SEQ)
        head_norm_stage(k, "fkn", proj[:, 8:12, :], fqk[:, 4:8, :], P, 4, RH, k.head_ones, param(k, "g_k_fox"),
                        1.0, 0, TA)
        rope_stage(k, q, kk, proj, gq, gk)
        attention_stage(k, q, kk, fqk[:, 0:4, :], fqk[:, 4:8, :], gq, gk, vm, o)
        linear_stage(k, "attn_out", seg["out"], whole_tiles(DC, 256), lambda f: o[:, f, :], SEQ,
                     lambda dve, m, ps: nc.vector.tensor_tensor(
                         k.h[:, m, META:TA], k.h[:, m, META:TA], ps[:, 0:SEQ], ALU.add), 4)
    with nc.sbuf_tensor("u2", [P, DC, TA], F32) as u:
        ffn(k, "2", k.h, u, TA, META, seg, param(k, "g_ffn2", DC), k.x[:, :, 0:SEQ])
    k.clear()
    second_model(k, ctx)


def shape_tables():
    half = ROPE // 2
    inv = 1.0 / (10000.0 ** (np.arange(half, dtype=np.float32) / np.float32(half)))
    ang = np.arange(TA, dtype=np.float32)[None, :] * inv.astype(np.float32)[:, None]
    cos, sin = np.ones((QK, TA), np.float32), np.zeros((QK, TA), np.float32)
    cos[NOPE:NOPE + half] = cos[NOPE + half:] = np.cos(ang)
    sin[NOPE:NOPE + half] = sin[NOPE + half:] = np.sin(ang)
    turn = np.zeros((QK, QK), np.float32)
    for i in range(half):
        turn[NOPE + half + i, NOPE + i] = -1.0
        turn[NOPE + i, NOPE + half + i] = 1.0
    return {"rope_cos": cos, "rope_sin": sin, "rope_turn": turn, "rwkv_masks": rwkv_masks()}


def second_segments(k, a):
    seg = k.seg
    w = lambda n: a[n][0]
    for l in range(2):

        def expert(i, j, l=l):
            if j < 4:
                src = a["moe_w_gate_2" if j % 2 == 0 else "moe_w_up_2"][l]
                src = src.rearrange("e (k p) m -> p e k m", p=P)[:, ds(i, 1), :, (j // 2) * 256:(j // 2) * 256 + 256]
                return [(lambda s: s[:, 0:DC * 256].rearrange("p (e k m) -> p e k m", e=1, k=DC), src)]
            src = a["moe_w_down_2"][l].rearrange("e (k p) m -> p e k m", p=P)
            src = src[:, ds(i, 1), :, (j - 4) * 512:(j - 4) * 512 + 512]
            return [(lambda s: s[:, 0:4 * 512].rearrange("p (e k m) -> p e k m", e=1, k=4), src)]
        seg[f"moe{l}"] = Segment(RING * NE, expert)
    seg["ga_u"] = Segment(8, lambda i, j: [columns(w("ga_w_in_2"), DC, (i * RING + j) * 256, 256)])
    seg["ga_v"] = Segment(8, lambda i, j: [columns(w("ga_w_in_2"), DC, GW + (i * RING + j) * 256, 256)])
    seg["ga_out"] = Segment(8, lambda i, j: [columns(w("ga_w_out_2"), GC, (i * RING + j) * P, P)])
    order = ["ga_v", "ga_u", "ga_out", "moe0"]
    order += rwkv_segments(k, a) + ["moe1"]
    return [seg[n] for n in order]


def gmlp(k):
    nc, a, seg = k.nc, k.a, k.seg
    V = [(0, SEQ), (SEQ, TB)]
    parts = [(t0, t1, k.gain1[:, v, :], k.mod[:, v, 0:DC]) for v, (t0, t1) in enumerate(V)]
    with nc.sbuf_tensor("gm_u", [P, GC, TB], F32) as u, nc.sbuf_tensor("gm_v", [P, 4, GW], F32) as v:
        with nc.sbuf_tensor("gm_h", [P, DC, TB], F32) as h:
            norm_stage(k, "gm_norm", k.x, DC, D, EPS, parts, h)
            gmlp_v_stage(k, h, v)
            with ExitStack() as ctx:
                norm, root = gmlp_norm(k, v, ctx)

                def gelu(act, m, ps):
                    if m == GC // 2:
                        root(act)
                    return nc.scalar.activation(u[:, m, :], ps[:, :], ACT.Gelu, bias=param(k, "ga_b_u", 1, m))
                linear_stage(k, "gm_u", seg["ga_u"], whole_tiles(DC, 256), lambda f: h[:, f, :], TB, gelu, 4,
                             on_scalar=True, first=norm)
        gmlp_spatial_stage(k, u, v)

        def write(dve, m, ps):
            for vv, (t0, t1) in enumerate(V):
                last = nc.vector.scalar_tensor_tensor(
                    out=k.x[:, m, t0:t1], in0=ps[:, t0:t1], scalar=k.mod[:, vv, 2 * DC + m:2 * DC + m + 1],
                    in1=k.x[:, m, t0:t1], op0=ALU.mult, op1=ALU.add)
            return last
        linear_stage(k, "gm_out", seg["ga_out"], whole_tiles(GC, P), lambda f: u[:, f, :], TB, write, 6)
    bias_stage(k)


def gmlp_v_stage(k, h, v):
    nc, seg = k.nc, k.seg["ga_v"]
    with ExitStack() as ctx:
        bias = ctx.enter_context(nc.sbuf_tensor("gm_bias", [P, GW], F32))
        landed, made, biased = (k.sem(f"gmv_{n}") for n in ("landed", "made", "biased"))
        block = ctx.enter_context(nc.Block())
        units = [(j, t) for j in range(seg.tiles) for t in range(4)]

        @block.sync
        def _(sp):
            for j in range(seg.tiles):
                sp.wait_ge(made, 4 * (j + 1))
                k.stream.start_number(sp, seg.first + j + RING)

        @block.tensor
        def _(pe):
            for n, (j, t) in enumerate(units):
                if t == 0:
                    k.stream.wait(pe, seg, j // RING, j % RING)
                if n >= 4:
                    pe.wait_ge(biased, n - 3)
                w = k.stream.slot(seg, j)
                for f in range(DC):
                    last = nc.tensor.matmul(k.bank[n % 4][:, 0:256], h[:, f, t * P:(t + 1) * P],
                                            w[:, f * 256:(f + 1) * 256], start=(f == 0), stop=(f == DC - 1))
                last.then_inc(made, 1)

        @block.vector
        def _(dve):
            dve.wait_ge(landed, 16)
            for n, (j, t) in enumerate(units):
                dve.wait_ge(made, n + 1)
                nc.vector.tensor_tensor(v[:, t, j * 256:(j + 1) * 256], k.bank[n % 4][:, 0:256],
                                        bias[:, j * 256:(j + 1) * 256], ALU.add).then_inc(biased, 1)

        @block.scalar
        def _(act):
            act.dma_start(bias[:, :], k.a["ga_b_in_2"][0:1, GW:2 * GW].to_broadcast([P, GW])).then_inc(landed, 16)
            for n, (j, t) in enumerate(units):
                act.wait_ge(biased, n + 1)
                nc.scalar.activation(v[:, t, j * 256:(j + 1) * 256], v[:, t, j * 256:(j + 1) * 256], ACT.Gelu)


def gmlp_norm(k, v, ctx):
    nc = k.nc
    g, b, sq = (ctx.enter_context(nc.sbuf_tensor(f"gm_{n}", [P, GW], F32)) for n in ("ln_g", "ln_b", "sq"))
    st = ctx.enter_context(nc.sbuf_tensor("gm_st", [P, 4, 6], F32))
    landed, done, ready, rooted = (k.sem(f"gmn_{n}") for n in ("landed", "done", "ready", "rooted"))
    with nc.Block() as block:
        @block.scalar
        def _(act):
            act.dma_start(g[:, :], k.a["ga_ln_g_2"].to_broadcast([P, GW])).then_inc(landed, 16)
            act.dma_start(b[:, :], k.a["ga_ln_b_2"].to_broadcast([P, GW])).then_inc(landed, 16)

    def run(dve):
        link = Chain(dve, done)
        for t in range(4):
            link(nc.vector.tensor_reduce(st[:, t, 0:1], v[:, t, :], AX.X, ALU.add))
            link(nc.vector.tensor_scalar(st[:, t, 1:2], st[:, t, 0:1], -1.0 / GW, None, ALU.mult))
            link(nc.vector.tensor_scalar(v[:, t, :], v[:, t, :], st[:, t, 1:2], None, ALU.add))
            link(nc.vector.tensor_tensor(sq[:, :], v[:, t, :], v[:, t, :], ALU.mult))
            link(nc.vector.tensor_reduce(st[:, t, 2:3], sq[:, :], AX.X, ALU.add))
        link(nc.vector.tensor_scalar(st[:, :, 3], st[:, :, 2], 1.0 / GW, LN_EPS, ALU.mult, ALU.add))
        nc.vector.nop().then_inc(ready, 1)
        dve.wait_ge(rooted, 2)
        link(nc.vector.tensor_tensor(st[:, :, 5], st[:, :, 4], st[:, :, 4], ALU.mult))
        link(nc.vector.scalar_tensor_tensor(out=st[:, :, 5], in0=st[:, :, 5], scalar=-0.5, in1=st[:, :, 3],
                                            op0=ALU.mult, op1=ALU.mult))
        link(nc.vector.scalar_tensor_tensor(out=st[:, :, 5], in0=st[:, :, 5], scalar=1.5, in1=st[:, :, 4],
                                            op0=ALU.add, op1=ALU.mult))
        dve.wait_ge(landed, 32)
        for t in range(4):
            link(nc.vector.scalar_tensor_tensor(out=v[:, t, :], in0=v[:, t, :], scalar=st[:, t, 5:6], in1=g[:, :],
                                                op0=ALU.mult, op1=ALU.mult))
            nc.vector.tensor_tensor(v[:, t, :], v[:, t, :], b[:, :], ALU.add)

    def root(act):
        act.wait_ge(ready, 1)
        nc.scalar.activation(st[:, :, 4], st[:, :, 3], ACT.Ln).then_inc(rooted, 1)
        act.wait_ge(rooted, 1)
        nc.scalar.activation(st[:, :, 4], st[:, :, 4], ACT.Exp, scale=-0.5).then_inc(rooted, 1)
    return run, root


def gmlp_spatial_stage(k, u, v):
    nc = k.nc
    with ExitStack() as ctx:
        ws = ctx.enter_context(nc.sbuf_tensor("gm_ws", [P, GC, P], F32))
        wt = ctx.enter_context(nc.sbuf_tensor("gm_wt", [P, GC, P], F32))
        bs = ctx.enter_context(nc.sbuf_tensor("gm_bs", [1, GC, P], F32))
        landed, blanded, turned, copied, mixed, used = (k.sem(f"gms_{n}") for n in (
            "landed", "blanded", "turned", "copied", "mixed", "used"))
        block = ctx.enter_context(nc.Block())

        @block.tensor
        def _(pe):
            pe.wait_ge(landed, 16)
            pe.wait_ge(blanded, 16)
            for q in range(4):
                for c in range(4):
                    last = nc.tensor.transpose(k.bank[q][:, c * P:(c + 1) * P], ws[:, 4 * q + c, :], k.ident[:, :])
                last.then_inc(turned, 1)
            for g in range(GC):
                pe.wait_ge(copied, g // 4 + 1)
                if g >= 4:
                    pe.wait_ge(used, g - 3)
                for t in range(4):
                    ps = k.bank[4 + g % 4][:, t * P:(t + 1) * P]
                    nc.tensor.matmul(ps, v[:, t, g * P:(g + 1) * P], wt[:, g, :], start=True, stop=False)
                    last = nc.tensor.matmul(ps, k.ones[0:1, :], bs[0:1, g, :], start=False, stop=True)
                last.then_inc(mixed, 1)

        @block.vector
        def _(dve):
            for q in range(4):
                dve.wait_ge(turned, q + 1)
                nc.vector.tensor_copy(wt[:, 4 * q:4 * q + 4, :].rearrange("p a b -> p (a b)"), k.bank[q][:, :])\
                    .then_inc(copied, 1)
            for g in range(GC):
                dve.wait_ge(mixed, g + 1)
                nc.vector.tensor_tensor(u[:, g, :], k.bank[4 + g % 4][:, :], u[:, g, :], ALU.mult).then_inc(used, 1)

        @block.scalar
        def _(act):
            act.dma_start(ws[:, :, :], k.a["ga_w_s_2"][0].rearrange("g p q -> p g q")).then_inc(landed, 16)
            act.dma_start(bs[:, :, :], k.a["ga_b_s_2"]).then_inc(blanded, 16)


def route_stage(k, l, hm, T, rows, slot_token, table, dest, desti, wts, out_rows):
    nc, a = k.nc, k.a
    TT = T // P
    nov = 2 * T // SLOTS - 1
    cap = NE * SLOTS + nov * SLOTS
    with ExitStack() as ctx:
        sb = lambda n, s, dt=F32: ctx.enter_context(nc.sbuf_tensor(f"rt{l}_{n}", s, dt))
        wr = sb("wr", [P, DC, NG + NE])
        bias = sb("bias", [P, NG + NE])
        hrow = sb("hrow", [P, 2, D])
        L = sb("logits", [P, TT, NG + NE])
        A = sb("assigned", [P, TT, NE])
        one = sb("onehots", [P, TT, 2, NE])
        w4 = sb("w4", [P, 4 * NG])
        gexp = sb("gexp", [P, TT, NG])
        rank = sb("rank", [P, NE])
        prod = sb("prod", [P, NE])
        lm = sb("lm", [P, 2, NE])
        st = sb("st", [P, TT, 16])
        before = sb("before", [P, P])
        pos = sb("pos", [P, TT, NE])
        cnt = sb("cnt", [P, 6, NE])
        eid = sb("eid", [P, 4])
        ones_row = sb("ones_row", [P, NE])
        ids = sb("ids", [P, TT], I32)
        tab_f = sb("tab_f", [P, 2])
        tab_i = sb("tab_i", [P, 2], I32)
        zero = sb("zero", [P, SLOTS], I32)
        zero_row = sb("zero_row", [SLOTS, D])
        names = ("wl", "made", "vdone", "exped", "gmaxed", "assigned", "placed", "rturned", "rcopied", "rstored0",
                 "rstored1", "consts", "zeroed", "scattered", "destined", "diffed", "tabled", "cleared")
        (wl, made, vdone, exped, gmaxed, assigned, placed, rturned, rcopied, rstored0, rstored1, consts, zeroed,
         scattered, destined, diffed, tabled, cleared) = (k.sem(f"rt_{n}") for n in names)
        rstored = (rstored0, rstored1)
        block = ctx.enter_context(nc.Block())

        @block.sync
        def _(sp):
            sp.dma_start(wr[:, :, 0:NG], a["moe_w_grp_2"][l].rearrange("(k p) m -> p k m", p=P)).then_inc(wl, 16)
            sp.dma_start(wr[:, :, NG:], a["moe_w_exp_2"][l].rearrange("(k p) m -> p k m", p=P)).then_inc(wl, 16)
            sp.dma_start(bias[:, 0:NG], a["moe_b_grp_2"][l:l + 1, :].to_broadcast([P, NG])).then_inc(wl, 16)
            sp.dma_start(bias[:, NG:], a["moe_b_exp_2"][l:l + 1, :].to_broadcast([P, NE])).then_inc(wl, 16)
            for t in range(TT):
                sp.wait_ge(rcopied, 2 * t + 2)
                sp.dma_start(rows[t * P:(t + 1) * P, :], hrow[:, t % 2, :]).then_inc(rstored[t % 2], 16)
            sp.wait_ge(consts, 8)
            for b in range(nov):
                sp.dma_start(out_rows[(NE + b) * SLOTS:(NE + b + 1) * SLOTS, :], zero_row[:, :]).then_inc(cleared, 16)
            sp.wait_ge(cleared, 16 * nov)
            for b in range(2):
                sp.wait_ge(rstored[b], 16 * (TT // 2))

        @block.gpsimd
        def _(pool):
            pool.memset(zero[:, :], 0).then_inc(consts, 1)
            pool.wait_ge(consts, 1)
            nblk = cap // SLOTS
            pool.dma_start(slot_token.rearrange("(b s) o -> b (s o)", s=SLOTS), zero[0:nblk, :]).then_inc(zeroed, 16)
            pool.iota(rank[:, :], [[-1, NE]], base=NE, channel_multiplier=0,
                      allow_small_or_imprecise_dtypes=True).then_inc(consts, 1)
            pool.iota(w4[:, 0:NG], [[-1, NG]], base=NG, channel_multiplier=0,
                      allow_small_or_imprecise_dtypes=True).then_inc(consts, 1)
            pool.iota(eid[:, 0:1], [[0, 1]], base=0, channel_multiplier=1,
                      allow_small_or_imprecise_dtypes=True).then_inc(consts, 1)
            pool.iota(ids[:, :], [[P, TT]], base=0, channel_multiplier=1).then_inc(consts, 1)
            pool.memset(before[:, :], 1.0).then_inc(consts, 1)
            pool.wait_ge(consts, 6)
            pool.affine_select(out=before[:, :], in_=before[:, :], compare_op=ALU.is_ge, fill=0.0, base=-1,
                               pattern=[[1, P]], channel_multiplier=-1).then_inc(consts, 1)
            pool.memset(zero_row[:, :], 0.0).then_inc(consts, 1)
            pool.wait_ge(zeroed, 16)
            pool.wait_ge(destined, 1)
            for t in range(TT):
                for c in range(2):
                    pool.indirect_dma_start(slot_token, bass.IndirectOffsetOnAxis(ap=desti[:, t, c:c + 1], axis=0),
                                            ids[:, t:t + 1], None).then_inc(scattered, 16)
            pool.wait_ge(scattered, 32 * TT)
            pool.wait_ge(tabled, 1)
            pool.dma_start(table, tab_i[0:16, :]).then_inc(zeroed, 16)
            pool.wait_ge(zeroed, 32)

        @block.tensor
        def _(pe):
            pe.wait_ge(wl, 64)
            for t in range(TT):
                for f in range(DC):
                    last = nc.tensor.matmul(k.bank[0][:, 64 * t:64 * t + NG + NE], hm[:, f, t * P:(t + 1) * P],
                                            wr[:, f, :], start=(f == 0), stop=(f == DC - 1))
                last.then_inc(made, 1)
            for t in range(TT):
                for half in range(2):
                    n = 2 * t + half
                    if n >= 4:
                        pe.wait_ge(rcopied, n - 3)
                    for c in range(4):
                        last = nc.tensor.transpose(k.bank[1 + n % 4][:, c * P:(c + 1) * P],
                                                   hm[:, half * 4 + c, t * P:(t + 1) * P], k.ident[:, :])
                    last.then_inc(rturned, 1)
            pe.wait_ge(consts, 7)
            for t in range(TT):
                pe.wait_ge(assigned, t + 1)
                for s in range(t + 1):
                    last = nc.tensor.matmul(k.bank[5][:, NE * t:NE * t + NE], before[:, :] if s == t else k.ones[:, :],
                                            A[:, s, :], start=(s == 0), stop=(s == t))
                last.then_inc(placed, 1)
            for s in range(TT):
                last = nc.tensor.matmul(k.bank[6][:, 0:NE], k.ones[:, :], A[:, s, :], start=(s == 0), stop=(s == TT - 1))
            last.then_inc(placed, 1)

        @block.scalar
        def _(act):
            for t in range(TT):
                act.wait_ge(gmaxed, t + 1)
                nc.scalar.activation(gexp[:, t, :], L[:, t, 0:NG], ACT.Exp, bias=st[:, t, 0:1],
                                     accum_out=st[:, t, 1:2]).then_inc(exped, 1)
                for half in range(2):
                    n = 2 * t + half
                    act.wait_ge(rturned, n + 1)
                    if t >= 2:
                        act.wait_ge(rstored[t % 2], 16 * (t // 2))
                    nc.scalar.activation(hrow[:, t % 2, half * 512:(half + 1) * 512], k.bank[1 + n % 4][:, :],
                                         ACT.Copy).then_inc(rcopied, 1)
            act.wait_ge(diffed, 1)
            nc.scalar.activation(st[:, :, 9], st[:, :, 8], ACT.Exp).then_inc(exped, 1)

        @block.vector
        def _(dve):
            link = Chain(dve, vdone)
            dve.wait_ge(consts, 3)
            link(nc.vector.memset(ones_row[:, :], 1.0))
            for t in range(TT):
                lt = L[:, t, :]
                s = lambda n: st[:, t, n:n + 1]
                if t == 0:
                    dve.wait_ge(made, TT)
                link(nc.vector.tensor_tensor(lt, k.bank[0][:, 64 * t:64 * t + NG + NE], bias[:, :], ALU.add))
                link(nc.vector.tensor_reduce(s(2), lt[:, 0:NG], AX.X, ALU.max))
                nc.vector.tensor_scalar(s(0), s(2), -1.0, None, ALU.mult).then_inc(gmaxed, 1)
                link(nc.vector.scalar_tensor_tensor(out=w4[:, 12:16], in0=lt[:, 0:NG], scalar=s(2), in1=w4[:, 0:NG],
                                                    op0=ALU.is_equal, op1=ALU.mult))
                link(nc.vector.tensor_reduce(s(3), w4[:, 12:16], AX.X, ALU.max))
                link(nc.vector.tensor_scalar(w4[:, 12:16], w4[:, 0:NG], s(3), None, ALU.is_equal))
                link(nc.vector.tensor_scalar(w4[:, 12:16], w4[:, 12:16], -NEG, NEG, ALU.mult, ALU.add))
                for g in range(NG):
                    last = nc.vector.tensor_scalar(lm[:, 0, g * EG:(g + 1) * EG],
                                                   lt[:, NG + g * EG:NG + (g + 1) * EG], w4[:, 12 + g:13 + g], None,
                                                   ALU.add)
                link(last)
                for c in range(2):
                    link(nc.vector.tensor_reduce(s(4 + c), lm[:, c, :], AX.X, ALU.max))
                    link(nc.vector.scalar_tensor_tensor(out=prod[:, :], in0=lm[:, c, :], scalar=s(4 + c),
                                                        in1=rank[:, :], op0=ALU.is_equal, op1=ALU.mult))
                    link(nc.vector.tensor_reduce(s(6 + c), prod[:, :], AX.X, ALU.max))
                    link(nc.vector.tensor_scalar(one[:, t, c, :], rank[:, :], s(6 + c), None, ALU.is_equal))
                    if c == 0:
                        link(nc.vector.scalar_tensor_tensor(out=lm[:, 1, :], in0=one[:, t, 0, :], scalar=4 * NEG,
                                                            in1=lm[:, 0, :], op0=ALU.mult, op1=ALU.add))
                nc.vector.tensor_tensor(A[:, t, :], one[:, t, 0, :], one[:, t, 1, :], ALU.add).then_inc(assigned, 1)
            link(nc.vector.tensor_tensor(st[:, :, 8], st[:, :, 5], st[:, :, 4], ALU.subtract))
            nc.vector.nop().then_inc(diffed, 1)
            dve.wait_ge(exped, TT + 1)
            link(nc.vector.scalar_tensor_tensor(out=st[:, :, 10], in0=st[:, :, 9], scalar=1.0, in1=st[:, :, 1],
                                                op0=ALU.add, op1=ALU.mult))
            link(nc.vector.reciprocal(wts[:, :, 0], st[:, :, 10]))
            link(nc.vector.tensor_tensor(wts[:, :, 1], wts[:, :, 0], st[:, :, 9], ALU.mult))
            dve.wait_ge(placed, TT + 1)
            count, many, upto, front, far = (cnt[:, n, :] for n in range(5))
            link(nc.vector.tensor_copy(count, k.bank[6][:, 0:NE]))
            link(nc.vector.tensor_scalar(many, count, float(SLOTS), None, ALU.is_gt))
            for j in range(2, T // SLOTS):
                link(nc.vector.scalar_tensor_tensor(out=many, in0=count, scalar=float(SLOTS * j), in1=many,
                                                    op0=ALU.is_gt, op1=ALU.add))
            link(nc.vector.tensor_tensor_scan(upto, ones_row[:, :], many, 0.0, ALU.mult, ALU.add))
            link(nc.vector.tensor_tensor(front, upto, many, ALU.subtract))
            link(nc.vector.scalar_tensor_tensor(out=far, in0=front, scalar=-1.0, in1=rank[:, :], op0=ALU.add,
                                                op1=ALU.add))
            link(nc.vector.tensor_scalar(far, far, float(SLOTS), None, ALU.mult))
            for t in range(TT):
                link(nc.vector.tensor_copy(pos[:, t, :], k.bank[5][:, NE * t:NE * t + NE]))
                for c in range(2):
                    s = lambda n: st[:, t, n:n + 1]
                    link(nc.vector.tensor_tensor(prod[:, :], pos[:, t, :], one[:, t, c, :], ALU.mult))
                    link(nc.vector.tensor_reduce(s(11), prod[:, :], AX.X, ALU.add))
                    link(nc.vector.tensor_tensor(prod[:, :], far, one[:, t, c, :], ALU.mult))
                    link(nc.vector.tensor_reduce(s(12), prod[:, :], AX.X, ALU.add))
                    link(nc.vector.tensor_scalar(s(13), s(11), float(SLOTS), None, ALU.is_ge))
                    link(nc.vector.scalar_tensor_tensor(out=s(12), in0=s(12), scalar=s(13), in1=s(11),
                                                        op0=ALU.mult, op1=ALU.add))
                    link(nc.vector.tensor_scalar(s(14), s(6 + c), -float(SLOTS), float(NE * SLOTS), ALU.mult, ALU.add))
                    link(nc.vector.tensor_tensor(dest[:, t, c:c + 1], s(14), s(12), ALU.add))
            link(nc.vector.tensor_copy(desti[:, :, :], dest[:, :, :]))
            nc.vector.nop().then_inc(destined, 1)
            link(nc.vector.tensor_scalar(prod[:, :], front, eid[:, 0:1], None, ALU.is_le))
            link(nc.vector.scalar_tensor_tensor(out=prod[:, :], in0=upto, scalar=eid[:, 0:1], in1=prod[:, :],
                                                op0=ALU.is_gt, op1=ALU.mult))
            link(nc.vector.tensor_scalar(far, rank[:, :], -1.0, float(NE), ALU.mult, ALU.add))
            link(nc.vector.tensor_tensor(prod[:, :], prod[:, :], far, ALU.mult))
            link(nc.vector.tensor_reduce(tab_f[:, 0:1], prod[:, :], AX.X, ALU.add))
            link(nc.vector.tensor_copy(tab_f[:, 1:2], upto[:, NE - 1:NE]))
            link(nc.vector.tensor_copy(tab_i[:, :], tab_f[:, :]))
            nc.vector.nop().then_inc(tabled, 1)


def experts_stage(k, l, rows, slots, out_rows):
    nc = k.nc
    seg = k.seg[f"moe{l}"]
    with ExitStack() as ctx:
        sb = lambda n, s, dt=F32: ctx.enter_context(nc.sbuf_tensor(f"ex{l}_{n}", s, dt))
        idx = [sb(f"idx{s}", [SLOTS, 1], I32) for s in range(2)]
        xg = sb("xg", [SLOTS, 2, D])
        xt = sb("xt", [P, 2, DC * SLOTS])
        act_out = sb("silu", [P, 2, 4 * SLOTS])
        hid = sb("hidden", [P, 2, 4 * SLOTS])
        y = sb("y", [SLOTS, 2, D])
        (picked, got0, got1, turned, copied, spent, silued, gated, kept_a, kept_d, put0, put1) = (
            k.sem(f"ex_{n}") for n in (
                "picked", "got0", "got1", "turned", "copied", "spent", "silued", "gated", "kept_a", "kept_d",
                "put0", "put1"))
        asked = k.sem("ex_asked")
        got, put = (got0, got1), (put0, put1)
        block = ctx.enter_context(nc.Block())
        half = 2 * SLOTS

        def pairs(eng, body):
            with eng.Fori(0, NE // 2 - 1) as i:
                for s in range(2):
                    body(i, s, i * 2 + s, False)
            for s in range(2):
                body(NE // 2 - 1, s, NE - 2 + s, s == 1)

        @block.sync
        def _(sp):
            k.stream.feed(sp, seg, spent, lambda j: (1, 1, 2, 2, 3, 4)[j], 4)

        @block.gpsimd
        def _(pool):
            def gather(i, s, e, last):
                pool.wait_ge(turned, e + 1)
                nc.gpsimd.tensor_copy(idx[s][:, :], slots[0:SLOTS, ds(e, 1)]).then_inc(picked, 1)
                pool.wait_ge(picked, e + 1)
                pool.sem_inc(asked, 1)
                pool.indirect_dma_start(xg[:, s, :], None, rows, bass.IndirectOffsetOnAxis(ap=idx[s][:, :], axis=0))\
                    .then_inc(got[s], 16)
            pairs(pool, gather)

        @block.tensor
        def _(pe):
            pe.sem_inc(turned, 2)

            def turn(s):
                for f in range(DC):
                    last = nc.tensor.transpose(k.bank[s][:, f * SLOTS:(f + 1) * SLOTS], xg[:, s, f * P:(f + 1) * P],
                                               k.ident[0:SLOTS, 0:SLOTS])
                last.then_inc(turned, 1)

            def expert(i, s, e, last_one):
                pe.wait_ge(copied, e + 1)
                for q in range(2):
                    for side in range(2):
                        k.stream.wait(pe, seg, e, 2 * q + side)
                    for side in range(2):
                        w = k.stream.slot(seg, 2 * q + side)
                        for c in range(2):
                            o = (2 * side + c) * SLOTS
                            for f in range(DC):
                                if not last_one and (q, side, c, f) == (1, 1, 1, DC - 1):
                                    pe.wait_ge(got[1 - s], (i + s) * 16 + 16)
                                last = nc.tensor.matmul(k.bank[2 + q][:, o:o + SLOTS],
                                                        w[:, f * 256 + c * P:f * 256 + (c + 1) * P],
                                                        xt[:, s, f * SLOTS:(f + 1) * SLOTS],
                                                        start=(f == 0), stop=(f == DC - 1))
                    last.then_inc(spent, 1)
                if not last_one:
                    turn(1 - s)
                pe.wait_ge(gated, e * 2 + 2)
                pe.wait_ge(kept_a, e + 1)
                pe.wait_ge(kept_d, e + 1)
                for n in range(2):
                    k.stream.wait(pe, seg, e, 4 + n)
                    w = k.stream.slot(seg, 4 + n)
                    for f in range(4):
                        last = nc.tensor.matmul(k.bank[4 + 2 * s + n][0:SLOTS, :], hid[:, s, f * SLOTS:(f + 1) * SLOTS],
                                                w[:, f * 512:(f + 1) * 512], start=(f == 0), stop=(f == 3))
                    last.then_inc(spent, 1)

            pe.wait_ge(got[0], 16)
            turn(0)
            pairs(pe, expert)

        @block.scalar
        def _(act):
            act.sem_inc(kept_a, 2)
            for s in range(2):
                act.sem_inc(put[s], 16)

            def expert(i, s, e, last_one):
                for q in range(2):
                    act.wait_ge(spent, e * 4 + q + 1)
                    nc.scalar.activation(act_out[:, s, q * half:(q + 1) * half],
                                         k.bank[2 + q][:, 0:half], ACT.Silu).then_inc(silued, 1)
                act.wait_ge(spent, e * 4 + 3)
                act.wait_ge(put[s], i * 16 + 16)
                nc.scalar.activation(y[:, s, 0:512], k.bank[4 + 2 * s][0:SLOTS, :], ACT.Copy).then_inc(kept_a, 1)
                act.wait_ge(kept_a, e + 3)
                act.wait_ge(kept_d, e + 3)
                act.dma_start(out_rows[ds(e * SLOTS, SLOTS), :], y[:, s, :]).then_inc(put[s], 16)
            pairs(act, expert)
            for s in range(2):
                act.wait_ge(put[s], 16 * (NE // 2) + 16)

        @block.vector
        def _(dve):
            dve.sem_inc(kept_d, 2)

            def copy(i, s, e):
                dve.wait_ge(turned, e + 3)
                nc.vector.tensor_copy(xt[:, s, :], k.bank[s][:, :]).then_inc(copied, 1)

            def expert(i, s, e, last_one):
                for q in range(2):
                    dve.wait_ge(silued, e * 2 + q + 1)
                    nc.vector.tensor_tensor(hid[:, s, q * half:(q + 1) * half], act_out[:, s, q * half:(q + 1) * half],
                                            k.bank[2 + q][:, half:2 * half],
                                            ALU.mult).then_inc(gated, 1)
                if not last_one:
                    copy(i, 1 - s, e + 1)
                dve.wait_ge(spent, e * 4 + 4)
                dve.wait_ge(put[s], i * 16 + 16)
                nc.vector.tensor_copy(y[:, s, 512:1024], k.bank[5 + 2 * s][0:SLOTS, :]).then_inc(kept_d, 1)

            copy(0, 0, 0)
            pairs(dve, expert)


def overflow_stage(k, l, nov, rows, slots, tab, out_rows):
    nc, a = k.nc, k.a
    with ExitStack() as ctx:
        sb = lambda n, s, dt=F32: ctx.enter_context(nc.sbuf_tensor(f"ov{l}_{n}", s, dt))
        w = [sb(f"w{n}", [P, 2048]) for n in range(6)]
        idx = sb("idx", [SLOTS, 1], I32)
        xg = sb("xg", [SLOTS, D])
        xt = sb("xt", [P, DC * SLOTS])
        act_out = sb("silu", [P, 4 * SLOTS])
        hid = sb("hidden", [P, 4 * SLOTS])
        y = sb("y", [SLOTS, D])
        landed = [k.sem(f"ov_landed{n}") for n in range(6)]
        (picked, got, turned, copied, spent, silued, gated, kept, put) = (
            k.sem(f"ov_{n}") for n in (
                "picked", "got", "turned", "copied", "spent", "silued", "gated", "kept", "put"))
        asked = k.sem("ov_asked")
        block = ctx.enter_context(nc.Block())

        def blocks(eng, body):
            count = eng.value_load(tab[0:1, 0, 1:2], min_val=0, max_val=nov)
            with eng.Fori(0, nov) as b:
                with eng.If(b < count):
                    body(b)
            return count

        @block.sync
        def _(sp):
            def load(b):
                e = sp.value_load(tab[0:1, ds(b, 1), 0:1].rearrange("p a b -> p (a b)"), min_val=0, max_val=NE - 1)
                sp.wait_ge(spent, b + 1)
                for j in range(6):
                    if j < 4:
                        src = a["moe_w_gate_2" if j % 2 == 0 else "moe_w_up_2"][l]
                        src = src.rearrange("e (k p) m -> p e k m", p=P)[:, ds(e, 1), :, (j // 2) * 256:(j // 2) * 256 + 256]
                        kc = DC
                    else:
                        src = a["moe_w_down_2"][l].rearrange("e (k p) m -> p e k m", p=P)
                        src = src[:, ds(e, 1), :, (j - 4) * 512:(j - 4) * 512 + 512]
                        kc = 4
                    sp.dma_start(w[j][:, :].rearrange("p (e k m) -> p e k m", e=1, k=kc), src).then_inc(landed[j], 16)
            blocks(sp, load)

        @block.gpsimd
        def _(pool):
            def gather(b):
                pool.wait_ge(turned, b + 1)
                nc.gpsimd.tensor_copy(idx[:, :], slots[0:SLOTS, ds(b + NE, 1)]).then_inc(picked, 1)
                pool.wait_ge(picked, b + 1)
                pool.sem_inc(asked, 1)
                pool.indirect_dma_start(xg[:, :], None, rows, bass.IndirectOffsetOnAxis(ap=idx[:, :], axis=0))\
                    .then_inc(got, 16)
            blocks(pool, gather)

        @block.tensor
        def _(pe):
            def block_(b):
                pe.wait_ge(got, b * 16 + 16)
                for f in range(DC):
                    last = nc.tensor.matmul(k.bank[0][:, f * SLOTS:(f + 1) * SLOTS], xg[:, f * P:(f + 1) * P],
                                            k.ident[0:SLOTS, 0:SLOTS], start=True, stop=True)
                last.then_inc(turned, 1)
                pe.wait_ge(copied, b + 1)
                for j in range(4):
                    pe.wait_ge(landed[j], b * 16 + 16)
                    for c in range(2):
                        o = (j % 2) * 4 * SLOTS + (2 * (j // 2) + c) * SLOTS
                        for f in range(DC):
                            last = nc.tensor.matmul(k.bank[2][:, o:o + SLOTS],
                                                    w[j][:, f * 256 + c * P:f * 256 + (c + 1) * P],
                                                    xt[:, f * SLOTS:(f + 1) * SLOTS], start=(f == 0), stop=(f == DC - 1))
                last.then_inc(silued, 1)
                pe.wait_ge(gated, b + 1)
                for n in range(2):
                    pe.wait_ge(landed[4 + n], b * 16 + 16)
                    for f in range(4):
                        last = nc.tensor.matmul(k.bank[4 + n][0:SLOTS, :], hid[:, f * SLOTS:(f + 1) * SLOTS],
                                                w[4 + n][:, f * 512:(f + 1) * 512], start=(f == 0), stop=(f == 3))
                last.then_inc(spent, 1)
            pe.sem_inc(turned, 1)
            pe.sem_inc(spent, 1)
            blocks(pe, block_)

        @block.scalar
        def _(act):
            def block_(b):
                act.wait_ge(silued, b * 2 + 1)
                nc.scalar.activation(act_out[:, :], k.bank[2][:, 0:4 * SLOTS], ACT.Silu).then_inc(silued, 1)
                act.wait_ge(kept, b + 1)
                act.dma_start(out_rows[ds(b * SLOTS + NE * SLOTS, SLOTS), :], y[:, :]).then_inc(put, 16)
            act.sem_inc(put, 16)
            blocks(act, block_)

        @block.vector
        def _(dve):
            def block_(b):
                dve.wait_ge(turned, b + 2)
                nc.vector.tensor_copy(xt[:, :], k.bank[0][:, :]).then_inc(copied, 1)
                dve.wait_ge(silued, b * 2 + 2)
                nc.vector.tensor_tensor(hid[:, :], act_out[:, :], k.bank[2][:, 4 * SLOTS:8 * SLOTS], ALU.mult)\
                    .then_inc(gated, 1)
                dve.wait_ge(spent, b + 2)
                dve.wait_ge(put, b * 16 + 16)
                for n in range(2):
                    last = nc.vector.tensor_copy(y[:, n * 512:(n + 1) * 512], k.bank[4 + n][0:SLOTS, :])
                last.then_inc(kept, 1)
            count = blocks(dve, block_)
            dve.wait_ge(put, count * 16 + 16)
            nc.vector.memset(y[0:1, 0:1], 0.0)


def combine_stage(k, l, T, desti, wts, out_rows):
    nc = k.nc
    TT = T // P
    with ExitStack() as ctx:
        y = ctx.enter_context(nc.sbuf_tensor(f"cb{l}_y", [P, TT, 2, D], F32))
        got = [k.sem(f"cb_got{t}") for t in range(TT)]
        weighed, summed, turned, added = (k.sem(f"cb_{n}") for n in (
            "weighed", "summed", "turned", "added"))
        block = ctx.enter_context(nc.Block())

        @block.gpsimd
        def _(pool):
            for t in range(TT):
                for c in range(2):
                    pool.indirect_dma_start(y[:, t, c, :], None, out_rows,
                                            bass.IndirectOffsetOnAxis(ap=desti[:, t, c:c + 1], axis=0))\
                        .then_inc(got[t], 16)

        @block.scalar
        def _(act):
            for t in range(TT):
                act.wait_ge(got[t], 32)
                nc.scalar.activation(y[:, t, 1, :], y[:, t, 1, :], ACT.Copy, scale=wts[:, t, 1:2]).then_inc(weighed, 1)

        @block.tensor
        def _(pe):
            for t in range(TT):
                pe.wait_ge(summed, t + 1)
                for half in range(2):
                    n = 2 * t + half
                    if n >= 4:
                        pe.wait_ge(added, n - 3)
                    for c in range(4):
                        f = (half * 4 + c) * P
                        last = nc.tensor.transpose(k.bank[n % 4][:, c * P:(c + 1) * P], y[:, t, 0, f:f + P],
                                                   k.ident[:, :])
                    last.then_inc(turned, 1)

        @block.vector
        def _(dve):
            for t in range(TT):
                dve.wait_ge(weighed, t + 1)
                nc.vector.scalar_tensor_tensor(out=y[:, t, 0, :], in0=y[:, t, 0, :], scalar=wts[:, t, 0:1],
                                               in1=y[:, t, 1, :], op0=ALU.mult, op1=ALU.add).then_inc(summed, 1)
                for half in range(2):
                    n = 2 * t + half
                    dve.wait_ge(turned, n + 1)
                    for c in range(4):
                        f = half * 4 + c
                        v = (t * P) // SEQ
                        last = nc.vector.scalar_tensor_tensor(
                            out=k.x[:, f, t * P:(t + 1) * P], in0=k.bank[n % 4][:, c * P:(c + 1) * P],
                            scalar=k.mod[:, v, 5 * DC + f:5 * DC + f + 1], in1=k.x[:, f, t * P:(t + 1) * P],
                            op0=ALU.mult, op1=ALU.add)
                    last.then_inc(added, 1)


def load_slots_stage(k, slot_token, table, slots, tab, nblk):
    nc = k.nc
    landed = k.sem("slots_landed")
    with nc.Block() as block:
        @block.sync
        def _(sp):
            with nc.allow_non_contiguous_dma(reason="token numbers, one block a column"):
                sp.dma_start(slots[0:SLOTS, 0:nblk], slot_token.rearrange("(b s) o -> s (b o)", s=SLOTS))\
                    .then_inc(landed, 16)
            sp.dma_start(tab[:, :, :], table.rearrange("(o b) c -> o b c", o=1)).then_inc(landed, 16)
            sp.wait_ge(landed, 32)


def moe(k, l, T):
    nc = k.nc
    nov = 2 * T // SLOTS - 1
    nblk = NE + nov
    V = [(0, SEQ), (SEQ, TB)][:T // SEQ]
    parts = [(t0, t1, k.gain2[:, v, :], k.mod[:, v, 3 * DC:4 * DC]) for v, (t0, t1) in enumerate(V)]
    rows = nc.dram_tensor(f"token_rows_{l}", (T, D), F32).ap()
    out_rows = nc.dram_tensor(f"slot_rows_{l}", (nblk * SLOTS, D), F32).ap()
    slot_token = nc.dram_tensor(f"slot_token_{l}", (nblk * SLOTS, 1), I32).ap()
    table = nc.dram_tensor(f"overflow_table_{l}", (16, 2), I32).ap()
    dest = k.sb(f"slot_of_{l}", [P, T // P, 2])
    desti = k.sb(f"slot_index_{l}", [P, T // P, 2], I32)
    wts = k.sb(f"weight_of_{l}", [P, T // P, 2])
    slots = k.sb(f"slots_{l}", [SLOTS, nblk], I32)
    tab = k.sb(f"table_{l}", [1, 16, 2], I32)
    with nc.sbuf_tensor(f"moe_h_{l}", [P, DC, T], F32) as hm:
        norm_stage(k, f"moe_norm{l}", k.x, DC, D, EPS, parts, hm)
        route_stage(k, l, hm, T, rows, slot_token, table, dest, desti, wts, out_rows)
    k.clear()
    load_slots_stage(k, slot_token, table, slots, tab, nblk)
    experts_stage(k, l, rows, slots, out_rows)
    overflow_stage(k, l, nov, rows, slots, tab, out_rows)
    combine_stage(k, l, T, desti, wts, out_rows)


def second_model(k, ctx):
    k.mod, (k.gain1, k.gain2) = k.mods[0], k.gains[0]
    gmlp(k)
    moe(k, 0, TB)
    k.mod, (k.gain1, k.gain2) = k.mods[1], k.gains[1]
    k.clear()
    rwkv(k)
    moe(k, 1, SEQ)
    final_stage(k)


def bias_stage(k):
    nc = k.nc
    done = k.sem("gate_bias")
    with nc.sbuf_tensor("gated_bias", [P, 2, DC], F32) as gb, nc.Block() as block:
        @block.vector
        def _(dve):
            for v in range(2):
                nc.vector.tensor_tensor(gb[:, v, :], k.mod[:, v, 2 * DC:3 * DC], param(k, "ga_b_out", DC), ALU.mult)\
                    .then_inc(done, 1)
            dve.wait_ge(done, 2)
            for v in range(2):
                for c in range(DC):
                    nc.vector.tensor_scalar(k.x[:, c, v * SEQ:(v + 1) * SEQ], k.x[:, c, v * SEQ:(v + 1) * SEQ],
                                            gb[:, v, c:c + 1], None, ALU.add)


def rwkv_segments(k, a):
    seg = k.seg
    names = ("rw_wr_2", "rw_wk_2", "rw_wv_2")
    for n in names:
        seg[n] = Segment(4, lambda i, j, n=n: [columns(a[n][0], DC, j * 256, 256)])

    def lora(name):
        def source(i, j):
            w = a[name][0]
            return [(lambda s, z=z: s[:, 0:DC * P].rearrange("p (k m) -> p k m", k=DC)[:, :, z * RH:(z + 1) * RH],
                     w[z].rearrange("(k p) m -> p k m", p=P)) for z in range(2)]
        return source
    seg["w1"], seg["a1"] = Segment(1, lora("rw_w1_2")), Segment(1, lora("rw_a1_2"))
    seg["g1"] = Segment(1, lambda i, j: [columns(a["rw_g1_2"][0], DC, 0, 160)])
    g2 = a["rw_g2_2"][0]
    seg["g2"] = Segment(1, lambda i, j: [(lambda s: s[:, 0:D], g2[0:P, :]), (lambda s: s[0:32, D:2 * D], g2[P:160, :])])
    seg["wo"] = Segment(4, lambda i, j: [columns(a["rw_wo_2"][0], DC, j * 256, 256)])
    return ["rw_wr_2", "w1", "rw_wk_2", "rw_wv_2", "a1", "g1", "g2", "wo"]


def shift_stage(k, h, xx):
    nc = k.nc
    done, zeroed = k.sem("shift_done"), k.sem("shift_zeroed")
    with nc.Block() as block:
        @block.gpsimd
        def _(pool):
            pool.memset(xx[:, :, :], 0.0).then_inc(zeroed, 1)

        @block.vector
        def _(dve):
            dve.wait_ge(zeroed, 1)
            W, q = 64, DC // 4
            for c in range(DC):
                lat = lambda x: x[:, c, 0:SEQ].rearrange("p (r w) -> p r w", w=W)
                to, of = lat(xx), lat(h)
                if c < q:
                    last = nc.vector.tensor_copy(to[:, :, 1:W], of[:, :, 0:W - 1])
                elif c < 2 * q:
                    last = nc.vector.tensor_copy(to[:, :, 0:W - 1], of[:, :, 1:W])
                elif c < 3 * q:
                    last = nc.vector.tensor_copy(xx[:, c, W:SEQ], h[:, c, 0:SEQ - W])
                else:
                    last = nc.vector.tensor_copy(xx[:, c, 0:SEQ - W], h[:, c, W:SEQ])
                last.then_inc(done, 1)
                if c < DC // 2:
                    last = nc.vector.tensor_copy(xx[:, c, SEQ + 1:TB], h[:, c, SEQ:TB - 1])
                else:
                    last = nc.vector.tensor_copy(xx[:, c, SEQ:TB - 1], h[:, c, SEQ + 1:TB])
                last.then_inc(done, 1)
            dve.wait_ge(done, 2 * DC)
            for c in range(DC):
                nc.vector.tensor_tensor(xx[:, c, :], xx[:, c, :], h[:, c, :], ALU.subtract)


def mix(k, xx, h, n, to, T=TB):
    def run(dve):
        for c in range(DC):
            k.nc.vector.scalar_tensor_tensor(out=to[:, c, 0:T], in0=xx[:, c, 0:T], scalar=param(k, "mu", 1, n * DC + c),
                                             in1=h[:, c, 0:T], op0=ALU.mult, op1=ALU.add)
    return run


def copy_to(nc, dst):
    return lambda dve, m, ps: nc.vector.tensor_copy(dst[:, m, :], ps[:, :])


def rwkv(k):
    nc, a, seg = k.nc, k.a, k.seg
    with ExitStack() as ctx:
        sb = lambda n, s: ctx.enter_context(nc.sbuf_tensor(f"rw_{n}", s, F32))
        gate = sb("gate", [P, DC, SEQ])
        lw, la = sb("lw", [P, TB]), sb("la", [P, TB])
        k.stream.hold = seg["wo"].first
        r, kx, v = (sb(n, [P, DC, TB]) for n in ("r", "k", "v"))
        with ExitStack() as c2:
            sb2 = lambda n, s: c2.enter_context(nc.sbuf_tensor(f"rw_{n}", s, F32))
            h, xx, xm0, xm1 = (sb2(n, [P, DC, TB]) for n in ("h", "xx", "mixed0", "mixed1"))
            parts = [(t0, t1, k.gain1[:, n, :], k.mod[:, n, 0:DC]) for n, (t0, t1) in enumerate([(0, SEQ), (SEQ, TB)])]
            norm_stage(k, "rw_norm", k.x, DC, D, EPS, parts, h, (xm0, xm1))
            shift_stage(k, h, xx)
            with nc.Block() as block:
                block.vector(mix(k, xx, h, 0, xm0))
            for n, name, dst in ((0, "rw_wr_2", r), (1, "w1", lw), (2, "rw_wk_2", kx), (3, "rw_wv_2", v),
                                 (4, "a1", la)):
                xm = (xm0, xm1)[n % 2]
                following = mix(k, xx, h, n + 1, (xm0, xm1)[(n + 1) % 2], TB if n < 4 else SEQ)
                if name in ("w1", "a1"):
                    f = ACT.Tanh if name == "w1" else ACT.Copy
                    linear_stage(k, name, seg[name], whole_tiles(DC, P), lambda f, xm=xm: xm[:, f, :], TB,
                                 lambda act, m, ps, f=f, dst=dst: nc.scalar.activation(dst[:, :], ps[:, :], f), 4,
                                 on_scalar=True, first=following)
                else:
                    linear_stage(k, name, seg[name], whole_tiles(DC, 256), lambda f, xm=xm: xm[:, f, :], TB,
                                 copy_to(nc, dst), 4, first=following)
            s1 = sb2("gate_hidden", [P, 2, SEQ])
            linear_stage(k, "g1", seg["g1"], whole_tiles(DC, 160), lambda f: xm1[:, f, 0:SEQ], SEQ,
                         lambda act, m, ps: nc.scalar.activation(
                             s1[0:(P, 32)[m], m, :], ps[0:(P, 32)[m], 0:SEQ], ACT.Sigmoid), 4, on_scalar=True)

            def g2(j):
                return [(True, True, [(lambda s, c=c: s[:, c * P:(c + 1) * P], 0),
                                      (lambda s, c=c: s[0:32, D + c * P:D + (c + 1) * P], 1)], P) for c in range(DC)]
            linear_stage(k, "g2", seg["g2"], g2, lambda f: s1[0:(P, 32)[f], f, :], SEQ,
                         lambda dve, m, ps: nc.vector.tensor_copy(gate[:, m, :], ps[:, 0:SEQ]), 4)
        k.clear()
        scan_heads(k, r, kx, v, lw, la, gate)
        with nc.Block() as block:
            block.sync(k.stream.resume)

        def write(dve, m, ps):
            return nc.vector.scalar_tensor_tensor(out=k.x[:, m, 0:SEQ], in0=ps[:, 0:SEQ],
                                                  scalar=k.mod[:, 0, 2 * DC + m:2 * DC + m + 1],
                                                  in1=k.x[:, m, 0:SEQ], op0=ALU.mult, op1=ALU.add)
        linear_stage(k, "wo", seg["wo"], whole_tiles(DC, 256), lambda f: gate[:, f, :], SEQ, write, 4)


LEVELS = 6
DECAY = -float(np.exp(-0.5))
M_US, M_LS, M_UI, M_LI, M_ID, M_LEVEL = 0, 1, 2, 3, 4, 5


def rwkv_masks():
    s, t = np.meshgrid(np.arange(CH), np.arange(CH), indexing="ij")
    tables = [t > s, t < s, t >= s, t <= s, t == s]
    for level in range(LEVELS):
        b = 1 << level
        tables.append((s // (2 * b) == t // (2 * b)) & (s // b != t // b))
    tables.append(np.broadcast_to(t > 0, t.shape))
    return np.stack([np.tile(m.astype(np.float32), (2, 1)) for m in tables], axis=1)


def scan_heads(k, r, kx, v, lw, la, gate):
    nc = k.nc
    with ExitStack() as ctx:
        sb = lambda n, s: ctx.enter_context(nc.sbuf_tensor(f"sc_{n}", s, F32))
        q = Kernel()
        q.masks = sb("masks", [P, M_LEVEL + LEVELS + 1, CH])
        q.starts = sb("chunk_starts", [P, TB])
        q.w2, q.a2 = sb("w2", [P, D]), sb("a2", [P, D])
        q.om = sb("one_minus_ka", [P, DC])
        names = ("w2c", "a2c")
        q.w2c, q.a2c = (sb(n, [P, P]) for n in names)
        q.pc, q.pn = sb("param_c", [P, 10]), sb("param_next", [P, 10])
        q.v = sb("v", [P, TB])
        q.at, q.bt, q.kt, q.rt = (sb(n, [P, 2, TB]) for n in ("at", "bt", "kt", "rt"))
        q.pend, q.pend_n = sb("pend", [P, 2, NCH]), sb("pend_next", [P, 2, NCH])
        q.bonus, q.bonus_n = sb("bonus", [P, SEQ]), sb("bonus_next", [P, SEQ])
        landed = k.sem("sc_landed")
        done = k.sem("sc_om")
        with nc.Block() as block:
            @block.sync
            def _(sp):
                sp.dma_start(q.masks[:, :, :], k.a["rwkv_masks"]).then_inc(landed, 16)
                sp.dma_start(q.w2[:, :], k.a["rw_w2_2"][0].rearrange("z r d -> (z r) d")).then_inc(landed, 16)
                sp.dma_start(q.a2[:, :], k.a["rw_a2_2"][0].rearrange("z r d -> (z r) d")).then_inc(landed, 16)
                sp.wait_ge(landed, 48)

            @block.vector
            def _(dve):
                nc.vector.tensor_scalar(q.om[:, :], param(k, "k_a", DC), -1.0, 1.0, ALU.mult, ALU.add)
                dve.wait_ge(landed, 48)
                nc.vector.tensor_copy(chunked(q.starts[:, :]), mask_of(q, M_LEVEL + LEVELS)).then_inc(done, 1)
        k.clear()
        pair = lambda slot, n: k.stream.slots[slot][:, n * 2 * TB:(n + 1) * 2 * TB]\
            .rearrange("p (z t) -> p z t", z=2)
        q.lg, q.F, q.G, q.Gp, q.az, q.km = (pair(n // 2, n % 2) for n in range(6))
        kk_sq, r0_t0 = pair(3, 0), pair(3, 1)
        q.kk, q.sq, q.r0, q.t0 = kk_sq[:, 0, :], kk_sq[:, 1, :], r0_t0[:, 0, :], r0_t0[:, 1, :]
        q.n, q.nt, q.akt, q.x, q.xt, q.rbk, q.btt, q.ktt = (
            sb(n, [P, 2, TB]) for n in ("n", "nt", "akt", "x", "xt", "rbk", "btt", "ktt"))
        q.t1, q.vt = q.bt, q.kt[:, 0, :]
        prepare = Prepare(k, q, 0, r, kx, lw, la)
        with nc.Block() as block:
            block.gpsimd(prepare.pool)

            @block.tensor
            def _(pe):
                for part in range(1, 5):
                    prepare.pe(pe, part)

            @block.scalar
            def _(act):
                for part in range(Prepare.PARTS):
                    prepare.act(act, part)

            @block.vector
            def _(dve):
                for part in range(Prepare.PARTS):
                    prepare.dve(dve, part)
        k.clear()

        def round_(c, following):
            scan_matrices(k, q, c, r, v)
            scan_invert(k, q, following)
            scan_states(k, q)
            scan_output(k, q, c, gate)
            k.clear()
        with nc.Fori(0, DC - 1) as c:
            round_(c, lambda: Prepare(k, q, c + 1, r, kx, lw, la))
        round_(DC - 1, lambda: None)


class Prepare:

    PARTS = 10

    def __init__(self, k, q, c, r, kx, lw, la):
        self.k, self.q, self.c, self.lw, self.la = k, q, c, lw, la
        self.rc = r[:, ds(c, 1), :].rearrange("p a t -> p (a t)")
        self.kc = kx[:, ds(c, 1), :].rearrange("p a t -> p (a t)")
        (self.wmade, self.smade, self.vdone, self.adone, self.pdone, self.summed, self.ready, self.kmade,
         self.scaled) = (k.sem(f"sp_{n}") for n in (
             "wmade", "smade", "vdone", "adone", "pdone", "summed", "ready", "kmade", "scaled"))
        self.link = None

    def pool(self, pool):
        nc, k, q, c = self.k.nc, self.k, self.q, self.c
        for n, name in enumerate(("k_k", "k_a", "r_k", "gn_g", "gn_b", "w0", "a0")):
            nc.gpsimd.tensor_copy(q.pn[:, n:n + 1], k.params[:, ds(c + k.col[name], 1)])
        for n, name in enumerate(("w0", "a0")):
            nc.gpsimd.tensor_copy(q.pn[:, 7 + n:8 + n], k.params[:, ds(c + (k.col[name] + DC), 1)])
        nc.gpsimd.tensor_copy(q.pn[:, 9:10], q.om[:, ds(c, 1)]).then_inc(self.pdone, 1)
        nc.gpsimd.tensor_copy(q.w2c[:, :], q.w2[:, ds(c * P, P)])
        nc.gpsimd.tensor_copy(q.a2c[:, :], q.a2[:, ds(c * P, P)]).then_inc(self.pdone, 1)

    def pe(self, pe, part):
        nc, k, q = self.k.nc, self.k, self.q
        if part == 1:
            pe.wait_ge(self.pdone, 2)
        if part <= 2:
            z = part - 1
            rows = slice(z * RH, (z + 1) * RH)
            pe.wait_ge(self.smade, 2 * z) if z else None
            nc.tensor.matmul(k.bank[6][:, :], q.w2c[rows, :], self.lw[rows, :], start=True, stop=True)
            nc.tensor.matmul(k.bank[7][:, :], q.a2c[rows, :], self.la[rows, :], start=True, stop=True)\
                .then_inc(self.wmade, 1)
        elif part == 3:
            pe.wait_ge(self.smade, 4)
            pe.wait_ge(self.adone, 1)
            nc.tensor.matmul(k.bank[6][:, :], k.head_ones[:, :], q.sq[:, :], start=True, stop=True)\
                .then_inc(self.summed, 1)
        else:
            pe.wait_ge(self.kmade, 1)
            nc.tensor.matmul(k.bank[7][:, 0:SEQ], k.head_ones[:, :], q.t0[:, 0:SEQ], start=True, stop=True)\
                .then_inc(self.summed, 1)

    def act(self, act, part):
        nc, k, q = self.k.nc, self.k, self.q
        p = lambda n: q.pn[:, n:n + 1]
        if part == 0:
            act.wait_ge(self.vdone, 1)
            nc.scalar.activation(q.sq[:, :], q.kk[:, :], ACT.Square).then_inc(self.adone, 1)
        if part in (0, 2):
            z = part // 2
            act.wait_ge(self.wmade, z + 1)
            nc.scalar.activation(q.az[:, z, :], k.bank[7][:, :], ACT.Sigmoid, bias=p(6 if z == 0 else 8))\
                .then_inc(self.smade, 1)
        elif part in (1, 3):
            z = part // 2
            nc.scalar.activation(q.lg[:, z, :], k.bank[6][:, :], ACT.Sigmoid, bias=p(5 if z == 0 else 7))\
                .then_inc(self.smade, 1)
        elif part == 6:
            act.wait_ge(self.ready, 1)
            nc.scalar.activation(q.r0[:, :], q.sq[:, :], ACT.Ln).then_inc(self.adone, 1)
        elif part == 7:
            act.wait_ge(self.adone, 2)
            nc.scalar.activation(q.r0[:, :], q.r0[:, :], ACT.Exp, scale=-0.5).then_inc(self.adone, 1)
        elif part == 8:
            act.wait_ge(self.scaled, 1)
            nc.scalar.activation(q.lg[:, :, :], q.G[:, :, :], ACT.Exp, scale=-1.0).then_inc(self.adone, 1)
        elif part == 9:
            act.wait_ge(self.adone, 4)
            nc.scalar.activation(q.G[:, :, :], q.G[:, :, :], ACT.Exp)
            nc.scalar.activation(q.Gp[:, :, :], q.Gp[:, :, :], ACT.Exp)
            nc.scalar.activation(q.pend_n[:, :, :], q.F[:, :, CH - 1::CH], ACT.Exp)
            act.wait_ge(self.summed, 2)
            nc.scalar.activation(q.bonus_n[:, :], k.bank[7][:, 0:SEQ], ACT.Copy)

    def dve(self, dve, part):
        nc, k, q = self.k.nc, self.k, self.q
        p = lambda n: q.pn[:, n:n + 1]
        link = self.link = self.link or Chain(dve, self.vdone)
        lg, F, G, Gp, az, km, kk, sq, r0, t0 = q.lg, q.F, q.G, q.Gp, q.az, q.km, q.kk, q.sq, q.r0, q.t0
        if part == 0:
            dve.wait_ge(self.pdone, 1)
            link(nc.vector.tensor_scalar(kk[:, :], self.kc, p(0), None, ALU.mult))
        elif part in (1, 3):
            z = part // 2
            dve.wait_ge(self.smade, 2 * z + 1)
            link(nc.vector.tensor_scalar(km[:, z, :], az[:, z, :], p(1), p(9), ALU.mult, ALU.add))
            nc.vector.tensor_tensor(km[:, z, :], km[:, z, :], self.kc, ALU.mult)
        elif part in (2, 4):
            z = part // 2 - 1
            dve.wait_ge(self.smade, 2 * z + 2)
            link(nc.vector.tensor_scalar(lg[:, z, :], lg[:, z, :], DECAY, None, ALU.mult))
            link(nc.vector.tensor_tensor_scan(F[:, z, :], q.starts[:, :], lg[:, z, :], 0.0, ALU.mult, ALU.add))
        elif part == 5:
            dve.wait_ge(self.summed, 1)
            nc.vector.tensor_scalar(sq[:, :], k.bank[6][:, :], 1e-12, None, ALU.add).then_inc(self.ready, 1)
            link(nc.vector.tensor_tensor(t0[:, 0:SEQ], km[:, 0, 0:SEQ], km[:, 1, 0:SEQ], ALU.add))
            nc.vector.scalar_tensor_tensor(out=t0[:, 0:SEQ], in0=t0[:, 0:SEQ], scalar=p(2), in1=self.rc[:, 0:SEQ],
                                           op0=ALU.mult, op1=ALU.mult).then_inc(self.kmade, 1)
        elif part == 6:
            nc.vector.tensor_copy(G[:, 0, :], F[:, 0, :])
            nc.vector.tensor_tensor(Gp[:, 0, :], F[:, 0, :], lg[:, 0, :], ALU.subtract)
        elif part == 7:
            for j in range(NCH):
                o = j * CH
                last = nc.vector.tensor_scalar(Gp[:, 1, o:o + CH], F[:, 1, o:o + CH], F[:, 1, o + CH - 1:o + CH], -1.0,
                                               ALU.subtract, ALU.mult)
            link(last)
            nc.vector.tensor_tensor(G[:, 1, :], Gp[:, 1, :], lg[:, 1, :], ALU.add).then_inc(self.scaled, 1)
        elif part == 8:
            dve.wait_ge(self.adone, 3)
            dve.wait_ge(self.summed, 2)
            link(nc.vector.tensor_tensor(t0[:, :], r0[:, :], r0[:, :], ALU.mult))
            link(nc.vector.scalar_tensor_tensor(out=t0[:, :], in0=t0[:, :], scalar=-0.5, in1=sq[:, :],
                                                op0=ALU.mult, op1=ALU.mult))
        elif part == 9:
            link(nc.vector.scalar_tensor_tensor(out=t0[:, :], in0=t0[:, :], scalar=1.5, in1=r0[:, :],
                                                op0=ALU.add, op1=ALU.mult))
            nc.vector.tensor_tensor(kk[:, :], kk[:, :], t0[:, :], ALU.mult)


HALVES = (0, RH)


def chunked(x):
    return x.rearrange("p (j s) -> p j s", s=CH)


def mask_of(q, n):
    return q.masks[:, n:n + 1, :].broadcast_to([P, NCH, CH])


def scan_matrices(k, q, c, r, v):
    nc = k.nc
    s = lambda n: k.sem(f"sm_{n}")
    made, emptied, vinit, operands, halfway, rt_made, v_made = (s(n) for n in (
        "made", "emptied", "vinit", "operands", "halfway", "rt_made", "v_made"))
    rc, vc = (x[:, ds(c, 1), :].rearrange("p a t -> p (a t)") for x in (r, v))
    up, low, incl = (M_US, M_LS), (M_LS, M_US), (M_UI, M_LI)
    jobs = []
    for z in range(2):
        jobs += [("nt", z, (q.bt, q.at), q.nt, up[z]), ("n", z, (q.at, q.bt), q.n, low[z])]
    jobs += [("akt", z, (q.kt, q.at), q.akt, up[z]) for z in range(2)]
    jobs += [("btt", z, (q.bt, None), q.btt, None) for z in range(2)]
    jobs += [("ktt", z, (q.kt, None), q.ktt, None) for z in range(2)]
    jobs += [("rbk", z, None, q.rbk, incl[z]) for z in range(2)]
    jobs.append(("vt", 0, (q.v, None), q.vt, None))
    with nc.Block() as block:
        @block.gpsimd
        def _(pool):
            for z in range(2):
                nc.gpsimd.tensor_tensor(q.rt[:, z, :], rc, q.G[:, z, :], ALU.mult).then_inc(rt_made, 1)
            nc.gpsimd.tensor_copy(q.v[:, :], vc).then_inc(v_made, 1)
            nc.gpsimd.tensor_copy(q.bonus[:, :], q.bonus_n[:, :])
            nc.gpsimd.tensor_copy(q.pend[:, :, :], q.pend_n[:, :, :])
            nc.gpsimd.tensor_copy(q.pc[:, :], q.pn[:, :])
            for z in range(2):
                pool.wait_ge(emptied, 2 * z + 2)
                for x, n in ((q.x, q.n), (q.xt, q.nt)):
                    nc.gpsimd.tensor_tensor(chunked(x[:, z, :]), chunked(n[:, z, :]), mask_of(q, M_LEVEL), ALU.mult)\
                        .then_inc(vinit, 1)
                pool.wait_ge(vinit, 2 * z + 2)
                for x in (q.x, q.xt):
                    nc.gpsimd.tensor_tensor(chunked(x[:, z, :]), chunked(x[:, z, :]), mask_of(q, M_ID), ALU.add)
                nc.gpsimd.tensor_tensor(chunked(q.n[:, z, :]), chunked(q.nt[:, z, :]), mask_of(q, M_LEVEL + 1), ALU.mult)

        @block.tensor
        def _(pe):
            for n, (kind, z, ops, dst, mask) in enumerate(jobs):
                pe.wait_ge(operands, 2 * z + 1 + (kind in ("akt", "rbk", "ktt")))
                if kind == "rbk":
                    pe.wait_ge(rt_made, z + 1)
                if kind == "vt":
                    pe.wait_ge(v_made, 1)
                if n >= 4:
                    pe.wait_ge(emptied, n - 3)
                ps = k.bank[n % 4]
                for j in range(NCH):
                    for h in HALVES:
                        rows = slice(h, h + RH)
                        to = ps[rows, j * CH:(j + 1) * CH]
                        t = slice(j * CH, (j + 1) * CH)
                        if kind == "rbk":
                            src = (q.bt, q.kt)[j // LCH]
                            t = slice((j % LCH) * CH, (j % LCH + 1) * CH)
                            last = nc.tensor.matmul(to, src[rows, z, t], q.rt[rows, z, t], start=True, stop=True)
                        elif ops[1] is None:
                            src = ops[0][rows, t] if kind == "vt" else ops[0][rows, z, t]
                            if h == 0:
                                last = nc.tensor.transpose(to, src, k.ident[rows, rows])
                            else:
                                last = nc.tensor.matmul(to, src, k.ident[rows, rows], start=True, stop=True)
                        else:
                            last = nc.tensor.matmul(to, ops[0][rows, z, t], ops[1][rows, z, t], start=True, stop=True)
                last.then_inc(made, 1)

        @block.vector
        def _(dve):
            for z in range(2):
                nc.vector.tensor_tensor(q.bt[:, z, :], q.kk[:, :], q.az[:, z, :], ALU.mult).then_inc(halfway, 1)
                nc.vector.scalar_tensor_tensor(out=q.at[:, z, :], in0=q.kk[:, :], scalar=-1.0, in1=q.Gp[:, z, :],
                                               op0=ALU.mult, op1=ALU.mult)
                dve.wait_ge(halfway, z + 1)
                nc.vector.tensor_tensor(q.bt[:, z, :], q.bt[:, z, :], q.lg[:, z, :], ALU.mult).then_inc(operands, 1)
                nc.vector.tensor_tensor(q.kt[:, z, :], q.km[:, z, :], q.lg[:, z, :], ALU.mult).then_inc(operands, 1)
            for n, (kind, z, ops, dst, mask) in enumerate(jobs):
                dve.wait_ge(made, n + 1)
                ps = k.bank[n % 4][:, :]
                if mask is not None:
                    nc.vector.tensor_tensor(chunked(dst[:, z, :]), chunked(ps), mask_of(q, mask), ALU.mult).then_inc(emptied, 1)
                else:
                    nc.vector.tensor_copy(dst[:, :] if kind == "vt" else dst[:, z, :], ps).then_inc(emptied, 1)


def blocks_matmul(nc, ps, lhsT, rhs):
    for h in HALVES:
        rows = slice(h, h + RH)
        for j in range(NCH):
            t = slice(j * CH, (j + 1) * CH)
            last = nc.tensor.matmul(ps[rows, t], lhsT[rows, t], rhs[rows, t], start=True, stop=True)
    return last


def scan_invert(k, q, following):
    nc = k.nc
    s = lambda n: k.sem(f"si_{n}")
    masked, tmade, tkept, xmade, xtmade, xkept, xtkept = (s(n) for n in (
        "masked", "tmade", "tkept", "xmade", "xtmade", "xkept", "xtkept"))
    steps = [(level, z) for level in range(1, LEVELS) for z in range(2)]
    last_level = LEVELS - 1
    prepare = following()
    noff = q.n
    with nc.Block() as block:
        @block.gpsimd
        def _(pool):
            if prepare is not None:
                prepare.pool(pool)
            for n, (level, z) in enumerate(steps):
                if level < last_level:
                    pool.wait_ge(tmade, n + 1)
                    nc.gpsimd.tensor_tensor(chunked(noff[:, z, :]), chunked(q.nt[:, z, :]),
                                            mask_of(q, M_LEVEL + level + 1), ALU.mult).then_inc(masked, 1)

        @block.tensor
        def _(pe):
            for n in range(0, len(steps), 2):
                level = steps[n][0]
                if prepare is not None and level < last_level:
                    prepare.pe(pe, level)
                for m in (n, n + 1):
                    z = steps[m][1]
                    if level > 1:
                        pe.wait_ge(masked, m - 1)
                        pe.wait_ge(xkept, m - 1)
                    blocks_matmul(nc, k.bank[z], noff[:, z, :], q.x[:, z, :]).then_inc(tmade, 1)
                for m in (n, n + 1):
                    z = steps[m][1]
                    pe.wait_ge(tkept, m + 1)
                    if level > 1:
                        pe.wait_ge(xtkept, m - 1)
                    if level < last_level:
                        blocks_matmul(nc, k.bank[2 + z], q.xt[:, z, :], q.t1[:, z, :]).then_inc(xmade, 1)
                    blocks_matmul(nc, k.bank[4 + z], q.t1[:, z, :], q.xt[:, z, :]).then_inc(xtmade, 1)

        @block.scalar
        def _(act):
            for n, (level, z) in enumerate(steps):
                if level < last_level:
                    act.wait_ge(xmade, n + 1)
                    nc.scalar.activation(q.x[:, z, :], k.bank[2 + z][:, :], ACT.Copy).then_inc(xkept, 1)
                if prepare is not None:
                    prepare.act(act, n)

        @block.vector
        def _(dve):
            for n in range(0, len(steps), 2):
                for m in (n, n + 1):
                    z = steps[m][1]
                    dve.wait_ge(tmade, m + 1)
                    nc.vector.tensor_tensor(chunked(q.t1[:, z, :]), chunked(k.bank[z][:, :]), mask_of(q, M_ID), ALU.add)\
                        .then_inc(tkept, 1)
                for m in (n, n + 1):
                    z = steps[m][1]
                    dve.wait_ge(xtmade, m + 1)
                    nc.vector.tensor_copy(q.xt[:, z, :], k.bank[4 + z][:, :]).then_inc(xtkept, 1)
                    if prepare is not None:
                        prepare.dve(dve, m)


def scan_states(k, q):
    nc = k.nc
    s = lambda n: k.sem(f"ss_{n}")
    rmade, rkept, samade, sakept, smade, skept, spre, zeroed, ymade = (s(n) for n in (
        "rmade", "rkept", "samade", "sakept", "smade", "skept", "spre", "zeroed", "ymade"))
    order = [[4, 5, 6, 7, 0, 1, 2, 3], [7, 6, 5, 4, 3, 2, 1, 0]]
    with ExitStack() as ctx:
        st, stp, rs, sa = ([q.n[:, z, n * RH:(n + 1) * RH] for z in range(2)] for n in range(4))
        block = ctx.enter_context(nc.Block())
        last_step = NCH - 1

        @block.tensor
        def _(pe):
            for i in range(NCH):
                for z in range(2):
                    j = order[z][i]
                    t = slice(j * CH, (j + 1) * CH)
                    n = 2 * i + z
                    if i:
                        pe.wait_ge(skept, n - 1)
                    for h in HALVES:
                        rows = slice(h, h + RH)
                        if i:
                            nc.tensor.matmul(k.bank[z][rows, 0:RH], q.at[rows, z, t], st[z][rows, :],
                                             start=True, stop=False)
                        last = nc.tensor.matmul(k.bank[z][rows, 0:RH], q.akt[rows, z, t], q.vt[rows, t],
                                                start=(i == 0), stop=True)
                    last.then_inc(rmade, 1)
                for z in range(2):
                    t = slice(order[z][i] * CH, (order[z][i] + 1) * CH)
                    n = 2 * i + z
                    pe.wait_ge(rkept, n + 1)
                    for h in HALVES:
                        rows = slice(h, h + RH)
                        last = nc.tensor.matmul(k.bank[z][rows, RH:2 * RH], q.xt[rows, z, t], rs[z][rows, :],
                                                start=True, stop=True)
                    last.then_inc(samade, 1)
                for z in range(2):
                    t = slice(order[z][i] * CH, (order[z][i] + 1) * CH)
                    n = 2 * i + z
                    pe.wait_ge(sakept, n + 1)
                    if i < last_step:
                        for h in HALVES:
                            rows = slice(h, h + RH)
                            ps = k.bank[z][rows, 2 * RH:3 * RH]
                            nc.tensor.matmul(ps, q.btt[rows, z, t], sa[z][rows, :], start=True, stop=False)
                            last = nc.tensor.matmul(ps, q.ktt[rows, z, t], q.vt[rows, t], start=False, stop=True)
                        last.then_inc(smade, 1)
                if i >= LCH:
                    for z in range(2):
                        j = order[z][i]
                        t, t2 = slice(j * CH, (j + 1) * CH), slice((LCH + j) * CH, (LCH + j + 1) * CH)
                        for h in HALVES:
                            rows = slice(h, h + RH)
                            ps = k.bank[2 + z][rows, t]
                            nc.tensor.matmul(ps, st[z][rows, :], q.rt[rows, z, t], start=True, stop=False)
                            nc.tensor.matmul(ps, sa[z][rows, :], q.rbk[rows, z, t], start=False, stop=False)
                            last = nc.tensor.matmul(ps, q.vt[rows, t], q.rbk[rows, z, t2], start=False, stop=True)
                        last.then_inc(ymade, 1)

        @block.vector
        def _(dve):
            for i in range(NCH):
                for z in range(2):
                    n = 2 * i + z
                    dve.wait_ge(rmade, n + 1)
                    nc.vector.tensor_copy(rs[z][:, :], k.bank[z][:, 0:RH]).then_inc(rkept, 1)
                for z in range(2):
                    n = 2 * i + z
                    dve.wait_ge(samade, n + 1)
                    if i > LCH:
                        dve.wait_ge(ymade, 2 * (i - LCH - 1) + z + 1)
                    elif i:
                        dve.wait_ge(smade, n - 1)
                    nc.vector.tensor_copy(sa[z][:, :], k.bank[z][:, RH:2 * RH]).then_inc(sakept, 1)
                if i < last_step:
                    for z in range(2):
                        n, j = 2 * i + z, order[z][i]
                        dve.wait_ge(smade, n + 1)
                        pend = q.pend[:, z, j:j + 1]
                        if i == 0:
                            nc.vector.tensor_scalar(st[z][:, :], k.bank[z][:, 2 * RH:3 * RH], pend, None, ALU.mult)\
                                .then_inc(skept, 1)
                            continue
                        nc.vector.tensor_scalar(stp[z][:, :], st[z][:, :], pend, None, ALU.mult).then_inc(spre, 1)
                        dve.wait_ge(spre, n - 1)
                        if i >= LCH:
                            dve.wait_ge(ymade, 2 * (i - LCH) + z + 1)
                        nc.vector.scalar_tensor_tensor(out=st[z][:, :], in0=k.bank[z][:, 2 * RH:3 * RH], scalar=pend,
                                                       in1=stp[z][:, :], op0=ALU.mult, op1=ALU.add).then_inc(skept, 1)


def scan_output(k, q, c, gate):
    nc = k.nc
    s = lambda n: k.sem(f"so_{n}")
    vdone, summed, adone, sqd = (s(n) for n in ("vdone", "summed", "adone", "sqd"))
    with ExitStack() as ctx:
        y, m, r0, t0 = q.n[:, 0, 0:SEQ], q.n[:, 0, SEQ:], q.n[:, 1, 0:SEQ], q.n[:, 1, SEQ:]
        block = ctx.enter_context(nc.Block())
        g = gate[:, ds(c, 1), :].rearrange("p a t -> p (a t)")

        @block.tensor
        def _(pe):
            pe.wait_ge(vdone, 2)
            nc.tensor.matmul(k.bank[4][:, 0:SEQ], k.head_ones[:, :], y[:, :], start=True, stop=True).then_inc(summed, 1)
            pe.wait_ge(adone, 1)
            nc.tensor.matmul(k.bank[5][:, 0:SEQ], k.head_ones[:, :], t0[:, :], start=True, stop=True)\
                .then_inc(summed, 1)

        @block.scalar
        def _(act):
            act.wait_ge(vdone, 3)
            nc.scalar.activation(t0[:, :], y[:, :], ACT.Square).then_inc(adone, 1)
            act.wait_ge(vdone, 4)
            nc.scalar.activation(r0[:, :], m[:, :], ACT.Ln).then_inc(adone, 1)
            act.wait_ge(adone, 2)
            nc.scalar.activation(r0[:, :], r0[:, :], ACT.Exp, scale=-0.5).then_inc(adone, 1)

        @block.vector
        def _(dve):
            link = Chain(dve, vdone)
            link(nc.vector.tensor_copy(y[:, :], k.bank[2][:, 0:SEQ]))
            link(nc.vector.tensor_tensor(y[:, :], y[:, :], k.bank[3][:, 0:SEQ], ALU.add))
            dve.wait_ge(summed, 1)
            link(nc.vector.scalar_tensor_tensor(out=y[:, :], in0=k.bank[4][:, 0:SEQ], scalar=-1.0 / RH, in1=y[:, :],
                                                op0=ALU.mult, op1=ALU.add))
            dve.wait_ge(summed, 2)
            link(nc.vector.tensor_scalar(m[:, :], k.bank[5][:, 0:SEQ], 1.0 / RH, GN_EPS, ALU.mult, ALU.add))
            dve.wait_ge(adone, 3)
            link(nc.vector.tensor_tensor(t0[:, :], r0[:, :], r0[:, :], ALU.mult))
            link(nc.vector.scalar_tensor_tensor(out=t0[:, :], in0=t0[:, :], scalar=-0.5, in1=m[:, :],
                                                op0=ALU.mult, op1=ALU.mult))
            link(nc.vector.scalar_tensor_tensor(out=t0[:, :], in0=t0[:, :], scalar=1.5, in1=r0[:, :],
                                                op0=ALU.add, op1=ALU.mult))
            link(nc.vector.tensor_tensor(y[:, :], y[:, :], t0[:, :], ALU.mult))
            link(nc.vector.tensor_scalar(y[:, :], y[:, :], q.pc[:, 3:4], q.pc[:, 4:5], ALU.mult, ALU.add))
            link(nc.vector.tensor_tensor(t0[:, :], q.bonus[:, :], q.v[:, 0:SEQ], ALU.mult))
            link(nc.vector.tensor_tensor(y[:, :], y[:, :], t0[:, :], ALU.add))
            nc.vector.tensor_tensor(g, y[:, :], g, ALU.mult)


def final_stage(k):
    nc = k.nc
    with nc.sbuf_tensor("fin", [P, DC, SEQ], F32) as f, nc.sbuf_tensor("fin_rows", [P, 2, D], F32) as rows:
        norm_stage(k, "final", k.x, DC, D, EPS, [(0, SEQ, param(k, "final", DC), None)], f)
        turned, copied, stored = (k.sem(f"fin_{n}") for n in ("turned", "copied", "stored"))
        with nc.Block() as block:
            @block.tensor
            def _(pe):
                for n in range(4):
                    t, half = n // 2, n % 2
                    for c in range(4):
                        last = nc.tensor.transpose(k.bank[n][:, c * P:(c + 1) * P],
                                                   f[:, half * 4 + c, t * P:(t + 1) * P], k.ident[:, :])
                    last.then_inc(turned, 1)

            @block.vector
            def _(dve):
                for n in range(4):
                    dve.wait_ge(turned, n + 1)
                    nc.vector.tensor_copy(rows[:, n // 2, (n % 2) * 512:(n % 2 + 1) * 512], k.bank[n][:, :])\
                        .then_inc(copied, 1)

            @block.sync
            def _(sp):
                for t in range(2):
                    sp.wait_ge(copied, 2 * t + 2)
                    sp.dma_start(k.a["out"][0, t * P:(t + 1) * P, :], rows[:, t, :]).then_inc(stored, 16)
                sp.wait_ge(stored, 32)


def kernel(**inputs):
    import concourse.bacc as bacc
    from concourse.bass_utils import run_bass_kernel_spmd

    nc = bacc.Bacc("TRN2", target_bir_lowering=False, num_devices=1)
    arrays, a = {}, {}
    for name, value in {**inputs, **shape_tables()}.items():
        value = np.ascontiguousarray(value)
        arrays[f"in_{name}_dram"] = value
        a[name] = nc.dram_tensor(f"in_{name}_dram", value.shape, mybir.dt.from_np(value.dtype),
                                 kind="ExternalInput").ap()
    a["out"] = nc.dram_tensor("out_0_dram", (1, SEQ, D), F32, kind="ExternalOutput").ap()
    program(nc, a)
    r = run_bass_kernel_spmd(nc, [arrays], core_ids=[0])
    return r.results[0]["out_0_dram"]
```
